# Optimizing a Trainium2 kernel written in Bass

```python
import math
import jax
import jax.numpy as jnp
from jax import lax
import numpy as np

D_MODEL = 1024
BATCH = 1
SEQ = 128
DEPTH = 2
DEC_BATCH = 1
DEC_SEQ = 512
PAST_LEN = 128

GRID_W = 64
RMS_EPS = 1e-6
F32 = jnp.float32
DN_HEADS = 4
DN_DK = 128
DN_DV = 128
DN_W = DN_HEADS * DN_DK
DN_CONV = 5
DN_CHUNK = 64
DA_HEADS = 4
DA_DH = 64
DA_DV = 2 * DA_DH
DA_QK = DA_HEADS * 2 * DA_DH
DA_V = DA_HEADS * DA_DV
Q_BLOCK = 128
ROPE_BASE = 10000.0
HY_W = 512
HY_SHORT = 3
HY_BANDS = 8
HY_EMB = 1 + 2 * HY_BANDS
HY_ORDER = 64
HY_FAST_DECAY = 0.3
HY_SLOW_DECAY = 1.5
HY_TARGET = 1e-2
N_BRANCH = 3
D_FF = ((8 * D_MODEL // 3 + 255) // 256) * 256
COL_SIZES = (DN_W, DN_W, DN_W, 2 * DN_HEADS, 2 * DN_HEADS, DN_W,
             DA_QK, DA_QK, DA_V, 3 * HY_W, N_BRANCH * D_MODEL)
N_IN = sum(COL_SIZES)

kernel_name = 'hybrid_diffusion_deltanet_diffattn_hyena_step'

def rmsnorm(x, g):
    xf = x.astype(F32)
    y = xf * lax.rsqrt(jnp.mean(xf * xf, axis=-1, keepdims=True) + RMS_EPS)
    return (y * g.astype(F32)).astype(x.dtype)

def l2norm(x):
    return x * lax.rsqrt(jnp.sum(x * x, axis=-1, keepdims=True) + RMS_EPS)

def split_columns(p):
    idx = []
    acc = 0
    for s in COL_SIZES[:-1]:
        acc += s
        idx.append(acc)
    return jnp.split(p, idx, axis=-1)

def depthwise_conv_centred(x, w, b=None):
    k, ch = w.shape
    pad = k // 2
    y = lax.conv_general_dilated(x, w[:, None, :].astype(x.dtype), window_strides=(1,),
                                 padding=[(pad, pad)], dimension_numbers=('NWC', 'WIO', 'NWC'),
                                 feature_group_count=ch)
    if b is not None:
        y = y + b.astype(x.dtype)
    return y

def axial_rope_tables(n_tok):
    rows = n_tok // GRID_W
    row_id = jnp.repeat(jnp.arange(rows), GRID_W).astype(F32)
    col_id = (jnp.arange(rows * GRID_W) % GRID_W).astype(F32)
    half = DA_DH // 2
    inv = ROPE_BASE ** (-jnp.arange(0, half, 2, dtype=F32) / half)
    ang_r = row_id[:, None] * inv
    ang_c = col_id[:, None] * inv
    return (jnp.cos(ang_r), jnp.sin(ang_r), jnp.cos(ang_c), jnp.sin(ang_c))

def _rotate(x, cos, sin):
    x1, x2 = jnp.split(x, 2, axis=-1)
    return jnp.concatenate([x1 * cos - x2 * sin, x1 * sin + x2 * cos], axis=-1)

def apply_axial_rope(x, tables):
    cr, sr, cc, sc = [t[None, :, None, None, :] for t in tables]
    xr, xc = jnp.split(x.astype(F32), 2, axis=-1)
    return jnp.concatenate([_rotate(xr, cr, sr), _rotate(xc, cc, sc)], axis=-1).astype(x.dtype)

def chunk_gated_delta(q, k, v, g, beta, s0):
    b, h, n_tok, _ = q.shape
    dv = v.shape[-1]
    c = DN_CHUNK
    n = n_tok // c
    q, k, v = (t.reshape(b, h, n, c, t.shape[-1]) for t in (q, k, v))
    g = g.reshape(b, h, n, c)
    beta = beta.reshape(b, h, n, c)
    gc = jnp.cumsum(g, axis=-1)
    tril = jnp.tril(jnp.ones((c, c), dtype=bool))
    strict = jnp.tril(jnp.ones((c, c), dtype=bool), -1)
    decay = jnp.exp(jnp.where(tril, gc[..., :, None] - gc[..., None, :], -jnp.inf))
    k_beta = k * beta[..., None]
    a = jnp.where(strict, jnp.einsum('bhnik,bhnjk->bhnij', k_beta, k) * decay, 0.0)
    m = a + jnp.eye(c, dtype=a.dtype)
    solve = lambda rhs: lax.linalg.triangular_solve(m, rhs, left_side=True, lower=True,
                                                    unit_diagonal=True)
    u = solve(v * beta[..., None])
    w = solve(k_beta * jnp.exp(gc)[..., None])
    qk = jnp.einsum('bhnik,bhnjk->bhnij', q, k) * decay

    def step(s, inp):
        q_i, k_i, u_i, w_i, qk_i, gc_i = inp
        v_new = u_i - jnp.einsum('bhck,bhkv->bhcv', w_i, s)
        o_i = (jnp.einsum('bhck,bhkv->bhcv', q_i * jnp.exp(gc_i)[..., None], s)
               + jnp.einsum('bhij,bhjv->bhiv', qk_i, v_new))
        g_last = gc_i[..., -1:]
        s = (s * jnp.exp(g_last)[..., None]
             + jnp.einsum('bhck,bhcv->bhkv', k_i * jnp.exp(g_last - gc_i)[..., None], v_new))
        return s, o_i

    xs = tuple(jnp.moveaxis(t, 2, 0) for t in (q, k, u, w, qk, gc))
    s_fin, o = lax.scan(step, s0, xs)
    return jnp.moveaxis(o, 0, 2).reshape(b, h, n_tok, dv), s_fin

def gated_deltanet(q, k, v, beta_logit, alpha_logit, z, conv_w, a_log, dt_bias, norm_g, s0):
    dt = q.dtype
    b, n_tok, _ = q.shape
    qkv = jax.nn.silu(depthwise_conv_centred(jnp.concatenate([q, k, v], axis=-1), conv_w))
    q, k, v = jnp.split(qkv.astype(F32), 3, axis=-1)
    heads = lambda t: t.reshape(b, n_tok, DN_HEADS, -1).transpose(0, 2, 1, 3)
    q = l2norm(heads(q)) * (DN_DK ** -0.5)
    k = l2norm(heads(k))
    v = heads(v)
    per_dir = lambda t: t.astype(F32).reshape(b, n_tok, 2, DN_HEADS).transpose(2, 0, 3, 1)
    beta = jax.nn.sigmoid(per_dir(beta_logit))
    g = -(jnp.exp(a_log.astype(F32))[:, None, :, None]
          * jax.nn.softplus(per_dir(alpha_logit) + dt_bias.astype(F32)[:, None, :, None]))
    s0 = s0.astype(F32)
    o_f, s_f = chunk_gated_delta(q, k, v, g[0], beta[0], s0[:, 0])
    flip = lambda t: jnp.flip(t, axis=2)
    o_b, s_b = chunk_gated_delta(flip(q), flip(k), flip(v), flip(g[1]), flip(beta[1]), s0[:, 1])
    o = (o_f + flip(o_b)).transpose(0, 2, 1, 3)
    o = rmsnorm(o, norm_g) * jax.nn.silu(z.astype(F32).reshape(b, n_tok, DN_HEADS, DN_DV))
    return o.reshape(b, n_tok, DN_W).astype(dt), jnp.stack([s_f, s_b], axis=1).astype(dt)

def diff_softmax_attention(q, k, v, lam):
    b, h, n_q = q.shape[:3]
    nb = n_q // Q_BLOCK
    qb = jnp.moveaxis(q.reshape(b, h, nb, Q_BLOCK, 2, DA_DH), 2, 0)
    scale = DA_DH ** -0.5

    def one_block(qi):
        s = jnp.einsum('bhqmd,bhkmd->bhmqk', qi, k).astype(F32) * scale
        p = jax.nn.softmax(s, axis=-1)
        a = p[:, :, 0] - lam * p[:, :, 1]
        return jnp.einsum('bhqk,bhkv->bhqv', a.astype(v.dtype), v)

    o = lax.map(one_block, qb)
    return jnp.moveaxis(o, 0, 2).reshape(b, h, n_q, DA_DV)

def differential_attention(q, k, v, lam_p, subln_g, layer, rope, ctx_k, ctx_v):
    b, n_tok, _ = q.shape
    q = q.reshape(b, n_tok, DA_HEADS, 2, DA_DH)
    k = k.reshape(b, n_tok, DA_HEADS, 2, DA_DH)
    v = v.reshape(b, n_tok, DA_HEADS, DA_DV).transpose(0, 2, 1, 3)
    lam_init = 0.8 - 0.6 * math.exp(-0.3 * layer)
    lp = lam_p.astype(F32)
    lam = jnp.exp(jnp.sum(lp[0] * lp[1])) - jnp.exp(jnp.sum(lp[2] * lp[3])) + lam_init
    if rope is not None:
        q = apply_axial_rope(q, rope)
        k = apply_axial_rope(k, rope)
    q = q.transpose(0, 2, 1, 3, 4)
    k = k.transpose(0, 2, 1, 3, 4)
    if ctx_k is None:
        keys, vals = k, v
    else:
        n_ctx = ctx_k.shape[2]
        keys = jnp.concatenate([ctx_k.reshape(b, DA_HEADS, n_ctx, 2, DA_DH).astype(k.dtype), k], axis=2)
        vals = jnp.concatenate([ctx_v.astype(v.dtype), v], axis=2)
    o = diff_softmax_attention(q, keys, vals, lam)
    o = rmsnorm(o, subln_g) * (1.0 - lam_init)
    o = o.transpose(0, 2, 1, 3).reshape(b, n_tok, DA_V)
    if ctx_k is None:
        return o, (k.reshape(b, DA_HEADS, n_tok, DA_DV), v)
    return o, None

def hyena_filter(n, w1, b1, freq, w2, b2, w3):
    j = jnp.arange(n, dtype=F32)
    t = j / (n - 1)
    ang = (2.0 * math.pi * j / n)[:, None] * jnp.linspace(1e-4, HY_BANDS - 1, HY_BANDS, dtype=F32)
    z = jnp.concatenate([t[:, None], jnp.cos(ang), -jnp.sin(ang)], axis=-1)
    fr = freq.astype(F32)
    hdn = jnp.sin(fr * (z @ w1.astype(F32) + b1.astype(F32)))
    hdn = jnp.sin(fr * (hdn @ w2.astype(F32) + b2.astype(F32)))
    h = hdn @ w3.astype(F32)
    half = n // 2
    dist = jnp.abs(j - half) / half
    max_decay = math.log(HY_TARGET) / HY_FAST_DECAY
    min_decay = math.log(HY_TARGET) / HY_SLOW_DECAY
    deltas = jnp.abs(jnp.linspace(min_decay, max_decay, HY_W, dtype=F32))
    h = h * jnp.exp(-dist[:, None] * deltas)
    return h / jnp.sum(jnp.abs(h), axis=0, keepdims=True)

def hyena(u, conv_w, conv_b, w1, b1, freq, w2, b2, w3, d_skip):
    n_tok = u.shape[1]
    uc = depthwise_conv_centred(u, conv_w, conv_b)
    x0, x1, v = jnp.split(uc, 3, axis=-1)
    h = hyena_filter(n_tok, w1, b1, freq, w2, b2, w3)
    gv = (v * x1).astype(F32)
    n_fft = 2 * n_tok
    y = jnp.fft.irfft(jnp.fft.rfft(gv, n=n_fft, axis=1) * jnp.fft.rfft(h, n=n_fft, axis=0)[None],
                      n=n_fft, axis=1)[:, n_tok // 2: n_tok // 2 + n_tok]
    y = y + gv * d_skip.astype(F32)
    return (y * x0.astype(F32)).astype(u.dtype)

def token_mixers(h, layer, lp, rope, ctx):
    b = h.shape[0]
    (q_a, k_a, v_a, beta_a, alpha_a, z_a, q_b, k_b, v_b, u_c, gate_logits) = split_columns(h @ lp['w_in'])
    s0 = jnp.zeros((b, 2, DN_HEADS, DN_DK, DN_DV), F32) if ctx is None else ctx[2]
    o_a, s_fin = gated_deltanet(q_a, k_a, v_a, beta_a, alpha_a, z_a, lp['dn_conv_w'], lp['dn_a_log'],
                                lp['dn_dt_bias'], lp['dn_norm_g'], s0)
    o_b, kv = differential_attention(q_b, k_b, v_b, lp['da_lambda'], lp['da_subln_g'], layer, rope,
                                     None if ctx is None else ctx[0], None if ctx is None else ctx[1])
    o_c = hyena(u_c, lp['hy_conv_w'], lp['hy_conv_b'], lp['hy_w1'], lp['hy_b1'], lp['hy_freq'],
                lp['hy_w2'], lp['hy_b2'], lp['hy_w3'], lp['hy_d'])
    g_a, g_b, g_c = jnp.split(jax.nn.sigmoid(gate_logits), 3, axis=-1)
    merged = g_a * (o_a @ lp['w_br_a']) + g_b * (o_b @ lp['w_br_b']) + g_c * (o_c @ lp['w_br_c'])
    out = merged @ lp['w_out']
    new_ctx = (kv[0], kv[1], s_fin) if ctx is None else None
    return out, new_ctx

def trunk_layer(x, cond, layer, lp, rope, ctx):
    mod = cond @ lp['w_mod'] + lp['b_mod']
    sh1, sc1, g1, sh2, sc2, g2 = jnp.split(mod[:, None, :], 6, axis=-1)
    hmix = rmsnorm(x, lp['norm1_g']) * (1 + sc1) + sh1
    mix, new_ctx = token_mixers(hmix, layer, lp, rope, ctx)
    x = x + g1 * mix
    hffn = rmsnorm(x, lp['norm2_g']) * (1 + sc2) + sh2
    gate, up = jnp.split(hffn @ lp['w_ffn_in'], 2, axis=-1)
    x = x + g2 * ((jax.nn.silu(gate) * up) @ lp['w_ffn_out'])
    return x, new_ctx

def setup_inputs(seed: int = 0) -> dict:
    key = jax.random.key(seed)
    ks = iter(jax.random.split(key, 48))
    nrm = lambda shape, s: jax.random.normal(next(ks), shape, F32) * s
    D = D_MODEL
    dt = jnp.exp(jax.random.uniform(next(ks), (DEPTH, 2, DN_HEADS), F32,
                                    minval=math.log(1e-3), maxval=math.log(1e-1)))
    return {
        'x_prompt': nrm((BATCH, SEQ, D), 1.0),
        'x_sample': nrm((DEC_BATCH, DEC_SEQ, D), 1.0),
        'cache_k': nrm((DEC_BATCH, DEPTH, DA_HEADS, PAST_LEN, DA_DV), 1.0),
        'cache_v': nrm((DEC_BATCH, DEPTH, DA_HEADS, PAST_LEN, DA_DV), 1.0),
        'state_dn': nrm((DEC_BATCH, DEPTH, 2, DN_HEADS, DN_DK, DN_DV), DN_DK ** -0.5),
        'c': nrm((DEC_BATCH, D), 1.0),
        'c_ctx': nrm((D,), 1.0),
        'norm1_g': 1.0 + nrm((DEPTH, D), 0.02),
        'norm2_g': 1.0 + nrm((DEPTH, D), 0.02),
        'w_mod': nrm((DEPTH, D, 6 * D), 0.5 * D ** -0.5),
        'b_mod': nrm((DEPTH, 6 * D), 0.02),
        'w_in': nrm((DEPTH, D, N_IN), D ** -0.5),
        'dn_conv_w': nrm((DEPTH, DN_CONV, 3 * DN_W), DN_CONV ** -0.5),
        'dn_a_log': jnp.log(jax.random.uniform(next(ks), (DEPTH, 2, DN_HEADS), F32, minval=1.0, maxval=16.0)),
        'dn_dt_bias': dt + jnp.log(-jnp.expm1(-dt)),
        'dn_norm_g': 1.0 + nrm((DEPTH, DN_DV), 0.02),
        'da_lambda': nrm((DEPTH, 4, DA_DH), 0.1),
        'da_subln_g': 1.0 + nrm((DEPTH, DA_DV), 0.02),
        'hy_conv_w': nrm((DEPTH, HY_SHORT, 3 * HY_W), HY_SHORT ** -0.5),
        'hy_conv_b': nrm((DEPTH, 3 * HY_W), 0.02),
        'hy_w1': nrm((DEPTH, HY_EMB, HY_ORDER), HY_EMB ** -0.5),
        'hy_b1': nrm((DEPTH, HY_ORDER), 0.02),
        'hy_freq': 1.0 + nrm((DEPTH, HY_ORDER), 0.02),
        'hy_w2': nrm((DEPTH, HY_ORDER, HY_ORDER), HY_ORDER ** -0.5),
        'hy_b2': nrm((DEPTH, HY_ORDER), 0.02),
        'hy_w3': nrm((DEPTH, HY_ORDER, HY_W), HY_ORDER ** -0.5),
        'hy_d': nrm((DEPTH, HY_W), 1.0),
        'w_br_a': nrm((DEPTH, DN_W, D), DN_W ** -0.5),
        'w_br_b': nrm((DEPTH, DA_V, D), DA_V ** -0.5),
        'w_br_c': nrm((DEPTH, HY_W, D), HY_W ** -0.5),
        'w_out': nrm((DEPTH, D, D), D ** -0.5),
        'w_ffn_in': nrm((DEPTH, D, 2 * D_FF), D ** -0.5),
        'w_ffn_out': nrm((DEPTH, D_FF, D), D_FF ** -0.5),
        'final_g': 1.0 + nrm((D,), 0.02),
    }

def reference(x_prompt, x_sample, cache_k, cache_v, state_dn, c, c_ctx, norm1_g, norm2_g, w_mod, b_mod,
              w_in, dn_conv_w, dn_a_log, dn_dt_bias, dn_norm_g, da_lambda, da_subln_g, hy_conv_w,
              hy_conv_b, hy_w1, hy_b1, hy_freq, hy_w2, hy_b2, hy_w3, hy_d, w_br_a, w_br_b, w_br_c,
              w_out, w_ffn_in, w_ffn_out, final_g):
    rope = axial_rope_tables(x_sample.shape[1])
    ctx_cond = jax.nn.silu(c_ctx)[None, :]
    lat_cond = jax.nn.silu(c)
    xp = x_prompt
    xs = x_sample
    new_k, new_v, new_s = [], [], []
    for l in range(DEPTH):
        lp = {
            'norm1_g': norm1_g[l], 'norm2_g': norm2_g[l], 'w_mod': w_mod[l], 'b_mod': b_mod[l],
            'w_in': w_in[l], 'dn_conv_w': dn_conv_w[l], 'dn_a_log': dn_a_log[l],
            'dn_dt_bias': dn_dt_bias[l], 'dn_norm_g': dn_norm_g[l], 'da_lambda': da_lambda[l],
            'da_subln_g': da_subln_g[l], 'hy_conv_w': hy_conv_w[l], 'hy_conv_b': hy_conv_b[l],
            'hy_w1': hy_w1[l], 'hy_b1': hy_b1[l], 'hy_freq': hy_freq[l], 'hy_w2': hy_w2[l],
            'hy_b2': hy_b2[l], 'hy_w3': hy_w3[l], 'hy_d': hy_d[l], 'w_br_a': w_br_a[l],
            'w_br_b': w_br_b[l], 'w_br_c': w_br_c[l], 'w_out': w_out[l], 'w_ffn_in': w_ffn_in[l],
            'w_ffn_out': w_ffn_out[l],
        }
        xp, (k_l, v_l, s_l) = trunk_layer(xp, ctx_cond, l, lp, None, None)
        new_k.append(k_l)
        new_v.append(v_l)
        new_s.append(s_l)
        xs, _ = trunk_layer(xs, lat_cond, l, lp, rope, (cache_k[:, l], cache_v[:, l], state_dn[:, l]))
    y_prompt = rmsnorm(xp, final_g)
    y_sample = rmsnorm(xs, final_g)
    new_cache_k = jnp.stack(new_k, axis=1)
    new_cache_v = jnp.stack(new_v, axis=1)
    new_state_dn = jnp.stack(new_s, axis=1)
    return (y_prompt, y_sample, new_cache_k, new_cache_v, new_state_dn)


_drawn_inputs = setup_inputs


def setup_inputs(seed=0):
    import zlib

    import numpy as np

    out = dict(_drawn_inputs(seed))
    spreads = {}
    factors = {'state_dn': 3.935,
     'norm2_g': 7.4,
     'dn_norm_g': 8.0,
     'da_lambda': 3.672,
     'da_subln_g': 8.0,
     'hy_conv_b': 6.801,
     'hy_b1': 8.0,
     'hy_freq': 8.0,
     'hy_b2': 8.0,
     'final_g': 2.848}
    for name, (base, spread) in spreads.items():
        noise = np.random.default_rng([zlib.crc32(name.encode()), seed]).standard_normal(out[name].shape)
        drawn = base * np.exp(spread * noise) if base else spread * noise
        out[name] = jnp.asarray(drawn.astype(out[name].dtype))
    for name, factor in factors.items():
        out[name] = (out[name] * factor).astype(out[name].dtype)
    return out
```

```python
from contextlib import ExitStack
import math

import numpy as np
import concourse.bass as bass
from concourse import mybir
from concourse.alu_op_type import AluOpType as ALU

F32 = mybir.dt.float32
ACT = mybir.ActivationFunctionType
AX_X = mybir.AxisListType.X

P = 128
D = 1024
KC = D // P
DEPTH = 2
NS, NP = 512, 128
NT = NS + NP
NCH = NT // P
H = 4
EPS = 1e-6
D_FF = 2816
FT = D_FF // P
GRID_W = 64
PADW = 648
CW = NS + 2 + NP
NLEV = 7
L_S, L_P = 768, 192
FQ_S, FQ_P = L_S // 2, L_P // 2
TWO_PI = 2.0 * math.pi
RING = 2
PANEL = 2048

N_MOD, N_A, N_B, N_V, N_C, N_MIX, N_OUT, N_F1, N_F2 = 24, 8, 4, 2, 6, 18, 4, 22, 12
AT_MOD = 0
AT_A = AT_MOD + N_MOD
AT_B = AT_A + N_A
AT_V = AT_B + N_B
AT_C = AT_V + N_V
AT_MIX = AT_C + N_C
AT_OUT = AT_MIX + N_MIX
AT_F1 = AT_OUT + N_OUT
AT_F2 = AT_F1 + N_F1
PANELS = AT_F2 + N_F2
assert PANELS % RING == 0


def offsets(parts):
    at, out = 0, {}
    for name, width in parts:
        out[name] = (at, at + width)
        at += width
    return out, at


PAR, N_PAR = offsets([
    ("b_mod", 48), ("g1", KC), ("g2", KC), ("conv", 60), ("hconv", 36), ("hconv_b", 12), ("a_log", 8),
    ("dt_bias", 8), ("dn_g", 1), ("sub_g", 1), ("lam", 256), ("w_ba", KC * 16), ("hy_w1", 64), ("hy_b1", 1),
    ("hy_fr", 1), ("hy_b2", 1), ("hy_w2", 64), ("hy_w3", 512), ("hy_d", 4), ("state", 8 * P), ("k_ctx", H * P),
    ("v_ctx", H * P), ("lam_init", 1), ("one_minus_lam", 1)])
CON, N_CON = offsets([
    ("ident", P), ("ones", P), ("tri", 2 * P), ("big", 2 * P), ("perm", P), ("levels", NLEV * 2 * P),
    ("final_g", KC), ("cond", KC * 2)])
ROPE, N_ROPE = offsets([("cos", NS), ("sin", NS)])
HYC, N_HYC = offsets([("z", NT), ("deltas", 512), ("ndist", NCH)])
N_FWD = 4 * L_S + L_P
N_INV = 6 * NS + 2 * NP


class Turns:

    def __init__(self, plan):
        total = {}
        self.where = {}
        for phase, times, fills in plan:
            per = {}
            for name, bank in fills:
                self.where[phase, name] = (bank, total.get(bank, 0), per.get(bank, 0))
                per[bank] = per.get(bank, 0) + 1
            for name, bank in fills:
                b, base, k = self.where[phase, name]
                self.where[phase, name] = (b, base, k, per[b])
            for b, n in per.items():
                total[b] = total.get(b, 0) + times * n
        self.total = total

    def at(self, phase, name, layer, step=0):
        bank, base, k, per = self.where[phase, name]
        return bank, layer * self.total[bank] + step * per + (base + k + 1)


def gemm_fills(panels):
    out = []
    for s in range(panels):
        out += [(f"s0_{s}", "G0"), (f"s1_{s}", "G1"), (f"p_{s}", "GP")]
    return out


GROUPS = [("f", 0, 4), ("b", 4, 4), ("p", 8, 2)]


def delta_fills():
    names = ["R_f", "R_b", "R_p", "ssq_q", "ssq_k", "ssq_p", "tok_k", "tok_v", "tok_p", "KK_s", "QK_s", "KQ_p"]
    names += [f"X0_{g}" for g, _, _ in GROUPS]
    for lev in range(1, NLEV):
        names += [f"P{lev}_{g}" for g, _, _ in GROUPS]
        for g, _, _ in GROUPS:
            names += [f"D{lev}_{g}"] if lev < NLEV - 1 else []
            names += [f"E{lev}_{g}"]
    names += ["vn_pf", "vn_pb", "o_p"]
    for step in range(4):
        names += [f"kq{step}_f", f"kq{step}_b", f"vn{step}_f", f"vn{step}_b", f"o{step}_f", f"o{step}_b"]
    names += ["oT_s", "oT_p"]
    return [(n, f"M{i % 5}") for i, n in enumerate(names)]


PLAN = [
    ("mod", N_MOD // 2, [("mod0", "M0"), ("mod1", "M1")]),
    ("norm1", 1, [("ss_s", "M2"), ("ss_p", "M3")]),
    ("gemmA", N_A // 2, gemm_fills(2)),
    ("ba", 1, [("ba", "M4"), ("cum", "M0")]),
    ("delta", H, delta_fills()),
    ("gemmB", N_B // 2, gemm_fills(2)),
    ("gemmV", 1, gemm_fills(2)),
    ("attn", H, [("rot_q", "M0"), ("rot_k", "M1")]
     + [f for qb in range(4) for f in ((f"S0_{qb}a", "M0"), (f"S0_{qb}b", "M1"), (f"S1_{qb}a", "M2"),
                                       (f"S1_{qb}b", "M3"), (f"T4_{qb}", "M4"), (f"T1_{qb}", "M4"))]
     + [("S_p0", "M0"), ("S_p1", "M2"), ("T_p", "M4"), ("o_s", "M1"), ("o_p", "M3"), ("oss_s", "M0"),
        ("oss_p", "M2")]),
    ("gemmC", N_C // 2, gemm_fills(2)),
    ("hyfil", 1, [("h1_s", "M0"), ("h1_p", "M1"), ("h2_s", "M2"), ("h2_p", "M3")]
     + [(f"h3_{c}", f"M{c}") for c in range(NCH)] + [("norm", "M0")]
     + [(f"H{i}", f"M{(i + 1) % 5}") for i in range(8)]),
    ("hytr", 4, [("g_s", "M0"), ("g_p", "M1")]),
    ("hydft", 1, [(f"X{i}", f"M{i % 5}") for i in range(8)]
     + [(f"y_s{c}", f"M{(c + 3) % 5}") for c in range(4)] + [("y_p", "M2")]),
    ("mix", 3, [f for half in range(2) for f in
                [(f"{n}_g{s}_{half}", b) for s in range(2) for n, b in (("s0", "G0"), ("s1", "G1"), ("p", "GP"))]
                + [(f"{n}_b{s}_{half}", b) for s in range(2) for n, b in (("s0", "G0"), ("s1", "G1"), ("p", "GP"))]]),
    ("out", N_OUT // 2, gemm_fills(2)),
    ("norm2", 1, [("ss_s", "M0"), ("ss_p", "M1")]),
    ("ffn1", N_F1 // 2, gemm_fills(2)),
    ("ffn2", 2, gemm_fills(2)),
]
TURNS = Turns(PLAN)
BANKS = ["M0", "M1", "M2", "M3", "M4", "G0", "G1", "GP"]


class Signal:

    def __init__(self, sem, per):
        self.sem, self.per = sem, per

    def at(self, step, k):
        return step * self.per + k


def trunk_program(nc, W, PARAMS, CONSTS, ROPES, HYCS, FWD, INV, X, Y, KNEW, VNEW, SNEW):
    ctx = ExitStack()
    with ctx:
        def sb(name, cols):
            return ctx.enter_context(nc.sbuf_tensor(name, [P, cols], F32))

        x = sb("x", KC * NT)
        h = sb("h", KC * NT)
        ring = sb("ring", RING * PANEL)
        big = sb("big", 16 * PADW + 12 * NT)
        outs = sb("outs", 12 * NT)
        par = sb("par", N_PAR)
        con = sb("con", N_CON)
        modc = sb("modc", 48 * 2)
        gain = sb("gain", 2 * KC * 2)
        cond = sb("cond_s", KC * 2)
        col = sb("col", 440)
        small = sb("small", 96)
        sc = sb("sc", 6410)

        xv = x[:, :].rearrange("p (k t) -> p k t", k=KC)
        hv = h[:, :].rearrange("p (k t) -> p k t", k=KC)
        rv = ring[:, :].rearrange("p (s n) -> p s n", s=RING)
        PA = big[:, 0:16 * PADW].rearrange("p (i t) -> p i t", t=PADW)
        PB0 = 16 * PADW
        ov = outs[:, :].rearrange("p (i t) -> p i t", t=NT)
        modv = modc[:, :].rearrange("p (n s) -> p n s", s=2)
        gainv = gain[:, :].rearrange("p (i n s) -> p i n s", i=2, s=2)
        condv = cond[:, :].rearrange("p (k s) -> p k s", s=2)
        pads = [PA[:, :, 0:2], PA[:, :, 514:516], PA[:, :, 644:648]]

        def pr(name, rows=P):
            a, b = PAR[name]
            return par[0:rows, a:b]

        def cn(name, rows=P):
            a, b = CON[name]
            return con[0:rows, a:b]

        def cut(tensor, at, *shape):
            n = int(np.prod(shape))
            v = tensor[:, at:at + n]
            if len(shape) == 2:
                v = v.rearrange("p (a b) -> p a b", a=shape[0])
            if len(shape) == 3:
                v = v.rearrange("p (a b c) -> p a b c", a=shape[0], b=shape[1])
            return v

        ident, ones = cn("ident"), cn("ones")
        tri = cn("tri").rearrange("p (d n) -> p d n", d=2)
        bigm = cn("big").rearrange("p (d n) -> p d n", d=2)
        levels = cn("levels").rearrange("p (l d n) -> p l d n", l=NLEV, d=2)

        def repeated(ap, n):
            return ap.unsqueeze(1).to_broadcast([P, n, ap.shape[-1]])

        cv = cut(sc, 0, 3, CW)
        sq = cut(sc, 1926, 2, NT)
        ktok = cut(sc, 3206, NCH, P)
        vtok = cut(sc, 3846, NCH, P)
        oacc = cut(sc, 4486, NCH, P)
        rr = cut(sc, 5126, 2, P)
        vn = cut(sc, 5382, 4, P)
        t1 = cut(sc, 5894, 2, P)
        S = cut(sc, 6150, 2, P)
        DT = cut(big, PB0, 10, P)
        AT = cut(big, PB0 + 1280, 10, P)
        GU = cut(big, PB0 + 2560, 10, P)
        kd = cut(big, PB0 + 3840, 10, P)
        snew = cut(big, PB0 + 5120, 8, P)
        X_ = cut(outs, 4 * NT, 10, P)
        XT = cut(outs, 4 * NT + 1280, 10, P)
        AL = cut(outs, 4 * NT + 2560, 10, P)
        PS = cut(outs, 4 * NT + 3840, 10, P)
        tok5 = (NCH, 8)
        beta = cut(col, 0, *tok5)
        gg = cut(col, 40, *tok5)
        gcum = cut(col, 80, *tok5)
        ngc = cut(col, 120, *tok5)
        egc = cut(col, 160, *tok5)
        negc = cut(col, 200, *tok5)
        egl = cut(col, 240, *tok5)
        ekd = cut(col, 280, *tok5)
        tmpc = cut(col, 320, *tok5)
        tmpd = cut(col, 360, *tok5)
        expa = cut(col, 400, 8)
        orn = cut(col, 408, NCH)
        epsc = cut(small, 0, 4)
        lamc = cut(small, 4, 8)
        subg = cut(small, 12, 1)
        mx = cut(small, 16, 2, 2)
        rsum = cut(small, 24, 2, 2)
        rinv = cut(small, 32, 2, 2)
        hyn = cut(small, 40, 2, 4)

        gh = cut(small, 48, NCH, 2)
        eh = cut(small, 58, NCH, 2)

        PBq = cut(big, PB0, 8, NT)
        VB = cut(big, PB0 + 8 * NT, NCH, 512)
        rope = sc[:, 0:N_ROPE]
        qall = cut(sc, 1024, NT)
        kall = cut(sc, 1664, 768)
        vall = cut(sc, 2432, 6, P)
        rtmp = cut(sc, 3200, NS)
        osb = cut(sc, 3712, NT)
        osq = cut(sc, 4352, NT)
        pp = cut(big, 0, 2, 2, NT)
        aa = cut(big, 2560, 2, NT)
        aT = cut(big, 3840, NCH, NS)
        aTp = cut(big, 6400, P)
        knew = cut(big, 6528, H, P)

        hyc = cut(big, 12 * PADW, N_HYC)
        fwd = cut(big, PB0, N_FWD)
        Hs = cut(big, PB0 + N_FWD, 8, NS)
        inv = cut(big, 4 * PADW, N_INV)
        Ys = cut(sc, 0, 6, NS)
        Yp = cut(big, 4 * PADW + N_INV, 2, NS)
        tok = cut(sc, 3072, NCH, 512)
        arg = cut(sc, 0, NT)
        redu = cut(sc, 640, NT)
        hdn = cut(sc, 1280, NT)
        dec = cut(sc, 1920, 512)
        ABSH = [cut(big, PB0 + N_FWD + c * 512, 512) for c in range(NCH)]
        hx1 = cut(sc, 0, CW)
        hv_ = cut(sc, 642, CW)
        ytmp = cut(sc, 1284, NT)
        gv = PA[:, 0:4, 0:NT]
        x0 = ov[:, 8:12, :]

        merged = cut(big, PB0, KC, NT)
        sig = cut(sc, 0, 4, NT)
        mtmp = cut(sc, 2560, 2, NT)
        actv = cut(big, 0, FT, NT)
        gsil = cut(sc, 0, 2, NT)
        rstd = cut(sc, 3840, NT)

        psum = {b: ctx.enter_context(nc.psum_tensor(f"ps_{b}", [P, 512], F32)) for b in ("M4", "G0", "G1", "GP")}
        pair0 = ctx.enter_context(nc.psum_tensor("ps_M01", [P, 1024], F32))
        pair1 = ctx.enter_context(nc.psum_tensor("ps_M23", [P, 1024], F32))
        bank = {b: psum[b][:, :] for b in psum}
        bank.update(M0=pair0[:, 0:512], M1=pair0[:, 512:1024], M2=pair1[:, 0:512], M3=pair1[:, 512:1024])

        def sem(name):
            return ctx.enter_context(nc.semaphore(name))

        def sig_(name, per):
            return Signal(sem(name), per)

        filled = {b: sem(f"filled_{b}") for b in BANKS}
        freed = {b: sem(f"freed_{b}") for b in BANKS}
        landed = [sem(f"panel_landed_{s}") for s in range(RING)]
        panel_used = sem("panel_used")
        consts_in = sem("consts_in")
        passed = sem("passed")
        cond_ready = sem("cond_ready")
        par_in = sig_("params_in", 16)
        rope_in = sig_("rope_in", 16)
        hyc_in = sig_("hyena_consts_in", 16)
        fwd_in = sig_("fwd_dft_in", 16)
        inv_in = sig_("inv_dft_in", 16)
        y_stored = sem("y_stored")
        state_stored = sig_("state_stored", 16)
        cache_stored = sig_("cache_stored", 32)
        attn_room = sem("attn_rooms_free")
        layer_done = sig_("layer_done", 1)
        pads_zero = sig_("pads_zero", 2)
        sq_ready = sig_("squares_ready", 2 * KC)
        rms_ready = sig_("rms_ready", 2)
        hnorm = sig_("h_scaled", 2 * KC)
        h_ready = sig_("h_ready", 2)
        proj_a = sig_("proj_a_ready", 1)
        g_ready = sig_("g_ready", 1)
        beta_done = sig_("beta_done", 1)
        ab_lin = sig_("alpha_biased", 1)
        sp_ready = sig_("softplus_parts", 1)
        cums = sig_("cumsums_copied", 1)
        cumx = sig_("cumsum_exps", 1)
        gu_ready = sig_("gu_ready", 1)
        kd_ready = sig_("kd_ready", 1)
        conv_done = sig_("conv_done", 3)
        silu_done = sig_("silu_done", 3)
        rq_ready = sig_("rq_ready", 1)
        qk_ready = sig_("qk_normalised", 1)
        tok_ready = sig_("tok_ready", 1)
        decay = sig_("decay_ready", 3)
        at_ready = sig_("at_ready", 3)
        al_ready = sig_("al_ready", 3 * NLEV)
        xt_ready = sig_("xt_ready", 3 * NLEV)
        x_ready = sig_("x_ready", 3 * (NLEV - 2))
        x0_ready = sig_("x0_ready", 3)
        p_ready = sig_("p_copied", 3 * (NLEV - 1))
        qkd_ready = sig_("qkd_ready", 1)
        r_ready = sig_("r_ready", 8)
        vn_ready = sig_("vn_ready", 10)
        s_ready = sig_("s_ready", 7)
        osum = sig_("o_summed", 1)
        orms = sig_("o_rms", 1)
        oscaled = sig_("o_scaled", 1)
        siluz = sig_("silu_z", 1)
        head_done = sig_("delta_head_done", 1)
        proj_b = sig_("proj_b_ready", 1)
        lam_done = sig_("lambda_ready", 2)
        lam_dot = sig_("lambda_dots", 1)
        qcopy = sig_("attn_copies", 1)
        rot_done = sig_("rotated", 2)
        neg_max = sig_("neg_max", 10)
        exp_done = sig_("exp_done", 10)
        a_ready = sig_("a_ready", 5)
        at_copied = sig_("aT_copied", 9)
        o_copied = sig_("o_copied", 2)
        osq_done = sig_("o_squared", 1)
        orms_b = sig_("o_rms_b", 1)
        attn_done = sig_("attn_head_done", 1)
        proj_c = sig_("proj_c_ready", 1)
        arg_ready = sig_("arg_ready", 2)
        sin_done = sig_("sin_done", 2)
        dec_ready = sig_("decay_table", NCH)
        filt_ready = sig_("filter_ready", NCH)
        abs_ready = sig_("abs_ready", NCH)
        spec_ready = sig_("filter_spectrum", 8)
        gv_ready = sig_("gv_ready", 1)
        x0_done = sig_("x0_done", 1)
        gvtok = sem("gv_by_token")
        xprod = sig_("spectra_multiplied", 4)
        hy_done = sig_("hyena_done", 1)
        gates = sem("gates_ready")
        merge = sem("merge_done")
        merged_ready = sig_("merged_ready", 1)
        xres1 = sig_("x_after_mix", 1)
        gate_silu = sem("gate_silu")
        act_ready = sem("act_ready")
        y_ready = sem("y_ready")

        block = ctx.enter_context(nc.Block())

        def turn(phase, name, layer, step=0):
            b, n = TURNS.at(phase, name, layer, step)
            return bank[b], filled[b], freed[b], n

        G3 = [(0, 0, 4), (1, 4, 4), (2, 8, 2)]

        @block.sync
        def _(sp):
            sp.dma_start(xv, X).then_inc(consts_in, 16)
            sp.dma_start(con[:, :], CONSTS).then_inc(consts_in, 16)
            for s in range(RING):
                sp.dma_start(rv[:, s, :], W[s]).then_inc(landed[s], 16)
            with sp.Fori(1, DEPTH * PANELS // RING) as i:
                for s in range(RING):
                    sp.wait_ge(panel_used, i * RING + (s - RING + 1))
                    sp.dma_start(rv[:, s, :], W[bass.ds(i * RING + s, 1)].rearrange("a p n -> p (a n)")
                                 ).then_inc(landed[s], 16)
            sp.wait_ge(y_ready, 2)
            sp.dma_start(Y, hv).then_inc(y_stored, 16)
            sp.wait_ge(y_stored, 16)
            sp.wait_ge(state_stored.sem, 16 * DEPTH)
            sp.wait_ge(cache_stored.sem, 32 * DEPTH)

        @block.tensor
        def _(pe):
            def panel(layer, at, step=0, per=0):
                s = at % RING
                pe.wait_ge(landed[s], 16 * (layer * (PANELS // RING) + step * (per // RING) + (at // RING + 1)))
                return rv[:, s, :].rearrange("p (k n) -> p k n", k=KC)

            def used():
                pe.drain().then_inc(panel_used, 1)

            def fill(phase, name, layer, step=0):
                ap, fl, fr, n = turn(phase, name, layer, step)
                pe.wait_ge(fr, n)
                return ap, fl

            def product(phase, names, layer, step, w, src, tiles=2):
                for t in range(2):
                    ap, fl = fill(phase, names[t], layer, step)
                    for k in range(KC):
                        m = pe.matmul(ap, w[:, k, t * P:(t + 1) * P], src[:, k, 0:NS], start=(k == 0), stop=(k == KC - 1))
                    m.then_inc(fl, 1)
                ap, fl = fill(phase, names[2], layer, step)
                for t in range(2):
                    for k in range(KC):
                        m = pe.matmul(ap[:, t * P:(t + 1) * P], w[:, k, t * P:(t + 1) * P], src[:, k, NS:NT],
                                      start=(k == 0), stop=(k == KC - 1))
                m.then_inc(fl, 1)

            def sum_squares(phase, layer, src, k_count, wait):
                aps, fls = fill(phase, "ss_s", layer)
                app, flp = fill(phase, "ss_p", layer)
                for k in range(k_count):
                    pe.wait_ge(wait.sem, wait.at(layer, (0 if phase == "norm1" else KC) + k + 1))
                    ms = pe.matmul(aps, ones, src[:, k, 0:NS], start=(k == 0), stop=(k == k_count - 1))
                    if k == k_count - 1:
                        ms.then_inc(fls, 1)
                    mp = pe.matmul(app[:, 0:NP], ones, src[:, k, NS:NT], start=(k == 0), stop=(k == k_count - 1))
                mp.then_inc(flp, 1)

            pe.wait_ge(consts_in, 32)
            with pe.Fori(0, DEPTH) as L:
                pe.wait_ge(cond_ready, 1)
                with pe.Fori(0, N_MOD // 2) as i:
                    for s in range(2):
                        w = panel(L, AT_MOD + s, i, 2)
                        ap, fl = fill("mod", f"mod{s}", L, i)
                        for t in range(2):
                            for k in range(KC):
                                m = pe.matmul(ap[:, 2 * t:2 * t + 2], w[:, k, t * P:(t + 1) * P], condv[:, k, :],
                                              start=(k == 0), stop=(k == KC - 1))
                        m.then_inc(fl, 1)
                        used()
                sum_squares("norm1", L, hv, KC, sq_ready)
                pe.wait_ge(h_ready.sem, h_ready.at(L, 1))
                pe.sem_inc(passed, 1)
                with pe.Fori(0, N_A // 2) as i:
                    for s in range(2):
                        w = panel(L, AT_A + s, i, 2)
                        product("gemmA", (f"s0_{s}", f"s1_{s}", f"p_{s}"), L, i, w, hv)
                        used()
                pe.wait_ge(par_in.sem, par_in.at(L, 16))
                w_ba = pr("w_ba").rearrange("p (k n) -> p k n", k=KC)
                ap, fl = fill("ba", "ba", L)
                for c in range(NCH):
                    for k in range(KC):
                        m = pe.matmul(ap[:, c * 16:(c + 1) * 16], hv[:, k, c * P:(c + 1) * P], w_ba[:, k, :],
                                      start=(k == 0), stop=(k == KC - 1))
                m.then_inc(fl, 1)
                pe.wait_ge(g_ready.sem, g_ready.at(L, 1))
                ap, fl = fill("ba", "cum", L)
                gflat = col[:, 40:80]
                pe.matmul(ap[:, 0:40], tri[:, 0, :], gflat, start=True, stop=True)
                pe.matmul(ap[:, 40:80], tri[:, 1, :], gflat, start=True, stop=True)
                pe.matmul(ap[:, 80:120], ones, gflat, start=True, stop=True).then_inc(fl, 1)

                with pe.Fori(0, H) as hd:
                    Q = L * H + hd

                    def f(name):
                        return fill("delta", name, L, hd)

                    pe.wait_ge(gu_ready.sem, gu_ready.at(Q, 1))
                    for g, first, n in G3:
                        ap, fl = f(["R_f", "R_b", "R_p"][g])
                        bm = bigm if g == 2 else repeated(bigm[:, g, :], 4)
                        pe.matmul(ap[:, 0:n * P].rearrange("p (a b) -> p a b", a=n), ident, bm, start=True, stop=False,
                                  skip_group_check=True)
                        for c in range(n):
                            m = pe.matmul(ap[:, c * P:(c + 1) * P], ones, GU[:, first + c, :], start=False,
                                          stop=(c == n - 1), skip_group_check=True)
                        m.then_inc(fl, 1)
                    pe.wait_ge(silu_done.sem, silu_done.at(Q, 2))
                    for j, name in enumerate(("ssq_q", "ssq_k")):
                        ap, fl = f(name)
                        pe.matmul(ap, ones, sq[:, j, 0:NS], start=True, stop=True).then_inc(fl, 1)
                    ap, fl = f("ssq_p")
                    for j in range(2):
                        m = pe.matmul(ap[:, j * P:(j + 1) * P], ones, sq[:, j, NS:NT], start=True, stop=True)
                    m.then_inc(fl, 1)
                    pe.wait_ge(qk_ready.sem, qk_ready.at(Q, 1))
                    pe.wait_ge(silu_done.sem, silu_done.at(Q, 3))
                    for j, name in ((1, "tok_k"), (2, "tok_v")):
                        ap, fl = f(name)
                        for c in range(4):
                            m = pe.transpose(ap[:, c * P:(c + 1) * P], cv[:, j, c * P:(c + 1) * P], ident)
                        m.then_inc(fl, 1)
                    ap, fl = f("tok_p")
                    for j in (1, 2):
                        m = pe.transpose(ap[:, (j - 1) * P:j * P], cv[:, j, NS + 2:NS + 2 + P], ident)
                    m.then_inc(fl, 1)

                    def qk(j, c):
                        at = c * P if c < 4 else NS + 2
                        return cv[:, j, at:at + P]

                    for j, name in ((1, "KK_s"), (0, "QK_s")):
                        ap, fl = f(name)
                        for c in range(4):
                            m = pe.matmul(ap[:, c * P:(c + 1) * P], qk(1, c), qk(j, c), start=True, stop=True)
                        m.then_inc(fl, 1)
                    ap, fl = f("KQ_p")
                    for i, j in enumerate((1, 0)):
                        m = pe.matmul(ap[:, i * P:(i + 1) * P], qk(1, 4), qk(j, 4), start=True, stop=True)
                    m.then_inc(fl, 1)
                    for g, first, n in G3:
                        pe.wait_ge(xt_ready.sem, xt_ready.at(Q, g + 1))
                        ap, fl = f(f"X0_{GROUPS[g][0]}")
                        for c in range(n):
                            m = pe.transpose(ap[:, c * P:(c + 1) * P], XT[:, first + c, :], ident)
                        m.then_inc(fl, 1)
                    for lev in range(1, NLEV):
                        for g, first, n in G3:
                            pe.wait_ge(al_ready.sem, al_ready.at(Q, 3 * lev + g + 1))
                            if lev == 1:
                                pe.wait_ge(x0_ready.sem, x0_ready.at(Q, g + 1))
                            else:
                                pe.wait_ge(x_ready.sem, x_ready.at(Q, 3 * (lev - 2) + g + 1))
                            ap, fl = f(f"P{lev}_{GROUPS[g][0]}")
                            for c in range(n):
                                m = pe.matmul(ap[:, c * P:(c + 1) * P], AL[:, first + c, :], X_[:, first + c, :],
                                              start=True, stop=True)
                            m.then_inc(fl, 1)
                        for g, first, n in G3:
                            pe.wait_ge(p_ready.sem, p_ready.at(Q, 3 * (lev - 1) + g + 1))
                            if lev > 1:
                                pe.wait_ge(xt_ready.sem, xt_ready.at(Q, 3 * (lev - 1) + g + 1))
                            if lev < NLEV - 1:
                                ap, fl = f(f"D{lev}_{GROUPS[g][0]}")
                                for c in range(n):
                                    m = pe.matmul(ap[:, c * P:(c + 1) * P], XT[:, first + c, :], PS[:, first + c, :],
                                                  start=True, stop=True)
                                m.then_inc(fl, 1)
                            ap, fl = f(f"E{lev}_{GROUPS[g][0]}")
                            for c in range(n):
                                m = pe.matmul(ap[:, c * P:(c + 1) * P], PS[:, first + c, :], XT[:, first + c, :],
                                              start=True, stop=True)
                            m.then_inc(fl, 1)
                    for d in range(2):
                        pe.wait_ge(xt_ready.sem, xt_ready.at(Q, 3 * (NLEV - 1) + 3))
                        ap, fl = f(["vn_pf", "vn_pb"][d])
                        pe.matmul(ap[:, 0:P], XT[:, 8 + d, :], vtok[:, 4, :], start=True, stop=True).then_inc(fl, 1)
                    pe.wait_ge(vn_ready.sem, vn_ready.at(Q, 2))
                    pe.wait_ge(qkd_ready.sem, qkd_ready.at(Q, 1))
                    pe.wait_ge(kd_ready.sem, kd_ready.at(Q, 1))
                    ap, fl = f("o_p")
                    pe.matmul(ap[:, 0:P], DT[:, 8, :], vn[:, 2, :], start=True, stop=False)
                    pe.matmul(ap[:, 0:P], DT[:, 9, :], vn[:, 3, :], start=False, stop=True)
                    pe.matmul(ap[:, P:2 * P], kd[:, 8, :], vn[:, 2, :], start=True, stop=True)
                    pe.matmul(ap[:, 2 * P:3 * P], kd[:, 9, :], vn[:, 3, :], start=True, stop=True).then_inc(fl, 1)
                    for step in range(4):
                        for d in range(2):
                            c = step if d == 0 else 3 - step
                            if step:
                                pe.wait_ge(s_ready.sem, s_ready.at(Q, 1 + 2 * (step - 1) + d + 1))
                            else:
                                pe.wait_ge(s_ready.sem, s_ready.at(Q, 1))
                            ap, fl = f(f"kq{step}_{'fb'[d]}")
                            pe.matmul(ap[:, 0:P], qk(1, c), S[:, d, :], start=True, stop=True)
                            pe.matmul(ap[:, P:2 * P], qk(0, c), S[:, d, :], start=True, stop=True).then_inc(fl, 1)
                        for d in range(2):
                            c = step if d == 0 else 3 - step
                            pe.wait_ge(r_ready.sem, r_ready.at(Q, 2 * step + d + 1))
                            ap, fl = f(f"vn{step}_{'fb'[d]}")
                            pe.matmul(ap[:, 0:P], XT[:, 4 * d + c, :], rr[:, d, :], start=True, stop=True).then_inc(fl, 1)
                        for d in range(2):
                            c = step if d == 0 else 3 - step
                            pe.wait_ge(vn_ready.sem, vn_ready.at(Q, 2 + 2 * step + d + 1))
                            ap, fl = f(f"o{step}_{'fb'[d]}")
                            m = pe.matmul(ap[:, 0:P], DT[:, 4 * d + c, :], vn[:, d, :], start=True, stop=True)
                            if step < 3:
                                m = pe.matmul(ap[:, P:2 * P], kd[:, 4 * d + c, :], vn[:, d, :], start=True, stop=True)
                            m.then_inc(fl, 1)
                    pe.wait_ge(oscaled.sem, oscaled.at(Q, 1))
                    ap, fl = f("oT_s")
                    for c in range(4):
                        m = pe.transpose(ap[:, c * P:(c + 1) * P], oacc[:, c, :], ident)
                    m.then_inc(fl, 1)
                    ap, fl = f("oT_p")
                    pe.transpose(ap[:, 0:P], oacc[:, 4, :], ident).then_inc(fl, 1)

                with pe.Fori(0, N_B // 2) as i:
                    for s in range(2):
                        w = panel(L, AT_B + s, i, 2)
                        product("gemmB", (f"s0_{s}", f"s1_{s}", f"p_{s}"), L, i, w, hv)
                        used()
                for s in range(2):
                    w = panel(L, AT_V + s)
                    for name, chunks in ((f"s0_{s}", (0, 1)), (f"s1_{s}", (2, 3)), (f"p_{s}", (4,))):
                        ap, fl = fill("gemmV", name, L)
                        for j, c in enumerate(chunks):
                            for k in range(KC):
                                m = pe.matmul(ap[:, j * 256:(j + 1) * 256], hv[:, k, c * P:(c + 1) * P], w[:, k, :],
                                              start=(k == 0), stop=(k == KC - 1))
                        m.then_inc(fl, 1)
                    used()

                with pe.Fori(0, H) as hd:
                    Q = L * H + hd

                    def f(name):
                        return fill("attn", name, L, hd)

                    pe.wait_ge(proj_b.sem, proj_b.at(L, 1))
                    for j, name in enumerate(("rot_q", "rot_k")):
                        ap, fl = f(name)
                        pe.matmul(ap, cn("perm"), PBq[:, bass.ds(hd + 4 * j, 1), 0:NS].rearrange("p a t -> p (a t)"),
                                  start=True, stop=True).then_inc(fl, 1)
                    pe.wait_ge(rot_done.sem, rot_done.at(Q, 2))
                    pe.wait_ge(qcopy.sem, qcopy.at(Q, 1))

                    def transposed(qb):
                        pe.wait_ge(a_ready.sem, a_ready.at(Q, qb + 1))
                        ap, fl = f(f"T4_{qb}")
                        for j in range(4):
                            m = pe.transpose(ap[:, j * P:(j + 1) * P], aa[:, qb % 2, j * P:(j + 1) * P], ident)
                        m.then_inc(fl, 1)
                        ap, fl = f(f"T1_{qb}")
                        pe.transpose(ap[:, 0:P], aa[:, qb % 2, 4 * P:5 * P], ident).then_inc(fl, 1)

                    for qb in range(4):
                        for m_ in range(2):
                            rows = slice(64 * m_, 64 * m_ + 64)
                            q_ = qall[rows, qb * P:(qb + 1) * P]
                            ap, fl = f(f"S{m_}_{qb}a")
                            pe.matmul(ap, q_, kall[rows, 0:NS], start=True, stop=True).then_inc(fl, 1)
                            ap, fl = f(f"S{m_}_{qb}b")
                            pe.matmul(ap[:, 0:P], q_, kall[rows, NS:NT], start=True, stop=True).then_inc(fl, 1)
                        if qb:
                            transposed(qb - 1)
                    for m_ in range(2):
                        rows = slice(64 * m_, 64 * m_ + 64)
                        ap, fl = f(f"S_p{m_}")
                        pe.matmul(ap[:, 0:P], qall[rows, NS:NT], kall[rows, NT:NT + P], start=True, stop=True
                                  ).then_inc(fl, 1)
                    transposed(3)
                    pe.wait_ge(a_ready.sem, a_ready.at(Q, 5))
                    ap, fl = f("T_p")
                    pe.transpose(ap[:, 0:P], aa[:, 0, 0:P], ident)
                    pe.transpose(ap[:, P:2 * P], kall[:, NT:NT + P], ident).then_inc(fl, 1)
                    pe.wait_ge(at_copied.sem, at_copied.at(Q, 8))
                    ap, fl = f("o_s")
                    for j in range(NCH):
                        m = pe.matmul(ap, vall[:, j, :], aT[:, j, :], start=(j == 0), stop=(j == NCH - 1))
                    m.then_inc(fl, 1)
                    pe.wait_ge(at_copied.sem, at_copied.at(Q, 9))
                    ap, fl = f("o_p")
                    pe.matmul(ap[:, 0:P], vall[:, 5, :], aTp, start=True, stop=True).then_inc(fl, 1)
                    pe.wait_ge(osq_done.sem, osq_done.at(Q, 1))
                    ap, fl = f("oss_s")
                    pe.matmul(ap, ones, osq[:, 0:NS], start=True, stop=True).then_inc(fl, 1)
                    ap, fl = f("oss_p")
                    pe.matmul(ap[:, 0:P], ones, osq[:, NS:NT], start=True, stop=True).then_inc(fl, 1)

                pe.wait_ge(attn_done.sem, attn_done.at(L, 0) * H + H)
                pe.sem_inc(passed, 1)
                with pe.Fori(0, N_C // 2) as i:
                    for s in range(2):
                        w = panel(L, AT_C + s, i, 2)
                        product("gemmC", (f"s0_{s}", f"s1_{s}", f"p_{s}"), L, i, w, hv)
                        used()
                pe.wait_ge(hyc_in.sem, hyc_in.at(L, 16))
                za, zb = HYC["z"]
                z_ = hyc[0:17, za:zb]
                for (name_s, name_p), wname, rows, src, k in ((("h1_s", "h1_p"), "hy_w1", 17, z_, 0),
                                                              (("h2_s", "h2_p"), "hy_w2", 64, hdn[0:64, :], 1)):
                    if k:
                        pe.wait_ge(sin_done.sem, sin_done.at(L, 1))
                    ap, fl = fill("hyfil", name_s, L)
                    pe.sem_inc(passed, 1)
                    pe.matmul(ap[0:64, :], pr(wname, rows), src[:, 0:NS], start=True, stop=True).then_inc(fl, 1)
                    ap, fl = fill("hyfil", name_p, L)
                    pe.sem_inc(passed, 1)
                    pe.matmul(ap[0:64, 0:NP], pr(wname, rows), src[:, NS:NT], start=True, stop=True).then_inc(fl, 1)
                pe.wait_ge(sin_done.sem, sin_done.at(L, 2))
                for c in range(NCH):
                    ap, fl = fill("hyfil", f"h3_{c}", L)
                    pe.matmul(ap, hdn[0:64, c * P:(c + 1) * P], pr("hy_w3", 64), start=True, stop=True).then_inc(fl, 1)
                ap, fl = fill("hyfil", "norm", L)
                for seq, chunks in ((0, (0, 1, 2, 3)), (1, (4,))):
                    for j in range(4):
                        for c in chunks:
                            if j == 0:
                                pe.wait_ge(abs_ready.sem, abs_ready.at(L, c + 1))
                            m = pe.matmul(ap[:, seq * 4 + j:seq * 4 + j + 1], ABSH[c][:, j * P:(j + 1) * P],
                                          ones[:, 0:1], start=(c == chunks[0]), stop=(c == chunks[-1]))
                m.then_inc(fl, 1)

                def spectra(phase, prefix):
                    for i in range(6):
                        ap, fl = fill(phase, f"{prefix}{i}", L)
                        for c in range(4):
                            m = pe.matmul(ap, fwd[:, c * L_S + i * P:c * L_S + (i + 1) * P], tok[:, c, :],
                                          start=(c == 0), stop=(c == 3))
                        m.then_inc(fl, 1)
                    for i in range(2):
                        ap, fl = fill(phase, f"{prefix}{6 + i}", L)
                        pe.matmul(ap[0:FQ_P, :], fwd[:, 4 * L_S + i * FQ_P:4 * L_S + (i + 1) * FQ_P], tok[:, 4, :],
                                  start=True, stop=True).then_inc(fl, 1)

                pe.wait_ge(fwd_in.sem, fwd_in.at(L, 16))
                pe.wait_ge(filt_ready.sem, filt_ready.at(L, NCH))
                spectra("hyfil", "H")
                with pe.Fori(0, 4) as j:
                    pe.wait_ge(gv_ready.sem, gv_ready.at(L * 4 + j, 1))
                    ap, fl = fill("hytr", "g_s", L, j)
                    for c in range(4):
                        m = pe.transpose(ap[:, c * P:(c + 1) * P], ytmp[:, c * P:(c + 1) * P], ident)
                    m.then_inc(fl, 1)
                    ap, fl = fill("hytr", "g_p", L, j)
                    pe.transpose(ap[:, 0:P], ytmp[:, NS:NT], ident).then_inc(fl, 1)
                pe.wait_ge(gvtok, L * 4 + 5)
                spectra("hydft", "X")
                pe.wait_ge(inv_in.sem, inv_in.at(L, 16))
                for j in range(4):
                    ap, fl = fill("hydft", f"y_s{j}", L)
                    for i in range(6):
                        if j == 0 and i < 3:
                            pe.wait_ge(xprod.sem, xprod.at(L, i + 1))
                        m = pe.matmul(ap, Ys[:, i, j * P:(j + 1) * P], inv[:, i * NS:(i + 1) * NS],
                                      start=(i == 0), stop=(i == 5))
                    m.then_inc(fl, 1)
                pe.wait_ge(xprod.sem, xprod.at(L, 4))
                ap, fl = fill("hydft", "y_p", L)
                for j in range(4):
                    for i in range(2):
                        m = pe.matmul(ap[:, j * P:(j + 1) * P], Yp[0:FQ_P, i, j * P:(j + 1) * P],
                                      inv[0:FQ_P, 6 * NS + i * NP:6 * NS + (i + 1) * NP], start=(i == 0), stop=(i == 1))
                m.then_inc(fl, 1)

                pe.wait_ge(hy_done.sem, hy_done.at(L, 1))
                pe.sem_inc(passed, 1)
                with pe.Fori(0, 3) as b:
                    for half in range(2):
                        for s in range(2):
                            w = panel(L, AT_MIX + 3 * half + s, b, 6)
                            product("mix", [f"{n}_g{s}_{half}" for n in ("s0", "s1", "p")], L, b, w, hv)
                            used()
                        s_ = (AT_MIX + 3 * half + 2) % RING
                        panel(L, AT_MIX + 3 * half + 2, b, 6)
                        w = rv[:, s_, :].rearrange("p (k n) -> p k n", k=4)
                        for s in range(2):
                            for t in range(2):
                                ap, fl = fill("mix", f"s{t}_b{s}_{half}", L, b)
                                for k in range(4):
                                    n0 = (2 * s + t) * P
                                    src = ov[:, bass.ds(b * 4 + k, 1), 0:NS].rearrange("p a t -> p (a t)")
                                    m = pe.matmul(ap, w[:, k, n0:n0 + P], src, start=(k == 0), stop=(k == 3))
                                m.then_inc(fl, 1)
                            ap, fl = fill("mix", f"p_b{s}_{half}", L, b)
                            for t in range(2):
                                for k in range(4):
                                    n0 = (2 * s + t) * P
                                    src = ov[:, bass.ds(b * 4 + k, 1), NS:NT].rearrange("p a t -> p (a t)")
                                    m = pe.matmul(ap[:, t * P:(t + 1) * P], w[:, k, n0:n0 + P], src,
                                                  start=(k == 0), stop=(k == 3))
                            m.then_inc(fl, 1)
                        used()
                pe.wait_ge(merged_ready.sem, merged_ready.at(L, 1))
                pe.sem_inc(passed, 1)
                with pe.Fori(0, N_OUT // 2) as i:
                    for s in range(2):
                        w = panel(L, AT_OUT + s, i, 2)
                        product("out", (f"s0_{s}", f"s1_{s}", f"p_{s}"), L, i, w, merged)
                        used()
                sum_squares("norm2", L, hv, KC, sq_ready)
                pe.wait_ge(h_ready.sem, h_ready.at(L, 2))
                pe.sem_inc(passed, 1)
                with pe.Fori(0, N_F1 // 2) as i:
                    for s in range(2):
                        w = panel(L, AT_F1 + s, i, 2)
                        product("ffn1", (f"s0_{s}", f"s1_{s}", f"p_{s}"), L, i, w, hv)
                        used()
                pe.wait_ge(act_ready, L * (N_F1 // 2) + (N_F1 // 2 + 1))
                pe.sem_inc(passed, 1)
                with pe.Fori(0, 2) as i:
                    for s in range(2):
                        a0, f0 = fill("ffn2", f"s0_{s}", L, i)
                        a1, f1 = fill("ffn2", f"s1_{s}", L, i)
                        a2, f2 = fill("ffn2", f"p_{s}", L, i)
                        for j in range(3):
                            w = panel(L, AT_F2 + 3 * s + j, i, 6)
                            n = min(KC, FT - KC * j)
                            last = j == 2
                            for t, (ap, fl) in enumerate(((a0, f0), (a1, f1))):
                                for k in range(n):
                                    m = pe.matmul(ap, w[:, k, t * P:(t + 1) * P], actv[:, KC * j + k, 0:NS],
                                                  start=(j == 0 and k == 0), stop=(last and k == n - 1))
                                if last:
                                    m.then_inc(fl, 1)
                            for t in range(2):
                                for k in range(n):
                                    m = pe.matmul(a2[:, t * P:(t + 1) * P], w[:, k, t * P:(t + 1) * P],
                                                  actv[:, KC * j + k, NS:NT], start=(j == 0 and k == 0 and t == 0),
                                                  stop=(last and k == n - 1), skip_group_check=True)
                            if last:
                                m.then_inc(f2, 1)
                            used()
            sum_squares("norm1", DEPTH, hv, KC, sq_ready)


        @block.scalar
        def _(act):
            def drained(phase, name, layer, step=0):
                ap, fl, fr, n = turn(phase, name, layer, step)
                act.wait_ge(fl, n)
                return ap, fr

            def copy_out(phase, names, layer, step, dst_s, dst_p, func=ACT.Copy, done=None):
                for t in range(2):
                    ap, fr = drained(phase, names[t], layer, step)
                    nc.scalar.activation(dst_s[t], ap, func).then_inc(fr, 1)
                ap, fr = drained(phase, names[2], layer, step)
                nc.scalar.activation(dst_p, ap[:, 0:2 * P].rearrange("p (a b) -> p a b", a=2), func).then_inc(fr, 1)

            def tiles(view, at, a, b):
                return view[:, bass.ds(at, 1), a:b].rearrange("p a t -> p (a t)")

            act.wait_ge(consts_in, 32)
            nc.scalar.activation(cond[:, :], cn("cond"), ACT.Silu).then_inc(cond_ready, 1)

            def squares(layer, base):
                for k in range(KC):
                    nc.scalar.activation(hv[:, k, :], xv[:, k, :], ACT.Square).then_inc(sq_ready.sem, 1)

            def rms_root(phase, layer, k):
                ap, fr = drained(phase, "ss_s", layer)
                nc.scalar.activation(rstd[:, 0:NS], ap, ACT.Sqrt, bias=epsc[:, 0:1], scale=1.0 / D).then_inc(fr, 1)
                ap, fr = drained(phase, "ss_p", layer)
                nc.scalar.activation(rstd[:, NS:NT], ap[:, 0:NP], ACT.Sqrt, bias=epsc[:, 0:1], scale=1.0 / D
                                     ).then_inc(fr, 1)
                act.drain().then_inc(rms_ready.sem, 1)

            def shift(layer, k0, mod_at):
                for k in range(KC):
                    act.wait_ge(hnorm.sem, hnorm.at(layer, k0 + k + 1))
                    nc.scalar.activation(hv[:, k, 0:NS], hv[:, k, 0:NS], ACT.Identity,
                                         bias=modv[:, mod_at + k, 0:1])
                    nc.scalar.activation(hv[:, k, NS:NT], hv[:, k, NS:NT], ACT.Identity,
                                         bias=modv[:, mod_at + k, 1:2])

            with act.Fori(0, DEPTH) as L:
                act.dma_start(par[:, :], PARAMS[bass.ds(L, 1)].rearrange("a p n -> p (a n)")).then_inc(par_in.sem, 16)
                squares(L, 0)
                rms_root("norm1", L, 1)
                shift(L, 0, 0)
                act.drain().then_inc(h_ready.sem, 1)
                act.wait_ge(pads_zero.sem, pads_zero.at(L, 1))
                with act.Fori(0, N_A // 2) as i:
                    for s in range(2):
                        t0 = i * 4 + 2 * s
                        copy_out("gemmA", (f"s0_{s}", f"s1_{s}", f"p_{s}"), L, i,
                                 [tiles(PA, t0 + t, 2, 514) for t in range(2)], PA[:, bass.ds(t0, 2), 516:644])
                act.drain().then_inc(proj_a.sem, 1)
                ap, fl, fr, n = turn("ba", "ba", L)
                act.wait_ge(fl, n)
                bav = ap[:, 0:80].rearrange("p (c n) -> p c n", c=NCH)
                nc.scalar.activation(beta, bav[:, :, 0:8], ACT.Sigmoid)
                act.drain().then_inc(beta_done.sem, 1)
                act.wait_ge(ab_lin.sem, ab_lin.at(L, 1))
                nc.scalar.activation(tmpd, tmpc, ACT.Abs)
                act.drain()
                nc.scalar.activation(tmpd, tmpd, ACT.Exp, scale=-1.0)
                nc.scalar.activation(expa, pr("a_log"), ACT.Exp)
                act.drain()
                nc.scalar.activation(tmpd, tmpd, ACT.Ln, bias=1.0)
                act.drain().then_inc(sp_ready.sem, 1)
                act.wait_ge(cums.sem, cums.at(L, 1))
                nc.scalar.activation(egc, gcum, ACT.Exp)
                nc.scalar.activation(egl, egl, ACT.Exp)
                nc.scalar.activation(ekd, ekd, ACT.Exp)
                act.drain().then_inc(cumx.sem, 1)

                with act.Fori(0, H) as hd:
                    Q = L * H + hd

                    def f(name):
                        return drained("delta", name, L, hd)

                    for g, first, n in G3:
                        ap, fr = f(["R_f", "R_b", "R_p"][g])
                        for c in range(n):
                            d = g if g < 2 else c
                            ch = c if g < 2 else 4
                            m = nc.scalar.activation(DT[:, first + c, :], ap[:, c * P:(c + 1) * P], ACT.Exp,
                                                     bias=ngc[:, ch, bass.ds(hd + 4 * d, 1)])
                        m.then_inc(fr, 1)
                        act.drain().then_inc(decay.sem, 1)
                    for j in range(3):
                        act.wait_ge(conv_done.sem, conv_done.at(Q, j + 1))
                        nc.scalar.activation(cv[:, j, :], cv[:, j, :], ACT.Silu)
                        act.drain()
                        if j < 2:
                            nc.scalar.activation(sq[:, j, 0:NS], cv[:, j, 0:NS], ACT.Square)
                            nc.scalar.activation(sq[:, j, NS:NT], cv[:, j, NS + 2:CW], ACT.Square)
                            act.drain().then_inc(silu_done.sem, 1)
                        else:
                            act.drain().then_inc(silu_done.sem, 1)
                    zt = PA[:, bass.ds(hd + 12, 1), 0:PADW].rearrange("p a t -> p (a t)")
                    nc.scalar.activation(zt, zt, ACT.Silu)
                    act.drain().then_inc(siluz.sem, 1)
                    for j, name in enumerate(("ssq_q", "ssq_k")):
                        ap, fr = f(name)
                        nc.scalar.activation(sq[:, j, 0:NS], ap, ACT.Sqrt, bias=epsc[:, 1 - j:2 - j],
                                             scale=float(P) if j == 0 else 1.0).then_inc(fr, 1)
                    ap, fr = f("ssq_p")
                    nc.scalar.activation(sq[:, 0, NS:NT], ap[:, 0:P], ACT.Sqrt, bias=epsc[:, 1:2], scale=float(P))
                    nc.scalar.activation(sq[:, 1, NS:NT], ap[:, P:2 * P], ACT.Sqrt, bias=epsc[:, 0:1]).then_inc(fr, 1)
                    act.drain().then_inc(rq_ready.sem, 1)
                    ap, fr = f("tok_k")
                    nc.scalar.activation(ktok[:, 0:4, :], ap.rearrange("p (a b) -> p a b", a=4), ACT.Copy).then_inc(fr, 1)
                    ap, fr = f("tok_v")
                    nc.scalar.activation(vtok[:, 0:4, :], ap.rearrange("p (a b) -> p a b", a=4), ACT.Copy).then_inc(fr, 1)
                    ap, fr = f("tok_p")
                    nc.scalar.activation(ktok[:, 4, :], ap[:, 0:P], ACT.Copy)
                    nc.scalar.activation(vtok[:, 4, :], ap[:, P:2 * P], ACT.Copy).then_inc(fr, 1)
                    act.drain().then_inc(tok_ready.sem, 1)
                    for g, first, n in G3:
                        ap, fr = f(f"X0_{GROUPS[g][0]}")
                        nc.scalar.activation(X_[:, first:first + n, :], ap[:, 0:n * P].rearrange("p (a b) -> p a b", a=n),
                                             ACT.Copy).then_inc(fr, 1)
                        act.drain().then_inc(x0_ready.sem, 1)
                    for lev in range(1, NLEV):
                        for g, first, n in G3:
                            ap, fr = f(f"P{lev}_{GROUPS[g][0]}")
                            nc.scalar.activation(PS[:, first:first + n, :],
                                                 ap[:, 0:n * P].rearrange("p (a b) -> p a b", a=n), ACT.Copy
                                                 ).then_inc(fr, 1)
                            act.drain().then_inc(p_ready.sem, 1)
                    for d in range(2):
                        ap, fr = f(["vn_pf", "vn_pb"][d])
                        nc.scalar.activation(vn[:, 2 + d, :], ap[:, 0:P], ACT.Copy,
                                             scale=beta[:, 4, bass.ds(hd + 4 * d, 1)]).then_inc(fr, 1)
                        act.drain().then_inc(vn_ready.sem, 1)
                    for step in range(4):
                        for d in range(2):
                            c = step if d == 0 else 3 - step
                            ap, fr = f(f"vn{step}_{'fb'[d]}")
                            nc.scalar.activation(vn[:, d, :], ap[:, 0:P], ACT.Copy,
                                                 scale=beta[:, c, bass.ds(hd + 4 * d, 1)]).then_inc(fr, 1)
                            act.drain().then_inc(vn_ready.sem, 1)
                    act.wait_ge(osum.sem, osum.at(Q, 1))
                    for c in range(NCH):
                        nc.scalar.activation(sq[:, 0, c * P:(c + 1) * P], oacc[:, c, :], ACT.Square, accum_out=orn[:, c:c + 1])
                    act.drain()
                    nc.scalar.activation(orn, orn, ACT.Sqrt, bias=epsc[:, 0:1], scale=1.0 / P)
                    act.drain().then_inc(orms.sem, 1)

                act.wait_ge(state_stored.sem, state_stored.at(L, 16))
                with act.Fori(0, N_B // 2) as i:
                    for s in range(2):
                        t0 = i * 4 + 2 * s
                        copy_out("gemmB", (f"s0_{s}", f"s1_{s}", f"p_{s}"), L, i,
                                 [tiles(PBq, t0 + t, 0, NS) for t in range(2)], PBq[:, bass.ds(t0, 2), NS:NT])
                for s in range(2):
                    for name, c, n in ((f"s0_{s}", 0, 2), (f"s1_{s}", 2, 2), (f"p_{s}", 4, 1)):
                        ap, fr = drained("gemmV", name, L)
                        nc.scalar.activation(VB[:, c:c + n, s * 256:(s + 1) * 256],
                                             ap[:, 0:n * 256].rearrange("p (a b) -> p a b", a=n), ACT.Copy
                                             ).then_inc(fr, 1)
                act.wait_ge(lam_dot.sem, lam_dot.at(L, 1))
                nc.scalar.activation(lamc[:, 2:4], lamc[:, 0:2], ACT.Exp)
                act.drain().then_inc(proj_b.sem, 1)

                with act.Fori(0, H) as hd:
                    Q = L * H + hd

                    def f(name):
                        return drained("attn", name, L, hd)

                    def turned(qb):
                        ap, fr = f(f"T4_{qb}")
                        nc.scalar.activation(aT[:, 0:4, qb * P:(qb + 1) * P], ap.rearrange("p (a b) -> p a b", a=4),
                                             ACT.Copy).then_inc(fr, 1)
                        ap, fr = f(f"T1_{qb}")
                        nc.scalar.activation(aT[:, 4, qb * P:(qb + 1) * P], ap[:, 0:P], ACT.Copy).then_inc(fr, 1)
                        act.drain().then_inc(at_copied.sem, 2)

                    for qb in range(5):
                        for m_ in range(2):
                            act.wait_ge(neg_max.sem, neg_max.at(Q, 2 * qb + m_ + 1))
                            if qb < 4:
                                pair = (pair0, pair1)[m_]
                                ba, _ = TURNS.at("attn", f"S{m_}_{qb}a", L, hd)
                                bb, _ = TURNS.at("attn", f"S{m_}_{qb}b", L, hd)
                                nc.scalar.activation(pp[:, qb % 2, m_, :], pair[:, 0:NT], ACT.Exp,
                                                     bias=mx[:, qb % 2, m_:m_ + 1], scale=0.125,
                                                     accum_out=rsum[:, qb % 2, m_:m_ + 1]).then_inc(freed[ba], 1)
                                act.drain().then_inc(freed[bb], 1)
                            else:
                                ap, fr = f(f"S_p{m_}")
                                nc.scalar.activation(pp[:, 0, m_, 0:P], ap[:, 0:P], ACT.Exp,
                                                     bias=mx[:, 0, m_:m_ + 1], scale=0.125,
                                                     accum_out=rsum[:, 0, m_:m_ + 1]).then_inc(fr, 1)
                            act.drain().then_inc(exp_done.sem, 1)
                        if 1 <= qb <= 4:
                            turned(qb - 1)
                    ap, fr = f("T_p")
                    nc.scalar.activation(aTp, ap[:, 0:P], ACT.Copy)
                    nc.scalar.activation(knew[:, bass.ds(hd, 1), :].rearrange("p a t -> p (a t)"), ap[:, P:2 * P],
                                         ACT.Copy).then_inc(fr, 1)
                    act.drain().then_inc(at_copied.sem, 1)
                    ap, fr = f("o_s")
                    nc.scalar.activation(osb[:, 0:NS], ap, ACT.Copy).then_inc(fr, 1)
                    ap, fr = f("o_p")
                    nc.scalar.activation(osb[:, NS:NT], ap[:, 0:P], ACT.Copy).then_inc(fr, 1)
                    act.drain()
                    nc.scalar.activation(osq, osb, ACT.Square)
                    act.drain().then_inc(osq_done.sem, 1)
                    ap, fr = f("oss_s")
                    nc.scalar.activation(osq[:, 0:NS], ap, ACT.Sqrt, bias=epsc[:, 0:1], scale=1.0 / P).then_inc(fr, 1)
                    ap, fr = f("oss_p")
                    nc.scalar.activation(osq[:, NS:NT], ap[:, 0:P], ACT.Sqrt, bias=epsc[:, 0:1], scale=1.0 / P
                                         ).then_inc(fr, 1)
                    act.drain().then_inc(orms_b.sem, 1)

                act.drain()
                act.dma_start(KNEW[bass.ds(L, 1)].rearrange("a p n -> p (a n)"), big[:, 6528:6528 + H * P]
                              ).then_inc(cache_stored.sem, 16)
                act.dma_start(VNEW[bass.ds(L, 1)].rearrange("a p n -> p (a n)"), VB[:, 4, :]
                              ).then_inc(cache_stored.sem, 16)
                act.wait_ge(attn_done.sem, attn_done.at(L, 0) * H + H)
                act.wait_ge(cache_stored.sem, cache_stored.at(L, 32))
                act.dma_start(hyc, HYCS).then_inc(hyc_in.sem, 16)
                act.dma_start(fwd, FWD).then_inc(fwd_in.sem, 16)
                act.wait_ge(pads_zero.sem, pads_zero.at(L, 2))
                with act.Fori(0, N_C // 2) as i:
                    for s in range(2):
                        t0 = i * 4 + 2 * s
                        copy_out("gemmC", (f"s0_{s}", f"s1_{s}", f"p_{s}"), L, i,
                                 [tiles(PA, t0 + t, 2, 514) for t in range(2)], PA[:, bass.ds(t0, 2), 516:644])
                act.drain().then_inc(proj_c.sem, 1)
                for j in range(2):
                    act.wait_ge(arg_ready.sem, arg_ready.at(L, j + 1))
                    nc.scalar.activation(hdn[0:64, :], arg[0:64, :], ACT.Sin)
                    act.drain().then_inc(sin_done.sem, 1)
                da, db = HYC["deltas"]
                na, _ = HYC["ndist"]
                for c in range(NCH):
                    if c:
                        act.wait_ge(filt_ready.sem, filt_ready.at(L, c))
                    nc.scalar.activation(dec, hyc[:, da:db], ACT.Exp, scale=hyc[:, na + c:na + c + 1])
                    act.drain().then_inc(dec_ready.sem, 1)
                for c in range(NCH):
                    act.wait_ge(filt_ready.sem, filt_ready.at(L, c + 1))
                    nc.scalar.activation(ABSH[c], tok[:, c, :], ACT.Abs)
                    act.drain().then_inc(abs_ready.sem, 1)
                ap, fl, fr, n = turn("hyfil", "norm", L)
                act.wait_ge(fl, n)
                for i in range(8):
                    ap, fr = drained("hyfil", f"H{i}", L)
                    rows = P if i < 6 else FQ_P
                    nc.scalar.activation(Hs[0:rows, i, :], ap[0:rows, :], ACT.Copy).then_inc(fr, 1)
                    act.drain().then_inc(spec_ready.sem, 1)
                with act.Fori(0, 4) as j:
                    ap, fr = drained("hytr", "g_s", L, j)
                    nc.scalar.activation(tok[:, 0:4, bass.ds(j * P, P)], ap.rearrange("p (a b) -> p a b", a=4), ACT.Copy
                                         ).then_inc(fr, 1)
                    ap, fr = drained("hytr", "g_p", L, j)
                    nc.scalar.activation(tok[:, 4, bass.ds(j * P, P)], ap[:, 0:P], ACT.Copy).then_inc(fr, 1)
                    act.drain().then_inc(gvtok, 1)
                act.wait_ge(gv_ready.sem, gv_ready.at(L * 4 + 3, 1))
                act.dma_start(inv, INV).then_inc(inv_in.sem, 16)

                with act.Fori(0, 3) as b:
                    for half in range(2):
                        B = (L * 3 + b) * 2 + half
                        for s in range(2):
                            for t in range(2):
                                ap, fr = drained("mix", f"s{t}_g{s}_{half}", L, b)
                                if s == 0 and t == 0:
                                    act.wait_ge(merge, B * 2 + 2)
                                nc.scalar.activation(sig[:, 2 * s + t, 0:NS], ap, ACT.Sigmoid).then_inc(fr, 1)
                            ap, fr = drained("mix", f"p_g{s}_{half}", L, b)
                            nc.scalar.activation(sig[:, 2 * s:2 * s + 2, NS:NT],
                                                 ap[:, 0:2 * P].rearrange("p (a b) -> p a b", a=2), ACT.Sigmoid
                                                 ).then_inc(fr, 1)
                        act.drain().then_inc(gates, 1)
                act.wait_ge(xres1.sem, xres1.at(L, 1))
                squares(L, KC)
                rms_root("norm2", L, 2)
                shift(L, KC, 24)
                act.drain().then_inc(h_ready.sem, 1)
                with act.Fori(0, N_F1 // 2) as i:
                    I = L * (N_F1 // 2) + i
                    for t in range(2):
                        ap, fr = drained("ffn1", f"s{t}_0", L, i)
                        if t == 0:
                            act.wait_ge(act_ready, I + 1)
                        nc.scalar.activation(gsil[:, t, 0:NS], ap, ACT.Silu).then_inc(fr, 1)
                    ap, fr = drained("ffn1", "p_0", L, i)
                    nc.scalar.activation(gsil[:, 0:2, NS:NT], ap[:, 0:2 * P].rearrange("p (a b) -> p a b", a=2), ACT.Silu
                                         ).then_inc(fr, 1)
                    act.drain().then_inc(gate_silu, 1)
                act.wait_ge(layer_done.sem, layer_done.at(L, 1))
            squares(DEPTH, 0)
            rms_root("norm1", DEPTH, 1)

        @block.vector
        def _(dve):
            def drained(phase, name, layer, step=0):
                ap, fl, fr, n = turn(phase, name, layer, step)
                dve.wait_ge(fl, n)
                return ap, fr

            tt, ts, stt = nc.vector.tensor_tensor, nc.vector.tensor_scalar, nc.vector.scalar_tensor_tensor

            def inverse_rms(k, value):
                dve.wait_ge(rms_ready.sem, value)
                nc.vector.reciprocal(rstd, rstd)
                dve.drain()

            dve.memset(epsc[:, 0:1], EPS)
            dve.memset(epsc[:, 1:2], P * EPS)
            for b in BANKS:
                dve.sem_inc(freed[b], 1)
            dve.sem_inc(merge, 2)
            dve.sem_inc(act_ready, 1)
            dve.sem_inc(gvtok, 1)
            dve.sem_inc(attn_room, 1)
            dve.drain()
            dve.wait_ge(consts_in, 32)
            with dve.Fori(0, DEPTH) as L:
                for v in pads:
                    dve.memset(v, 0.0)
                dve.drain().then_inc(pads_zero.sem, 1)
                dve.wait_ge(par_in.sem, par_in.at(L, 16))
                dve.sem_inc(passed, 1)
                with dve.Fori(0, N_MOD // 2) as i:
                    for s in range(2):
                        ap, fr = drained("mod", f"mod{s}", L, i)
                        bm = pr("b_mod")[:, bass.ds(i * 4 + 2 * s, 2)].unsqueeze(2).to_broadcast([P, 2, 2])
                        tt(modv[:, bass.ds(i * 4 + 2 * s, 2), :], ap[:, 0:4].rearrange("p (a b) -> p a b", a=2), bm, ALU.add
                           ).then_inc(fr, 1)
                dve.drain()
                for i, (at, g) in enumerate(((8, "g1"), (32, "g2"))):
                    stt(gainv[:, i, :, :], modv[:, at:at + KC, :], 1.0,
                        pr(g).unsqueeze(2).to_broadcast([P, KC, 2]), ALU.add, ALU.mult)
                dve.drain()

                def scale(i, layer, value):
                    inverse_rms(i, value)
                    for k in range(KC):
                        for q, (a, b) in enumerate(((0, NS), (NS, NT))):
                            stt(hv[:, k, a:b], xv[:, k, a:b], gainv[:, i, k, q:q + 1], rstd[:, a:b], ALU.mult, ALU.mult)
                        dve.drain().then_inc(hnorm.sem, 1)

                scale(0, L, rms_ready.at(L, 1))

                lv = pr("lam").rearrange("p (i n) -> p i n", i=4)
                for i in range(2):
                    tt(cut(sc, 4480 + 64 * i, 64), lv[:, 2 * i, :], lv[:, 2 * i + 1, :], ALU.mult)
                dve.drain()
                nc.vector.tensor_reduce(lamc[:, 0:2], cut(sc, 4480, 2, 64), AX_X, ALU.add)
                ts(subg, pr("sub_g"), pr("one_minus_lam"), None, ALU.mult)
                dve.drain().then_inc(lam_dot.sem, 1)

                ap, fl, fr, n = turn("ba", "ba", L)
                dve.wait_ge(proj_a.sem, proj_a.at(L, 1))
                dve.wait_ge(fl, n)
                dve.wait_ge(beta_done.sem, beta_done.at(L, 1))
                bav = ap[:, 0:80].rearrange("p (c n) -> p c n", c=NCH)
                tt(tmpc, bav[:, :, 8:16], pr("dt_bias").unsqueeze(1).to_broadcast([P, NCH, 8]), ALU.add)
                dve.drain().then_inc(ab_lin.sem, 1)
                dve.wait_ge(sp_ready.sem, sp_ready.at(L, 1))
                ts(gg, tmpc, 0.0, None, ALU.max).then_inc(fr, 1)
                dve.drain()
                tt(gg, gg, tmpd, ALU.add)
                dve.drain()
                stt(gg, gg, -1.0, expa.unsqueeze(1).to_broadcast([P, NCH, 8]), ALU.mult, ALU.mult)
                dve.drain().then_inc(g_ready.sem, 1)
                ap, fr = drained("ba", "cum", L)
                cumv = ap[:, 0:120].rearrange("p (w c n) -> p w c n", w=3, c=NCH)
                for d in range(2):
                    nc.vector.tensor_copy(gcum[:, :, 4 * d:4 * d + 4], cumv[:, d, :, 4 * d:4 * d + 4])
                nc.vector.tensor_copy(egl, cumv[:, 2, :, :]).then_inc(fr, 1)
                dve.drain()
                ts(ngc, gcum, -1.0, None, ALU.mult)
                tt(ekd, egl, gcum, ALU.subtract)
                dve.drain().then_inc(cums.sem, 1)
                dve.wait_ge(cumx.sem, cumx.at(L, 1))
                ts(negc, egc, -1.0, None, ALU.mult)
                dve.drain()

                with dve.Fori(0, H) as hd:
                    Q = L * H + hd

                    def f(name):
                        return drained("delta", name, L, hd)

                    cw = pr("conv").rearrange("p (i d) -> p i d", d=5)
                    for j in range(3):
                        src = PA[:, bass.ds(hd + 4 * j, 1), 0:PADW].rearrange("p a t -> p (a t)")

                        def w(d):
                            return cw[:, bass.ds(hd + 4 * j, 1), d]
                        ts(cv[:, j, :], src[:, 0:CW], w(0), None, ALU.mult)
                        dve.drain()
                        for d in range(1, 5):
                            stt(cv[:, j, :], src[:, d:d + CW], w(d), cv[:, j, :], ALU.mult, ALU.add)
                            dve.drain().then_inc(conv_done.sem, 1) if d == 4 else dve.drain()
                    dve.wait_ge(rq_ready.sem, rq_ready.at(Q, 1))
                    nc.vector.reciprocal(sq, sq)
                    dve.drain()
                    for j in range(2):
                        tt(cv[:, j, 0:NS], cv[:, j, 0:NS], sq[:, j, 0:NS], ALU.mult)
                        tt(cv[:, j, NS + 2:CW], cv[:, j, NS + 2:CW], sq[:, j, NS:NT], ALU.mult)
                    dve.drain().then_inc(qk_ready.sem, 1)
                    kk, frk = f("KK_s")
                    qq, frq = f("QK_s")
                    kp, frp = f("KQ_p")

                    def interaction(g, first, n):
                        dve.wait_ge(decay.sem, decay.at(Q, g + 1))
                        for c in range(n):
                            src = kk[:, c * P:(c + 1) * P] if g < 2 else kp[:, 0:P]
                            d = g if g < 2 else c
                            ch = c if g < 2 else 4
                            stt(AT[:, first + c, :], src, beta[:, ch, bass.ds(hd + 4 * d, 1)], DT[:, first + c, :],
                                ALU.mult, ALU.mult)
                        dve.drain().then_inc(at_ready.sem, 1)
                        for c in range(n) if g == 2 else range(1):
                            a, b = (first + c, first + c + 1) if g == 2 else (first, first + n)
                            src = (kp[:, P:2 * P].rearrange("p (a b) -> p a b", a=1) if g == 2
                                   else qq.rearrange("p (a b) -> p a b", a=4))
                            m = tt(DT[:, a:b, :], src, DT[:, a:b, :], ALU.mult)
                        return m

                    interaction(0, 0, 4)
                    interaction(1, 4, 4)
                    dve.drain().then_inc(frk, 1)
                    dve.drain().then_inc(frq, 1)
                    interaction(2, 8, 2).then_inc(frp, 1)
                    dve.drain().then_inc(qkd_ready.sem, 1)
                    for g, first, n in G3:
                        dve.wait_ge(al_ready.sem, al_ready.at(Q, g + 1))
                        stt(XT[:, first:first + n, :], AL[:, first:first + n, :], -1.0, repeated(ident, n), ALU.mult, ALU.add)
                        dve.drain().then_inc(xt_ready.sem, 1)
                    for lev in range(1, NLEV):
                        for g, first, n in G3:
                            m3 = slice(first, first + n)
                            if lev < NLEV - 1:
                                ap, fr = f(f"D{lev}_{GROUPS[g][0]}")
                                if lev == 1:
                                    dve.wait_ge(x0_ready.sem, x0_ready.at(Q, g + 1))
                                tt(X_[:, m3, :], X_[:, m3, :], ap[:, 0:n * P].rearrange("p (a b) -> p a b", a=n),
                                   ALU.subtract).then_inc(fr, 1)
                                dve.drain().then_inc(x_ready.sem, 1)
                            ap, fr = f(f"E{lev}_{GROUPS[g][0]}")
                            tt(XT[:, m3, :], XT[:, m3, :], ap[:, 0:n * P].rearrange("p (a b) -> p a b", a=n),
                               ALU.subtract).then_inc(fr, 1)
                            dve.drain().then_inc(xt_ready.sem, 1)
                    sv = pr("state").rearrange("p (i n) -> p i n", i=8)
                    for d in range(2):
                        nc.vector.tensor_copy(S[:, d, :], sv[:, bass.ds(hd + 4 * d, 1), :].rearrange("p a n -> p (a n)"))
                    dve.drain().then_inc(s_ready.sem, 1)
                    dve.wait_ge(tok_ready.sem, tok_ready.at(Q, 1))
                    ap, fr = f("o_p")
                    nc.vector.tensor_copy(oacc[:, 4, :], ap[:, 0:P])
                    for d in range(2):
                        m = nc.vector.tensor_copy(snew[:, bass.ds(hd + 4 * d, 1), :].rearrange("p a n -> p (a n)"),
                                                  ap[:, (1 + d) * P:(2 + d) * P])
                    m.then_inc(fr, 1)
                    for step in range(4):
                        for d in range(2):
                            c = step if d == 0 else 3 - step
                            cd = bass.ds(hd + 4 * d, 1)
                            ap, fr = f(f"kq{step}_{'fb'[d]}")
                            stt(rr[:, d, :], ap[:, 0:P], negc[:, c, cd], vtok[:, c, :], ALU.mult, ALU.add)
                            dve.drain().then_inc(r_ready.sem, 1)
                            if step < 2:
                                ts(t1[:, d, :], ap[:, P:2 * P], egc[:, c, cd], None, ALU.mult).then_inc(fr, 1)
                            else:
                                stt(t1[:, d, :], ap[:, P:2 * P], egc[:, c, cd], oacc[:, c, :], ALU.mult, ALU.add
                                    ).then_inc(fr, 1)
                        dve.drain()
                        for d in range(2):
                            c = step if d == 0 else 3 - step
                            cd = bass.ds(hd + 4 * d, 1)
                            ap, fr = f(f"o{step}_{'fb'[d]}")
                            if step < 3:
                                stt(S[:, d, :], S[:, d, :], egl[:, c, cd], ap[:, P:2 * P], ALU.mult, ALU.add)
                                dve.drain().then_inc(s_ready.sem, 1)
                            tt(oacc[:, c, :], t1[:, d, :], ap[:, 0:P], ALU.add).then_inc(fr, 1)
                        dve.drain()
                    dve.drain().then_inc(osum.sem, 1)
                    dve.wait_ge(orms.sem, orms.at(Q, 1))
                    nc.vector.reciprocal(orn, orn)
                    dve.drain()
                    for c in range(NCH):
                        ts(oacc[:, c, :], oacc[:, c, :], orn[:, c:c + 1], None, ALU.mult)
                    dve.drain().then_inc(oscaled.sem, 1)
                    dve.wait_ge(siluz.sem, siluz.at(Q, 1))
                    zt = PA[:, bass.ds(hd + 12, 1), 0:PADW].rearrange("p a t -> p (a t)")
                    ot = ov[:, bass.ds(hd, 1), :].rearrange("p a t -> p (a t)")
                    ap, fr = f("oT_s")
                    stt(ot[:, 0:NS], ap, pr("dn_g"), zt[:, 2:514], ALU.mult, ALU.mult).then_inc(fr, 1)
                    ap, fr = f("oT_p")
                    stt(ot[:, NS:NT], ap[:, 0:P], pr("dn_g"), zt[:, 516:644], ALU.mult, ALU.mult).then_inc(fr, 1)
                    dve.drain().then_inc(head_done.sem, 1)

                dve.wait_ge(proj_b.sem, proj_b.at(L, 1))
                tt(lamc[:, 4:5], lamc[:, 3:4], lamc[:, 2:3], ALU.subtract)
                dve.drain()
                tt(lamc[:, 5:6], lamc[:, 4:5], pr("lam_init"), ALU.subtract)
                dve.drain()

                with dve.Fori(0, H) as hd:
                    Q = L * H + hd

                    def f(name):
                        return drained("attn", name, L, hd)

                    dve.wait_ge(rope_in.sem, rope_in.at(L, 16))
                    ca, cb = ROPE["cos"]
                    sa, sb_ = ROPE["sin"]
                    for j, (name, dst) in enumerate((("rot_q", qall), ("rot_k", kall))):
                        src = PBq[:, bass.ds(hd + 4 * j, 1), 0:NS].rearrange("p a t -> p (a t)")
                        tt(dst[:, 0:NS], src, rope[:, ca:cb], ALU.mult)
                        ap, fr = f(name)
                        tt(rtmp, ap, rope[:, sa:sb_], ALU.mult).then_inc(fr, 1)
                        dve.drain()
                        tt(dst[:, 0:NS], dst[:, 0:NS], rtmp, ALU.add)
                        dve.drain().then_inc(rot_done.sem, 1)

                    def maxima(qb):
                        for m_ in range(2):
                            if qb < 4:
                                for part in "ab":
                                    b, n = TURNS.at("attn", f"S{m_}_{qb}{part}", L, hd)
                                    dve.wait_ge(filled[b], n)
                                src = (pair0, pair1)[m_][:, 0:NT]
                            else:
                                b, n = TURNS.at("attn", f"S_p{m_}", L, hd)
                                dve.wait_ge(filled[b], n)
                                src = bank[b][:, 0:P]
                            q = qb % 2
                            nc.vector.reduce_max(mx[:, q, m_:m_ + 1], src, AX_X)
                            dve.drain()
                            ts(mx[:, q, m_:m_ + 1], mx[:, q, m_:m_ + 1], -0.125, None, ALU.mult)
                            dve.drain().then_inc(neg_max.sem, 1)

                    def combine(qb):
                        q = qb % 2
                        w_ = NT if qb < 4 else P
                        dve.wait_ge(exp_done.sem, exp_done.at(Q, 2 * qb + 2))
                        if qb >= 2:
                            dve.wait_ge(at_copied.sem, at_copied.at(Q, 2 * (qb - 2) + 2))
                        nc.vector.reciprocal(rinv[:, q, :], rsum[:, q, :])
                        dve.drain()
                        ts(rinv[:, q, 1:2], rinv[:, q, 1:2], lamc[:, 5:6], None, ALU.mult)
                        ts(aa[:, q, 0:w_], pp[:, q, 0, 0:w_], rinv[:, q, 0:1], None, ALU.mult)
                        dve.drain()
                        stt(aa[:, q, 0:w_], pp[:, q, 1, 0:w_], rinv[:, q, 1:2], aa[:, q, 0:w_], ALU.mult, ALU.add)
                        dve.drain().then_inc(a_ready.sem, 1)

                    maxima(0)
                    for qb in range(1, 5):
                        maxima(qb)
                        combine(qb - 1)
                    combine(4)
                    dve.wait_ge(orms_b.sem, orms_b.at(Q, 1))
                    nc.vector.reciprocal(osq, osq)
                    dve.drain()
                    stt(ov[:, bass.ds(hd + 4, 1), :].rearrange("p a t -> p (a t)"), osb, subg, osq, ALU.mult, ALU.mult)
                    dve.drain().then_inc(attn_done.sem, 1)
                    dve.drain().then_inc(attn_room, 1)

                dve.wait_ge(cache_stored.sem, cache_stored.at(L, 32))
                for v in pads:
                    dve.memset(v[:, 0:12, :], 0.0)
                dve.drain().then_inc(pads_zero.sem, 1)
                for j, (ns_, np_, b_) in enumerate((("h1_s", "h1_p", "hy_b1"), ("h2_s", "h2_p", "hy_b2"))):
                    ap, fr = drained("hyfil", ns_, L)
                    ts(arg[0:64, 0:NS], ap[0:64, :], pr(b_, 64), pr("hy_fr", 64), ALU.add, ALU.mult).then_inc(fr, 1)
                    ap, fr = drained("hyfil", np_, L)
                    ts(arg[0:64, NS:NT], ap[0:64, 0:NP], pr(b_, 64), pr("hy_fr", 64), ALU.add, ALU.mult).then_inc(fr, 1)
                    dve.drain()
                    ts(redu[0:64, :], arg[0:64, :], 1.0 / TWO_PI, ROUND, ALU.mult, ALU.add)
                    dve.drain()
                    ts(redu[0:64, :], redu[0:64, :], -ROUND, None, ALU.add)
                    dve.drain()
                    for part in TWO_PI_PARTS:
                        stt(arg[0:64, :], redu[0:64, :], -part, arg[0:64, :], ALU.mult, ALU.add)
                        dve.drain()
                    ts(arg[0:64, :], arg[0:64, :], PI_BELOW, -PI_BELOW, ALU.min, ALU.max)
                    dve.drain().then_inc(arg_ready.sem, 1)
                for c in range(NCH):
                    ap, fr = drained("hyfil", f"h3_{c}", L)
                    dve.wait_ge(dec_ready.sem, dec_ready.at(L, c + 1))
                    tt(tok[:, c, :], ap, dec, ALU.mult).then_inc(fr, 1)
                    dve.drain().then_inc(filt_ready.sem, 1)
                ap, fr = drained("hyfil", "norm", L)
                nc.vector.reciprocal(hyn, ap[:, 0:8].rearrange("p (a b) -> p a b", a=2)).then_inc(fr, 1)
                dve.drain()
                for q, length in ((0, L_S), (1, L_P)):
                    ts(hyn[:, q, :], hyn[:, q, :], 2.0 / length, None, ALU.mult)
                dve.drain()
                dve.wait_ge(proj_c.sem, proj_c.at(L, 1))
                dve.sem_inc(passed, 1)
                hw = pr("hconv").rearrange("p (i d) -> p i d", d=3)
                with dve.Fori(0, 4) as j:
                    for part, dst in ((0, None), (1, hx1), (2, hv_)):
                        src = PA[:, bass.ds(j + 4 * part, 1), 0:PADW].rearrange("p a t -> p (a t)")
                        tile_w = [hw[:, bass.ds(j + 4 * part, 1), d] for d in range(3)]
                        bias = pr("hconv_b")[:, bass.ds(j + 4 * part, 1)]
                        to = hx1 if part == 0 else dst
                        ts(to, src[:, 1:1 + CW], tile_w[0], bias, ALU.mult, ALU.add)
                        dve.drain()
                        stt(to, src[:, 2:2 + CW], tile_w[1], to, ALU.mult, ALU.add)
                        dve.drain()
                        stt(to, src[:, 3:3 + CW], tile_w[2], to, ALU.mult, ALU.add)
                        dve.drain()
                        if part == 0:
                            xo = ov[:, bass.ds(j + 8, 1), :].rearrange("p a t -> p (a t)")
                            nc.vector.tensor_copy(xo[:, 0:NS], to[:, 0:NS])
                            nc.vector.tensor_copy(xo[:, NS:NT], to[:, NS + 2:CW])
                            dve.drain()
                    g_ = PA[:, bass.ds(j, 1), 0:NT].rearrange("p a t -> p (a t)")
                    dve.wait_ge(spec_ready.sem, spec_ready.at(L, 8))
                    with ExitStack():
                        tt(g_[:, 0:NS], hx1[:, 0:NS], hv_[:, 0:NS], ALU.mult)
                        tt(g_[:, NS:NT], hx1[:, NS + 2:CW], hv_[:, NS + 2:CW], ALU.mult)
                        dve.drain()
                        dve.wait_ge(gvtok, L * 4 + j + 1)
                        dve.sem_inc(passed, 1)
                        nc.vector.tensor_copy(ytmp, g_)
                    dve.drain().then_inc(gv_ready.sem, 1)
                for i in range(4):
                    rows = P if i < 3 else FQ_P
                    ic, is_ = (i, 3 + i) if i < 3 else (6, 7)
                    xc, frc = drained("hydft", f"X{ic}", L)
                    xs, frs = drained("hydft", f"X{is_}", L)
                    hc, hs = Hs[0:rows, ic, :], Hs[0:rows, is_, :]
                    yc, ys = (Ys[:, i, :], Ys[:, 3 + i, :]) if i < 3 else (Yp[0:rows, 0, :], Yp[0:rows, 1, :])
                    u = cut(big, 11 * PADW, 512)[0:rows, :]
                    u2 = cut(big, 11 * PADW + 512, 512)[0:rows, :]
                    tt(yc, xc[0:rows, :], hc, ALU.mult)
                    tt(u, xs[0:rows, :], hs, ALU.mult)
                    tt(ys, xc[0:rows, :], hs, ALU.mult).then_inc(frc, 1)
                    tt(u2, xs[0:rows, :], hc, ALU.mult).then_inc(frs, 1)
                    dve.drain()
                    tt(yc, yc, u, ALU.subtract)
                    tt(ys, ys, u2, ALU.add)
                    dve.drain().then_inc(xprod.sem, 1)
                for j in range(4):
                    ts(PA[:, j, 0:NT], PA[:, j, 0:NT], pr("hy_d")[:, j:j + 1], None, ALU.mult)
                dve.drain()
                for j in range(4):
                    ap, fr = drained("hydft", f"y_s{j}", L)
                    g_ = PA[:, j, 0:NS]
                    stt(g_, ap, hyn[:, 0, j:j + 1], g_, ALU.mult, ALU.add).then_inc(fr, 1)
                ap, fr = drained("hydft", "y_p", L)
                for j in range(4):
                    g_ = PA[:, j, NS:NT]
                    m = stt(g_, ap[:, j * P:(j + 1) * P], hyn[:, 1, j:j + 1], g_, ALU.mult, ALU.add)
                m.then_inc(fr, 1)
                dve.drain()
                for j in range(4):
                    tt(ov[:, 8 + j, :], ov[:, 8 + j, :], PA[:, j, 0:NT], ALU.mult)
                dve.memset(merged, 0.0)
                dve.drain().then_inc(hy_done.sem, 1)

                with dve.Fori(0, 3) as b:
                    for half in range(2):
                        B = (L * 3 + b) * 2 + half
                        dve.wait_ge(gates, B + 1)
                        for s in range(2):
                            t0 = 4 * half + 2 * s
                            for t in range(2):
                                ap, fr = drained("mix", f"s{t}_b{s}_{half}", L, b)
                                tt(mtmp[:, t, 0:NS], ap, sig[:, 2 * s + t, 0:NS], ALU.mult).then_inc(fr, 1)
                            ap, fr = drained("mix", f"p_b{s}_{half}", L, b)
                            tt(mtmp[:, :, NS:NT], ap[:, 0:2 * P].rearrange("p (a b) -> p a b", a=2),
                               sig[:, 2 * s:2 * s + 2, NS:NT], ALU.mult).then_inc(fr, 1)
                            dve.drain()
                            tt(merged[:, t0:t0 + 2, :], merged[:, t0:t0 + 2, :], mtmp, ALU.add)
                            dve.drain().then_inc(merge, 1)
                dve.drain().then_inc(merged_ready.sem, 1)

                def residual(phase, step, t0, names, mod_at):
                    for t in range(2):
                        ap, fr = drained(phase, names[t], L, step)
                        xt = xv[:, bass.ds(t0 + t, 1), 0:NS].rearrange("p a t -> p (a t)")
                        gc = modv[:, bass.ds(t0 + (mod_at + t), 1), 0]
                        stt(xt, ap, gc, xt, ALU.mult, ALU.add).then_inc(fr, 1)
                    ap, fr = drained(phase, names[2], L, step)
                    for t in range(2):
                        xt = xv[:, bass.ds(t0 + t, 1), NS:NT].rearrange("p a t -> p (a t)")
                        gc = modv[:, bass.ds(t0 + (mod_at + t), 1), 1]
                        m = stt(xt, ap[:, t * P:(t + 1) * P], gc, xt, ALU.mult, ALU.add)
                    m.then_inc(fr, 1)

                with dve.Fori(0, N_OUT // 2) as i:
                    for s in range(2):
                        residual("out", i, i * 4 + 2 * s, (f"s0_{s}", f"s1_{s}", f"p_{s}"), 16)
                dve.drain().then_inc(xres1.sem, 1)
                scale(1, L, rms_ready.at(L, 2))
                with dve.Fori(0, N_F1 // 2) as i:
                    I = L * (N_F1 // 2) + i
                    dve.wait_ge(gate_silu, I + 1)
                    for t in range(2):
                        ap, fr = drained("ffn1", f"s{t}_1", L, i)
                        to = actv[:, bass.ds(i * 2 + t, 1), 0:NS].rearrange("p a t -> p (a t)")
                        tt(to, ap, gsil[:, t, 0:NS], ALU.mult).then_inc(fr, 1)
                    ap, fr = drained("ffn1", "p_1", L, i)
                    tt(actv[:, bass.ds(i * 2, 2), NS:NT], ap[:, 0:2 * P].rearrange("p (a b) -> p a b", a=2),
                       gsil[:, 0:2, NS:NT], ALU.mult).then_inc(fr, 1)
                    dve.drain().then_inc(act_ready, 1)
                with dve.Fori(0, 2) as i:
                    for s in range(2):
                        residual("ffn2", i, i * 4 + 2 * s, (f"s0_{s}", f"s1_{s}", f"p_{s}"), 40)
                dve.drain().then_inc(layer_done.sem, 1)
            inverse_rms(0, rms_ready.at(DEPTH, 1))
            for q, (a, b) in enumerate(((0, NS), (NS, NT))):
                for k in range(KC):
                    stt(hv[:, k, a:b], xv[:, k, a:b], cn("final_g")[:, k:k + 1], rstd[:, a:b], ALU.mult, ALU.mult)
                dve.drain().then_inc(y_ready, 1)

        @block.gpsimd
        def _(pool):
            with pool.Fori(0, DEPTH) as L:
                pool.wait_ge(g_ready.sem, g_ready.at(L, 1))
                pool.wait_ge(cumx.sem, cumx.at(L, 1))
                pool.sem_inc(passed, 1)
                with pool.Fori(0, H) as hd:
                    Q = L * H + hd
                    def head_columns(src):
                        return src.rearrange("p c (d h) -> p c d h", d=2)[:, :, :, bass.ds(hd, 1)].rearrange(
                            "p c d a -> p c (d a)")
                    nc.gpsimd.tensor_copy(gh, head_columns(gg))
                    nc.gpsimd.tensor_copy(eh, head_columns(ekd))
                    pool.drain()
                    for g, first, n in G3:
                        for c in range(n):
                            d = g if g < 2 else c
                            ch = c if g < 2 else 4
                            nc.gpsimd.tensor_scalar(GU[:, first + c, :], tri[:, d, :], gh[:, ch, d:d + 1],
                                                    None, ALU.mult)
                    pool.drain().then_inc(gu_ready.sem, 1)

                    def level(lev):
                        for g, first, n in G3:
                            if lev == 0:
                                pool.wait_ge(at_ready.sem, at_ready.at(Q, g + 1))
                            elif lev == 1:
                                pool.wait_ge(xt_ready.sem, xt_ready.at(Q, g + 1))
                            else:
                                pool.wait_ge(p_ready.sem, p_ready.at(Q, 3 * (lev - 2) + g + 1))
                            m3 = slice(first, first + n)
                            mask = levels[:, lev, :, :] if g == 2 else repeated(levels[:, lev, g, :], n)
                            nc.gpsimd.tensor_tensor(AL[:, m3, :], AT[:, m3, :], mask, ALU.mult)
                            pool.drain().then_inc(al_ready.sem, 1)

                    level(0)
                    level(1)
                    pool.wait_ge(tok_ready.sem, tok_ready.at(Q, 1))
                    pool.sem_inc(passed, 1)
                    for g, first, n in G3:
                        for c in range(n):
                            d = g if g < 2 else c
                            ch = c if g < 2 else 4
                            nc.gpsimd.tensor_scalar(kd[:, first + c, :], ktok[:, ch, :], eh[:, ch, d:d + 1],
                                                    None, ALU.mult)
                    pool.drain().then_inc(kd_ready.sem, 1)
                    for lev in range(2, NLEV):
                        level(lev)
                pool.wait_ge(head_done.sem, head_done.at(L, 0) * H + H)
                pool.dma_start(SNEW[bass.ds(L, 1)].rearrange("a p n -> p (a n)"), big[:, PB0 + 5120:PB0 + 6144]
                               ).then_inc(state_stored.sem, 16)
                pool.dma_start(rope, ROPES).then_inc(rope_in.sem, 16)
                pool.wait_ge(proj_b.sem, proj_b.at(L, 1))
                pool.sem_inc(passed, 1)
                with pool.Fori(0, H) as hd:
                    Q = L * H + hd
                    with ExitStack():
                        src_q = PBq[:, bass.ds(hd, 1), NS:NT].rearrange("p a t -> p (a t)")
                        src_k = PBq[:, bass.ds(hd + 4, 1), NS:NT].rearrange("p a t -> p (a t)")
                        kc = pr("k_ctx").rearrange("p (i n) -> p i n", i=H)[:, bass.ds(hd, 1), :].rearrange("p a t -> p (a t)")
                        vc = pr("v_ctx").rearrange("p (i n) -> p i n", i=H)[:, bass.ds(hd, 1), :].rearrange("p a t -> p (a t)")
                        pool.wait_ge(attn_room, Q + 1)
                        nc.gpsimd.tensor_copy(qall[:, NS:NT], src_q)
                        nc.gpsimd.tensor_copy(kall[:, NT:NT + P], src_k)
                        nc.gpsimd.tensor_copy(kall[:, NS:NT], kc)
                        nc.gpsimd.tensor_copy(vall[:, 0:4, :], VB[:, 0:4, bass.ds(hd * P, P)])
                        nc.gpsimd.tensor_copy(vall[:, 5, :], VB[:, 4, bass.ds(hd * P, P)])
                        nc.gpsimd.tensor_copy(vall[:, 4, :], vc)
                    pool.drain().then_inc(qcopy.sem, 1)


ROUND = 1.5 * 2.0 ** 23
PI_BELOW = float(np.nextafter(np.float32(math.pi), np.float32(0)))


def two_pi_parts():
    a = 6.28125
    b = float(np.float32(round((TWO_PI - a) * 2 ** 21) / 2 ** 21))
    return a, b, float(np.float32(TWO_PI - a - b))


TWO_PI_PARTS = two_pi_parts()


def axial_rope():
    half = 32
    inv = (np.float32(10000.0) ** (-np.arange(0, half, 2, dtype=np.float32) / half)).astype(np.float32)
    t = np.arange(NS)
    pos = {0: (t // GRID_W).astype(np.float32), 1: (t % GRID_W).astype(np.float32)}
    cos, sin = np.zeros((P, NS), np.float32), np.zeros((P, NS), np.float32)
    for c in range(P):
        ang = (pos[(c % 64) // 32] * inv[c % 16]).astype(np.float32)
        cos[c], sin[c] = np.cos(ang), np.sin(ang)
    return np.concatenate([cos, sin], axis=1)


def constants(c, c_ctx, final_g):
    con = np.zeros((P, N_CON), np.float32)
    i = np.arange(P)

    def put(name, a):
        con[:, CON[name][0]:CON[name][1]] = a.reshape(P, -1)
    put("ident", np.eye(P, dtype=np.float32))
    put("ones", np.ones((P, P), np.float32))
    fwd = (i[:, None] <= i[None, :]).astype(np.float32)
    put("tri", np.stack([fwd, fwd.T], 1))
    put("big", np.where(np.stack([fwd, fwd.T], 1) > 0, 0.0, -1e30).astype(np.float32))
    perm = np.zeros((P, P), np.float32)
    for m in range(P):
        perm[m + 16 if m % 32 < 16 else m - 16, m] = -1.0 if m % 32 < 16 else 1.0
    put("perm", perm)
    lev = np.zeros((P, NLEV, 2, P), np.float32)
    for n in range(NLEV):
        same = (i[:, None] >> (n + 1)) == (i[None, :] >> (n + 1))
        f = same & ((i[:, None] >> n) % 2 == 0) & ((i[None, :] >> n) % 2 == 1)
        lev[:, n, 0], lev[:, n, 1] = f, f.T
    put("levels", lev)
    put("final_g", final_g.reshape(KC, P).T)
    put("cond", np.stack([c.reshape(KC, P).T, c_ctx.reshape(KC, P).T], 2))
    return con


def hyena_constants():
    hyc = np.zeros((P, N_HYC), np.float32)
    lo, hi = abs(math.log(1e-2) / 1.5), abs(math.log(1e-2) / 0.3)
    hyc[:, HYC["deltas"][0]:HYC["deltas"][1]] = np.linspace(lo, hi, 512, dtype=np.float32)
    at = 0
    for n in (NS, NP):
        j = np.arange(n, dtype=np.float32)
        t = j / np.float32(n - 1)
        ang = (np.float32(2.0 * math.pi) * j / np.float32(n))[:, None] * np.linspace(1e-4, 7, 8, dtype=np.float32)
        z = np.concatenate([t[:, None], np.cos(ang), -np.sin(ang)], axis=1).astype(np.float32)
        hyc[0:17, HYC["z"][0] + at:HYC["z"][0] + at + n] = z.T
        dist = np.abs(j - n // 2) / np.float32(n // 2)
        a = HYC["ndist"][0] + at // P
        hyc[:, a:a + n // P] = -dist.reshape(n // P, P).T
        at += n
    return hyc


def dft_tables():
    fwd, inv = np.zeros((P, N_FWD), np.float32), np.zeros((P, N_INV), np.float32)
    for n, length, tiles in ((NS, L_S, 3), (NP, L_P, 1)):
        fq = length // 2
        w = 2 * math.pi * (np.arange(fq) + 0.5) / length
        a = np.arange(n)[:, None] * w[None, :]
        both = np.concatenate([np.cos(a), np.sin(a)], 1)
        b = w[:, None] * (np.arange(n) + n // 2)[None, :]
        if n == NS:
            fwd[:, 0:4 * L_S] = both.reshape(4, P, 2 * fq).transpose(1, 0, 2).reshape(P, -1)
            back = np.concatenate([np.cos(b), np.sin(b)], 0)
            inv[:, 0:6 * NS] = back.reshape(6, P, NS).transpose(1, 0, 2).reshape(P, -1)
        else:
            fwd[:, 4 * L_S:] = both
            inv[0:fq, 6 * NS:] = np.concatenate([np.cos(b), np.sin(b)], 1)
    return fwd, inv


def panels(w, width=256):
    k, n = w.shape
    return w.reshape(k // P, P, n // width, width).transpose(2, 1, 0, 3).reshape(n // width, P, -1)


def kernel(x_prompt, x_sample, cache_k, cache_v, state_dn, c, c_ctx, norm1_g, norm2_g, w_mod, b_mod, w_in, dn_conv_w,
           dn_a_log, dn_dt_bias, dn_norm_g, da_lambda, da_subln_g, hy_conv_w, hy_conv_b, hy_w1, hy_b1, hy_freq,
           hy_w2, hy_b2, hy_w3, hy_d, w_br_a, w_br_b, w_br_c, w_out, w_ffn_in, w_ffn_out, final_g):
    import concourse.bacc as _bacc
    from concourse.bass_utils import run_bass_kernel_spmd as _run

    W = np.zeros((DEPTH * PANELS, P, PANEL), np.float32)
    par = np.zeros((DEPTH, P, N_PAR), np.float32)
    for l in range(DEPTH):
        wi = np.asarray(w_in[l])
        cols = lambda a, n: wi[:, a:a + n]
        parts = [panels(np.asarray(w_mod[l])), panels(cols(0, 1536)), panels(cols(1552, 512)), panels(cols(2064, 1024)),
                 panels(cols(3088, 512)), panels(cols(3600, 1536))]
        for b, w_br in enumerate((w_br_a, w_br_b, w_br_c)):
            for half in range(2):
                parts.append(panels(cols(5136 + b * D + half * 512, 512)))
                parts.append(panels(np.asarray(w_br[l])[:, half * 512:(half + 1) * 512], 512))
        parts.append(panels(np.asarray(w_out[l])))
        f1 = np.asarray(w_ffn_in[l])
        for i in range(N_F1 // 2):
            parts.append(panels(f1[:, i * 256:(i + 1) * 256]))
            parts.append(panels(f1[:, D_FF + i * 256:D_FF + (i + 1) * 256]))
        f2 = np.asarray(w_ffn_out[l])
        at = l * PANELS
        for part in parts:
            W[at:at + part.shape[0]] = part
            at += part.shape[0]
        for n in range(D // 256):
            for j in range(3):
                rows = f2[j * KC * P:min((j + 1) * KC * P, D_FF), n * 256:(n + 1) * 256]
                part = panels(rows)
                W[at, :, 0:part.shape[2]] = part[0]
                at += 1

        def put(name, a, rows=P):
            a = np.asarray(a)
            par[l, 0:rows, PAR[name][0]:PAR[name][1]] = a.reshape(rows, -1)

        def column(v):
            v = np.asarray(v)
            return v.reshape(-1, P).T

        def everywhere(v):
            v = np.asarray(v).reshape(1, -1)
            return np.broadcast_to(v, (P, v.shape[1]))
        put("b_mod", column(b_mod[l]))
        put("g1", column(norm1_g[l]))
        put("g2", column(norm2_g[l]))
        put("conv", np.asarray(dn_conv_w[l]).reshape(5, 12, P).transpose(2, 1, 0))
        put("hconv", np.asarray(hy_conv_w[l]).reshape(3, 12, P).transpose(2, 1, 0))
        put("hconv_b", column(hy_conv_b[l]))
        put("a_log", everywhere(dn_a_log[l]))
        put("dt_bias", everywhere(dn_dt_bias[l]))
        put("dn_g", column(dn_norm_g[l]))
        put("sub_g", column(da_subln_g[l]))
        put("lam", everywhere(da_lambda[l]))
        put("w_ba", wi[:, 1536:1552].reshape(KC, P, 16).transpose(1, 0, 2))
        put("hy_w1", hy_w1[l], 17)
        put("hy_b1", hy_b1[l], 64)
        put("hy_fr", hy_freq[l], 64)
        put("hy_b2", hy_b2[l], 64)
        put("hy_w2", hy_w2[l], 64)
        put("hy_w3", hy_w3[l], 64)
        put("hy_d", column(hy_d[l]))
        put("state", np.asarray(state_dn)[0, l].reshape(8, P, P).transpose(1, 0, 2))
        put("k_ctx", np.asarray(cache_k)[0, l].transpose(2, 0, 1))
        put("v_ctx", np.asarray(cache_v)[0, l].transpose(1, 0, 2))
        lam_init = 0.8 - 0.6 * math.exp(-0.3 * l)
        put("lam_init", np.full((P, 1), lam_init, np.float32))
        put("one_minus_lam", np.full((P, 1), 1.0 - lam_init, np.float32))

    x = np.concatenate([np.asarray(x_sample)[0], np.asarray(x_prompt)[0]], 0)
    fwd, inv = dft_tables()
    arrays = {
        "W": W, "PARAMS": par, "CONSTS": constants(np.asarray(c), np.asarray(c_ctx), np.asarray(final_g)),
        "ROPES": axial_rope(), "HYCS": hyena_constants(), "FWD": fwd, "INV": inv,
        "X": np.ascontiguousarray(x.T.reshape(KC, P, NT).transpose(1, 0, 2)),
    }
    nc = _bacc.Bacc("TRN2", target_bir_lowering=False, num_devices=1)
    args = {n: nc.dram_tensor(f"in_{n}", a.shape, F32, kind="ExternalInput").ap() for n, a in arrays.items()}
    shapes = {"Y": (P, KC, NT), "KNEW": (DEPTH, P, H * P), "VNEW": (DEPTH, P, H * P), "SNEW": (DEPTH, P, 8 * P)}
    args.update({n: nc.dram_tensor(f"out_{n}", s, F32, kind="ExternalOutput").ap() for n, s in shapes.items()})
    trunk_program(nc, **args)
    r = _run(nc, [{f"in_{n}": a for n, a in arrays.items()}], core_ids=[0]).results[0]
    y = np.asarray(r["out_Y"]).transpose(1, 0, 2).reshape(D, NT).T
    k_new = np.asarray(r["out_KNEW"]).reshape(DEPTH, P, H, P).transpose(0, 2, 1, 3)
    v_new = np.asarray(r["out_VNEW"]).reshape(DEPTH, P, H, P).transpose(0, 2, 1, 3)
    s_new = np.asarray(r["out_SNEW"]).reshape(DEPTH, P, 2, H, P).transpose(0, 2, 3, 1, 4)
    return (np.ascontiguousarray(y[None, NS:]), np.ascontiguousarray(y[None, :NS]),
            np.ascontiguousarray(k_new[None]), np.ascontiguousarray(v_new[None]), np.ascontiguousarray(s_new[None]))
```

```python
from contextlib import ExitStack
import math

import numpy as np
import concourse.bass as bass
from concourse import mybir
from concourse.alu_op_type import AluOpType as ALU

F32 = mybir.dt.float32
F32R = mybir.dt.float32r
ACT = mybir.ActivationFunctionType
AX_X = mybir.AxisListType.X

P = 128
D = 1024
KC = D // P
DEPTH = 2
NS, NP = 512, 128
NT = NS + NP
NCH = NT // P
H = 4
EPS = 1e-6
D_FF = 2816
FT = D_FF // P
GRID_W = 64
PADW = 648
CW = NS + 2 + NP
NLEV = 7
L_S, L_P = 768, 192
FQ_S, FQ_P = L_S // 2, L_P // 2
TWO_PI = 2.0 * math.pi
RAW = 4
HI = 2
UNIT = 1024


def stream():
    return [("A", 4, "wwww"), ("delta", H, "m" * 8), ("B", 2, "wwww"), ("V", 1, "wwww"), ("attn", H, "mmmm"),
            ("C", 3, "wwww"), ("mix", 3, "w" * 12), ("out", 2, "wwww"),
            ("f1_0", 4, "wwww"), ("f2_0", 2, "wwww"), ("f1_1", 4, "wwww"), ("f2_1", 2, "wwww"),
            ("f1_2", 3, "wwww"), ("f2_2", 2, "wwww")]


FIRST_MOD = 16
PHASE_AT, UNITS, SPLITS = {}, 0, 0
for _name, _times, _kinds in stream():
    PHASE_AT[_name] = (UNITS, SPLITS, _kinds)
    UNITS += _times * len(_kinds)
    SPLITS += _times * _kinds.count("w")
assert UNITS % RAW == 0 and FIRST_MOD % RAW == 0
F_GROUPS = [(0, 8), (8, 8), (16, 6)]


def offsets(parts):
    at, out = 0, {}
    for name, width in parts:
        out[name] = (at, at + width)
        at += width
    return out, at


PAR, N_PAR = offsets([
    ("b_mod", 48), ("b_next", 16), ("g1", KC), ("g2", KC), ("conv", 65), ("hconv", 36), ("hconv_b", 12), ("a_log", 8),
    ("dt_bias", 8), ("dn_g", 1), ("sub_g", 1), ("lam", 256), ("w_ba", KC * 16), ("hy_w1", 64), ("hy_b1", 1),
    ("hy_fr", 1), ("hy_b2", 1), ("hy_w2", 64), ("hy_w3", 512), ("hy_d", 4), ("state", 8 * P), ("k_ctx", H * P),
    ("v_ctx", H * P), ("lam_init", 1), ("one_minus_lam", 1)])
CON, N_CON = offsets([
    ("ident", P), ("ones", P), ("tri", 2 * P), ("big", 2 * P), ("perm", P), ("levels", NLEV * 2 * P),
    ("final_g", KC), ("cond", KC * 2), ("b_first", 16)])
ROPE, N_ROPE = offsets([("cos", NS), ("sin", NS)])
HYC, N_HYC = offsets([("z", NT), ("deltas", 512), ("ndist", NCH)])
N_FWD = 4 * L_S + L_P
N_INV = 6 * NS + 2 * NP


class Turns:

    def __init__(self, plan):
        total = {}
        self.where = {}
        for phase, times, fills in plan:
            per = {}
            for name, bank in fills:
                self.where[phase, name] = (bank, total.get(bank, 0), per.get(bank, 0))
                per[bank] = per.get(bank, 0) + 1
            for name, bank in fills:
                b, base, k = self.where[phase, name]
                self.where[phase, name] = (b, base, k, per[b])
            for b, n in per.items():
                total[b] = total.get(b, 0) + times * n
        self.total = total

    def at(self, phase, name, layer, step=0):
        bank, base, k, per = self.where[phase, name]
        ahead = FIRST_FILLS if bank == "GP" else 0
        return bank, layer * self.total[bank] + step * per + (ahead + base + k + 1)


def tile_fills(prefix, tiles):
    return [f for t in range(tiles) for f in ((f"{prefix}{t}_a", ("G0", "GP")[t % 2]),
                                              (f"{prefix}{t}_b", ("G1", "M4")[t % 2]))]



def mod_fills(n):
    return [(f"{kind}{i}", "GP") for i in range(n) for kind in ("rows", "cols")]


GROUPS = [("f", 0, 4), ("b", 4, 4), ("p", 8, 2)]


def delta_fills():
    names = ["R_f", "R_b", "R_p", "tok_k", "tok_v", "tok_p", "KK_s", "QK_s", "KQ_p"]
    names += [f"X0_{g}" for g, _, _ in GROUPS]
    for lev in range(1, NLEV):
        names += [f"P{lev}_{g}" for g, _, _ in GROUPS]
        for g, _, _ in GROUPS:
            names += [f"D{lev}_{g}"] if lev < NLEV - 1 else []
            names += [f"E{lev}_{g}"]
    names += ["vn_pf", "vn_pb"]
    names += ["ssq_q", "ssq_k", "ssq_p"]
    names += ["o_p"]
    for step in range(4):
        names += [f"kq{step}_f", f"kq{step}_b", f"vn{step}_f", f"vn{step}_b", f"o{step}_f", f"o{step}_b"]
    names += ["oT_s", "oT_p"]
    return [(n, f"M{i % 5}") for i, n in enumerate(names)]


SCORE_BANKS = [("M0", "M1"), ("M2", "M3"), ("G0", "G1")]

PLAN = [
    ("norm1", 1, [("ss_s", "M2"), ("ss_p", "M3")]),
    ("A", 4, tile_fills("t", 4)),
    ("ba", 1, [("ba", "M4"), ("cum", "M0")]),
    ("first", 1, [("ssq_q", "M1"), ("ssq_k", "M2"), ("ssq_p", "M3")]),
    ("delta", H, delta_fills() + mod_fills(2)),
    ("B", 2, tile_fills("t", 4)),
    ("V", 1, [(f"c{c}_{s}", ("G0", "G1", "GP")[c]) for s in range(2) for c in range(3)]),
    ("attn", H, [("rot_q", "M0"), ("rot_k", "M1")]
     + [f for qb in range(4) for f in
        [(f"S{m}_{qb}{part}", SCORE_BANKS[(2 * qb + m) % 3][part == "b"]) for m in range(2) for part in "ab"]
        + [(f"T4_{qb}", "M4"), (f"T1_{qb}", "M4")]]
     + [("S_p0", "M0"), ("S_p1", "M2"), ("T_p", "M4"), ("o_s", "M1"), ("o_p", "M3"), ("oss_s", "M0"),
        ("oss_p", "M2")] + mod_fills(1)),
    ("C", 3, tile_fills("t", 4)),
    ("hyfil", 1, [("h1_s", "M0"), ("h1_p", "M1"), ("h2_s", "M2"), ("h2_p", "M3")]
     + [(f"h3_{c}", f"M{c}") for c in range(NCH)] + [("norm", "M0")]
     + [(f"H{i}", f"M{(i + 1) % 5}") for i in range(8)]),
    ("hytr", 1, [f for j in range(4) for f in ((f"g_s{j}", f"M{2 * j % 5}"), (f"g_p{j}", f"M{(2 * j + 1) % 5}"))]),
    ("hydft", 1, [(f"X{i}", f"M{i % 5}") for i in range(8)]
     + [(f"y_s{c}", f"M{(c + 3) % 5}") for c in range(4)] + [("y_p", "M2")]),
    ("mix", 3, [f for half in range(2) for kind in "gb" for f in tile_fills(f"{kind}{half}_", 4)]),
    ("out", 2, tile_fills("t", 4)),
    ("norm2", 1, [("ss_s", "M2"), ("ss_p", "M3")]),
    ("f1_0", 4, tile_fills("t", 4)), ("f2_0", 2, tile_fills("t", 4)),
    ("f1_1", 4, tile_fills("t", 4)), ("f2_1", 2, tile_fills("t", 4)),
    ("f1_2", 3, tile_fills("t", 4)), ("f2_2", 2, tile_fills("t", 4)),
]
FIRST_FILLS = 2 * (FIRST_MOD // 4)
TURNS = Turns(PLAN)
BANKS = ["M0", "M1", "M2", "M3", "M4", "G0", "G1", "GP"]


class Signal:

    def __init__(self, sem, per):
        self.sem, self.per = sem, per

    def at(self, step, k):
        return step * self.per + k


def trunk_program(nc, W, PARAMS, CONSTS, ROPES, HYCS, FWD, INV, X, Y, KNEW, VNEW, SNEW):
    ctx = ExitStack()
    with ctx:
        start = -(-nc.sbuf_base // 32) * 32
        arena = ctx.enter_context(nc.sbuf_tensor("arena", [P, (nc.sbuf_usable_end - start) // 4 - 16], F32))
        at_now = [start]
        place = {}

        def sb(name, cols):
            place[name] = at_now[0]
            t = nc.alloc_sbuf_tensor_at(name, [P, cols], F32, offset=at_now[0])
            at_now[0] += -(-cols * 4 // 32) * 32
            assert at_now[0] <= nc.sbuf_usable_end, name
            return t

        def rounded(name, room, col, cols):
            return nc.alloc_sbuf_tensor_at(name, [P, cols], F32R, offset=place[room] + 4 * col)

        x = sb("x", KC * NT)
        h = sb("h", KC * NT)
        ring = sb("ring", RAW * UNIT)
        whi_ = sb("whi_room", HI * UNIT)
        big = sb("big", 16 * PADW + 12 * NT)
        outs = sb("outs", 12 * NT)
        par = sb("par", N_PAR)
        con = sb("con", N_CON)
        modc = sb("modc", 48 * 2)
        gain = sb("gain", 2 * KC * 2)
        cond = sb("cond_s", KC * 2)
        col = sb("col", 440)
        small = sb("small", 96)
        sc = sb("sc", 4352)

        wlo = rounded("w_lo", "ring", 0, RAW * UNIT)
        whi = rounded("w_hi", "whi_room", 0, HI * UNIT)
        PB0 = 16 * PADW
        room_a = rounded("room_a", "big", 0, 16 * NT)
        room_b = rounded("room_b", "big", PB0, 12 * NT)
        room_o = rounded("room_o", "outs", 0, 12 * NT)

        def tiles_of(room, first, n):
            return [room[:, (first + i) * NT:(first + i + 1) * NT] for i in range(n)]

        h_a = (tiles_of(room_b, 0, 8), tiles_of(room_b, 8, 4) + tiles_of(room_o, 4, 4))
        h_b = (tiles_of(room_a, 0, 8), tiles_of(room_a, 8, 8))
        h_c = (tiles_of(room_b, 0, 8), tiles_of(room_b, 8, 4) + tiles_of(room_o, 8, 4))
        o_m = (tiles_of(room_b, 0, 4), tiles_of(room_b, 4, 4))
        h_f = (tiles_of(room_o, 0, 8), tiles_of(room_o, 8, 4) + tiles_of(room_b, 0, 4))
        act_f = h_b

        xv = x[:, :].rearrange("p (k t) -> p k t", k=KC)
        hv = h[:, :].rearrange("p (k t) -> p k t", k=KC)
        PA = big[:, 0:16 * PADW].rearrange("p (i t) -> p i t", t=PADW)
        ov = outs[:, :].rearrange("p (i t) -> p i t", t=NT)
        modv = modc[:, :].rearrange("p (n s) -> p n s", s=2)
        gainv = gain[:, :].rearrange("p (i n s) -> p i n s", i=2, s=2)
        condv = cond[:, :].rearrange("p (k s) -> p k s", s=2)
        pads = [PA[:, :, 0:2], PA[:, :, 514:516], PA[:, :, 644:648]]

        def pr(name, rows=P):
            a, b = PAR[name]
            return par[0:rows, a:b]

        def cn(name, rows=P):
            a, b = CON[name]
            return con[0:rows, a:b]

        def cut(tensor, at, *shape):
            n = int(np.prod(shape))
            v = tensor[:, at:at + n]
            if len(shape) == 2:
                v = v.rearrange("p (a b) -> p a b", a=shape[0])
            if len(shape) == 3:
                v = v.rearrange("p (a b c) -> p a b c", a=shape[0], b=shape[1])
            return v

        ident_r = rounded("ident_r", "con", CON["ident"][0], P)
        ones_r = rounded("ones_r", "con", CON["ones"][0], P)
        big_r = rounded("big_r", "con", CON["big"][0], 2 * P)
        ident, ones = ident_r[:, :].bitcast(F32), ones_r[:, :].bitcast(F32)
        tri = cn("tri").rearrange("p (d n) -> p d n", d=2)
        levels = cn("levels").rearrange("p (l d n) -> p l d n", l=NLEV, d=2)

        def repeated(ap, n):
            return ap.unsqueeze(1).to_broadcast([P, n, ap.shape[-1]])

        cv = cut(sc, 0, 2, CW)
        ahead = cut(whi_, 0, 3, CW)
        mod_rows = sc[0:2, 1288:1800]
        mod_rows_b = sc[0:2, 3712:4224]
        osq_d = cut(sc, 3976, P)
        gh_hi = nc.alloc_sbuf_tensor_at("gh_hi", [P, 16], F32R, offset=place["sc"] + 4 * 4104)
        gh_lo = cut(sc, 4120, NCH, 2)
        ghh = gh_hi[:, 0:10].rearrange("p (c d) -> p c d", d=2)
        sq = cut(sc, 1926, 2, NT)
        rr = cut(sc, 3206, 2, P)
        vn = cut(sc, 3462, 4, P)
        ktok = cut(big, PB0 + 4864, NCH, P)
        vtok = cut(big, PB0 + 5504, NCH, P)
        oacc = cut(big, PB0 + 6144, NCH, P)
        t1 = cut(big, PB0 + 6784, 2, P)
        S = cut(big, PB0 + 7040, 2, P)
        DT = cut(big, PB0, 10, P)
        AT = cut(big, PB0 + 1280, 10, P)
        kd = cut(big, PB0 + 2560, 10, P)
        snew = cut(big, PB0 + 3840, 8, P)
        X_ = cut(outs, 4 * NT, 10, P)
        XT = cut(outs, 4 * NT + 1280, 10, P)
        AL = cut(outs, 4 * NT + 2560, 10, P)
        PS = cut(outs, 4 * NT + 3840, 10, P)
        gu_hi = rounded("gu_hi", "outs", 4 * NT + 2560, 10 * P)
        gu_lo = rounded("gu_lo", "outs", 4 * NT + 3840, 10 * P)
        tok5 = (NCH, 8)
        beta = cut(col, 0, *tok5)
        gg = cut(col, 40, *tok5)
        gcum = cut(col, 80, *tok5)
        ngc = cut(col, 120, *tok5)
        egc = cut(col, 160, *tok5)
        negc = cut(col, 200, *tok5)
        egl = cut(col, 240, *tok5)
        ekd = cut(col, 280, *tok5)
        tmpc = cut(col, 320, *tok5)
        tmpd = cut(col, 360, *tok5)
        expa = cut(col, 400, 8)
        orn = cut(col, 408, NCH)
        epsc = cut(small, 0, 4)
        lamc = cut(small, 4, 8)
        subg = cut(small, 12, 1)
        mx = cut(small, 16, 2, 2)
        rsum = cut(small, 24, 2, 2)
        rinv = cut(small, 32, 2, 2)
        hyn = cut(small, 40, 2, 4)

        gh = cut(small, 48, NCH, 2)
        eh = cut(small, 58, NCH, 2)

        PBq = cut(big, PB0, 8, NT)
        VB = cut(big, PB0 + 8 * NT, NCH, 512)
        rope = sc[:, 0:N_ROPE]
        qall = cut(sc, 1024, NT)
        kall = cut(sc, 1664, 768)
        vall = cut(sc, 2432, 6, P)
        rtmp = cut(sc, 3200, NS)
        osb = cut(big, 7040, NT)
        osq = cut(big, 7680, NT)
        pp = cut(big, 0, 2, 2, NT)
        aa = cut(big, 2560, 2, NT)
        aT = cut(big, 3840, NCH, NS)
        aTp = cut(big, 6400, P)
        knew = cut(big, 6528, H, P)

        hyc = cut(sc, 3072, N_HYC)
        fwd = cut(big, PB0, N_FWD)
        Hs = cut(big, PB0 + N_FWD, 8, NS)
        inv = cut(big, 4 * PADW, N_INV)
        Ys = cut(sc, 0, 6, NS)
        Yp = cut(big, 4 * PADW + N_INV, 2, NS)
        tok = cut(big, 12 * PADW, NCH, 512)
        arg = cut(sc, 0, NT)
        redu = cut(sc, 640, NT)
        hdn = cut(sc, 1280, NT)
        dec = cut(sc, 1920, 512)
        ABSH = [cut(big, PB0 + N_FWD + c * 512, 512) for c in range(NCH)]
        ctmp = cut(sc, 0, CW)

        merged = hv
        sig = cut(big, PB0 + 5120, 4, NT)
        mtmp = cut(sc, 0, 2, NT)
        gsil = cut(big, PB0 + 4 * NT, 2, NT)
        rstd = cut(sc, 3200, NT)

        pair_g = ctx.enter_context(nc.psum_tensor("ps_G01", [P, 1024], F32))
        pair_h = ctx.enter_context(nc.psum_tensor("ps_GPM4", [P, 1024], F32))
        pair0 = ctx.enter_context(nc.psum_tensor("ps_M01", [P, 1024], F32))
        pair1 = ctx.enter_context(nc.psum_tensor("ps_M23", [P, 1024], F32))
        bank = dict(G0=pair_g[:, 0:512], G1=pair_g[:, 512:1024], GP=pair_h[:, 0:512], M4=pair_h[:, 512:1024],
                    M0=pair0[:, 0:512], M1=pair0[:, 512:1024], M2=pair1[:, 0:512], M3=pair1[:, 512:1024])
        HALF = NT // 2
        over_banks = [pair[:, 512 - HALF:512 + HALF] for pair in (pair_g, pair_h)]

        def sem(name):
            return ctx.enter_context(nc.semaphore(name))

        def sig_(name, per):
            return Signal(sem(name), per)

        filled = {b: sem(f"filled_{b}") for b in BANKS}
        freed = {b: sem(f"freed_{b}") for b in BANKS}
        landed = [sem(f"unit_landed_{s}") for s in range(RAW)]
        unit_used = sem("unit_used")
        unit_split = sem("unit_split")
        h_split = sig_("h_split", 4)
        o_split = sem("o_split")
        m_split = sig_("merged_split", 1)
        hf_split = sig_("h_ffn_split", 1)
        inverse_done = sem("inverse_done")
        mod_ready = sig_("mod_ready", 1)
        hi_ready = sig_("hi_tiles_ready", 4 * KC)
        om_hi = sem("o_hi_ready")
        mg_hi = sig_("merged_hi_ready", KC)
        hf_hi = sig_("h_ffn_hi_ready", KC)
        act_lin = sem("act_product_ready")
        act_hi = sem("act_hi_ready")
        consts_in = sem("consts_in")
        passed = sem("passed")
        cond_ready = sem("cond_ready")
        rows_first = sem("first_mod_rows")
        rows_delta = sig_("mod_rows_delta", 2)
        rows_attn = sig_("mod_rows_attn", 1)
        mod_turned = sem("mod_turned")
        par_in = sig_("params_in", 16)
        rope_in = sig_("rope_in", 16)
        hyc_in = sig_("hyena_consts_in", 16)
        fwd_in = sig_("fwd_dft_in", 16)
        inv_in = sig_("inv_dft_in", 16)
        y_stored = sem("y_stored")
        state_stored = sig_("state_stored", 16)
        cache_stored = sig_("cache_stored", 32)
        attn_room = sem("attn_rooms_free")
        layer_done = sig_("layer_done", 1)
        pads_zero = sig_("pads_zero", 2)
        sq_ready = sig_("squares_ready", 2 * KC)
        rms_ready = sig_("rms_ready", 2)
        hnorm = sig_("h_scaled", 2 * KC)
        h_ready = sig_("h_ready", 2)
        proj_a = sig_("proj_a_ready", 1)
        g_ready = sig_("g_ready", 1)
        beta_done = sig_("beta_done", 1)
        ab_lin = sig_("alpha_biased", 1)
        sp_ready = sig_("softplus_parts", 1)
        cums = sig_("cumsums_copied", 1)
        cumx = sig_("cumsum_exps", 1)
        gu_ready = sig_("gu_ready", 1)
        kd_ready = sig_("kd_ready", 1)
        conv_done = sig_("conv_done", 3)
        silu_done = sig_("silu_done", 3)
        rq_ready = sig_("rq_ready", 1)
        qk_ready = sig_("qk_normalised", 1)
        tok_ready = sig_("tok_ready", 1)
        decay = sig_("decay_ready", 3)
        at_ready = sig_("at_ready", 3)
        al_ready = sig_("al_ready", 3 * NLEV)
        xt_ready = sig_("xt_ready", 3 * NLEV)
        x_ready = sig_("x_ready", 3 * (NLEV - 2))
        x0_ready = sig_("x0_ready", 3)
        p_ready = sig_("p_copied", 3 * (NLEV - 1))
        qkd_ready = sig_("qkd_ready", 1)
        r_ready = sig_("r_ready", 8)
        vn_ready = sig_("vn_ready", 10)
        s_ready = sig_("s_ready", 7)
        osum = sig_("o_summed", 1)
        orms = sig_("o_rms", 1)
        oscaled = sig_("o_scaled", 1)
        siluz = sig_("silu_z", 1)
        head_done = sig_("delta_head_done", 1)
        proj_b = sig_("proj_b_ready", 1)
        lam_done = sig_("lambda_ready", 2)
        lam_dot = sig_("lambda_dots", 1)
        qcopy = sig_("attn_copies", 1)
        rot_done = sig_("rotated", 2)
        neg_max = sig_("neg_max", 10)
        exp_done = sig_("exp_done", 10)
        a_ready = sig_("a_ready", 5)
        at_copied = sig_("aT_copied", 9)
        o_copied = sig_("o_copied", 2)
        osq_done = sig_("o_squared", 1)
        orms_b = sig_("o_rms_b", 1)
        attn_done = sig_("attn_head_done", 1)
        c_tile = sem("proj_c_tiles")
        arg_ready = sig_("arg_ready", 2)
        sin_done = sig_("sin_done", 2)
        dec_ready = sig_("decay_table", NCH)
        filt_ready = sig_("filter_ready", NCH)
        abs_ready = sig_("abs_ready", NCH)
        spec_ready = sig_("filter_spectrum", 8)
        gv_ready = sig_("gv_ready", 4)
        gvtok = sig_("gv_by_token", 4)
        xprod = sig_("spectra_multiplied", 4)
        hy_done = sig_("hyena_done", 1)
        gates = sem("gates_ready")
        branch_even = sem("even_branch_tile_ready")
        merge = sem("merge_done")
        merged_ready = sig_("merged_ready", 1)
        xres1 = sig_("x_after_mix", 1)
        gate_silu = sem("gate_silu")
        act_ready = sem("act_ready")
        act_room = sem("act_room_free")
        y_ready = sem("y_ready")

        block = ctx.enter_context(nc.Block())

        def turn(phase, name, layer, step=0):
            b, n = TURNS.at(phase, name, layer, step)
            return bank[b], filled[b], freed[b], n

        def unit_no(phase, k, layer, step):
            return layer * UNITS + step * len(PHASE_AT[phase][2]) + (FIRST_MOD + PHASE_AT[phase][0] + k)

        def unit_filled(phase, k, layer, step):
            return unit_used, unit_no(phase, k, layer, step) + 1

        G3 = [(0, 0, 4), (1, 4, 4), (2, 8, 2)]

        def staging(layer, n):
            return layer * (H + 1) + n

        @block.sync
        def _(sp):
            sp.dma_start(xv, X).then_inc(consts_in, 16)
            sp.dma_start(con[:, :], CONSTS).then_inc(consts_in, 16)
            rv = ring[:, :].rearrange("p (s n) -> p s n", s=RAW)
            for s in range(RAW):
                sp.dma_start(rv[:, s, :], W[s]).then_inc(landed[s], 16)
            with sp.Fori(1, (FIRST_MOD + DEPTH * UNITS) // RAW) as i:
                for s in range(RAW):
                    sp.wait_ge(unit_used, i * RAW + (s - RAW + 1))
                    sp.dma_start(rv[:, s, :], W[bass.ds(i * RAW + s, 1)].rearrange("a p n -> p (a n)")
                                 ).then_inc(landed[s], 16)
            sp.wait_ge(y_ready, 2)
            sp.dma_start(Y, hv).then_inc(y_stored, 16)
            sp.wait_ge(y_stored, 16)
            sp.wait_ge(state_stored.sem, 16 * DEPTH)
            sp.wait_ge(cache_stored.sem, 32 * DEPTH)

        @block.tensor
        def _(pe):
            def raw_unit(number_k, slot):
                pe.wait_ge(landed[slot], number_k)
                return ring[:, slot * UNIT:(slot + 1) * UNIT].rearrange("p (k n) -> p k n", k=KC)

            def parts(phase, k, layer, step, n=P):
                kinds = PHASE_AT[phase][2]
                q = kinds[:k].count("w")
                pe.wait_ge(unit_split, layer * SPLITS + step * kinds.count("w") + (PHASE_AT[phase][1] + q + 1))
                lo = (PHASE_AT[phase][0] + k) % RAW
                hi = (PHASE_AT[phase][1] + q) % HI
                return (whi[:, hi * UNIT:(hi + 1) * UNIT].rearrange("p (k n) -> p k n", n=n),
                        wlo[:, lo * UNIT:(lo + 1) * UNIT].rearrange("p (k n) -> p k n", n=n))

            def by_parts(ap, w, n0, acts, a, b, chunks=KC, turned=None):
                for k in range(chunks):
                    for i, (wi, ai) in enumerate(((0, 0), (0, 1), (1, 0))):
                        m = pe.matmul(ap, w[wi][:, k, n0:n0 + P], acts[ai][k][:, a:b], start=(k == 0 and i == 0),
                                      stop=(k == chunks - 1 and i == 2))
                        if turned is not None and k == 0 and i == 0:
                            m.then_inc(turned, 1)
                return m

            def tile_product(phase, name, t, layer, step, w, n0, acts, chunks=KC):
                _, fl_b = fill(phase, name + "_b", layer, step)
                _, fl_a = fill(phase, name + "_a", layer, step)
                tile = over_banks[t % 2]
                by_parts(tile[:, 0:HALF], w, n0, acts, 0, HALF, chunks, fl_a)
                return by_parts(tile[:, HALF:NT], w, n0, acts, HALF, NT, chunks, fl_b)

            def fill(phase, name, layer, step=0):
                ap, fl, fr, n = turn(phase, name, layer, step)
                pe.wait_ge(fr, n)
                return ap, fl

            def products(phase, prefix, k, layer, step, acts, chunks=KC):
                for t in range(4):
                    w = parts(phase, k + t, layer, step)
                    tile_product(phase, f"{prefix}{t}", t, layer, step, w, 0, acts, chunks).then_inc(unit_used, 1)

            def modulation(k, slot, number):
                w = raw_unit(number, slot)
                for c in range(KC):
                    m = pe.matmul(bank["GP"][0:2, k * P:(k + 1) * P], condv[:, c, :], w[:, c, :],
                                  start=(c == 0), stop=(c == KC - 1))
                m.then_inc(unit_used, 1)

            def mod_units(phase, ks, layer, step):
                per = len(PHASE_AT[phase][2])
                for k in ks:
                    if k % 4 == 0:
                        fill(phase, f"rows{k // 4}", layer, step)
                    n = FIRST_MOD + PHASE_AT[phase][0] + k
                    modulation(k % 4, n % RAW, 16 * (layer * (UNITS // RAW) + step * (per // RAW) + (n // RAW + 1)))

            def turn_rows(rows):
                pe.sem_inc(passed, 1)
                for t in range(4):
                    m = pe.transpose(bank["GP"][:, 2 * t:2 * t + 2], rows[:, t * P:(t + 1) * P], ident[0:2, 0:2])
                m.then_inc(mod_turned, 1)

            def sum_squares(phase, layer, src, k_count, wait):
                aps, fls = fill(phase, "ss_s", layer)
                app, flp = fill(phase, "ss_p", layer)
                for k in range(k_count):
                    pe.wait_ge(wait.sem, wait.at(layer, (0 if phase == "norm1" else KC) + k + 1))
                    ms = pe.matmul(aps, ones, src[:, k, 0:NS], start=(k == 0), stop=(k == k_count - 1))
                    if k == k_count - 1:
                        ms.then_inc(fls, 1)
                    mp = pe.matmul(app[:, 0:NP], ones, src[:, k, NS:NT], start=(k == 0), stop=(k == k_count - 1))
                mp.then_inc(flp, 1)

            pe.wait_ge(consts_in, 32)
            pe.wait_ge(cond_ready, 1)
            with pe.Fori(0, FIRST_MOD // 4) as i:
                pe.wait_ge(freed["GP"], i * 2 + 1)
                for s in range(4):
                    modulation(s, s, 16 * i + 16)
                pe.wait_ge(rows_first, i + 1)
                turn_rows(mod_rows)
            with pe.Fori(0, DEPTH) as L:
                sum_squares("norm1", L, hv, KC, sq_ready)
                pe.wait_ge(h_split.sem, h_split.at(L, 1))
                pe.sem_inc(passed, 1)
                with pe.Fori(0, 4) as i:
                    products("A", "t", 0, L, i, h_a)
                pe.wait_ge(par_in.sem, par_in.at(L, 16))
                w_ba = pr("w_ba").rearrange("p (k n) -> p k n", k=KC)
                ap, fl = fill("ba", "ba", L)
                for c in range(NCH):
                    for k in range(KC):
                        m = pe.matmul(ap[:, c * 16:(c + 1) * 16], hv[:, k, c * P:(c + 1) * P], w_ba[:, k, :],
                                      start=(k == 0), stop=(k == KC - 1))
                m.then_inc(fl, 1)
                pe.wait_ge(g_ready.sem, g_ready.at(L, 1))
                ap, fl = fill("ba", "cum", L)
                gflat = col[:, 40:80]
                pe.matmul(ap[:, 0:40], tri[:, 0, :], gflat, start=True, stop=True)
                pe.matmul(ap[:, 40:80], tri[:, 1, :], gflat, start=True, stop=True)
                pe.matmul(ap[:, 80:120], ones, gflat, start=True, stop=True).then_inc(fl, 1)

                def norms_squared(j, filler, n):
                    if j == 0:
                        pe.wait_ge(silu_done.sem, silu_done.at(staging(L, n), 2))
                    ap, fl = filler(("ssq_q", "ssq_k", "ssq_p")[j])
                    if j < 2:
                        m = pe.matmul(ap, ones, sq[:, j, 0:NS], start=True, stop=True)
                    else:
                        for i in range(2):
                            m = pe.matmul(ap[:, i * P:(i + 1) * P], ones, sq[:, i, NS:NT], start=True, stop=True)
                    m.then_inc(fl, 1)

                for j in range(3):
                    norms_squared(j, lambda name: fill("first", name, L), 0)

                with pe.Fori(0, H) as hd:
                    Q = L * H + hd

                    def f(name):
                        return fill("delta", name, L, hd)

                    pe.wait_ge(gu_ready.sem, gu_ready.at(Q, 1))
                    for g, first, n in G3:
                        ap, fl = f(["R_f", "R_b", "R_p"][g])
                        out = ap[:, 0:n * P].rearrange("p (a b) -> p a b", a=n)
                        br = big_r[:, :].rearrange("p (d n) -> p d n", d=2)
                        pe.matmul(out, ident_r[:, :], br if g == 2 else repeated(br[:, g, :], 4), start=True, stop=False)
                        pe.matmul(ap[:, 0:n * P], ones_r[:, :], gu_hi[:, first * P:(first + n) * P], start=False, stop=False)
                        pe.matmul(ap[:, 0:n * P], ones_r[:, :], gu_lo[:, first * P:(first + n) * P], start=False, stop=True
                                  ).then_inc(fl, 1)
                    pe.wait_ge(qk_ready.sem, qk_ready.at(Q, 1))
                    pe.wait_ge(silu_done.sem, silu_done.at(staging(L, hd), 3))
                    kv = (cv[:, 1, :], ahead[:, 2, :])
                    for src, name in zip(kv, ("tok_k", "tok_v")):
                        ap, fl = f(name)
                        for c in range(4):
                            m = pe.transpose(ap[:, c * P:(c + 1) * P], src[:, c * P:(c + 1) * P], ident)
                        m.then_inc(fl, 1)
                    ap, fl = f("tok_p")
                    for i, src in enumerate(kv):
                        m = pe.transpose(ap[:, i * P:(i + 1) * P], src[:, NS + 2:NS + 2 + P], ident)
                    m.then_inc(fl, 1)

                    def qk(j, c):
                        at = c * P if c < 4 else NS + 2
                        return cv[:, j, at:at + P]

                    for j, name in ((1, "KK_s"), (0, "QK_s")):
                        ap, fl = f(name)
                        for c in range(4):
                            m = pe.matmul(ap[:, c * P:(c + 1) * P], qk(1, c), qk(j, c), start=True, stop=True)
                        m.then_inc(fl, 1)
                    ap, fl = f("KQ_p")
                    for i, j in enumerate((1, 0)):
                        m = pe.matmul(ap[:, i * P:(i + 1) * P], qk(1, 4), qk(j, 4), start=True, stop=True)
                    m.then_inc(fl, 1)
                    mod_units("delta", (0, 1, 2, 3), L, hd)
                    for g, first, n in G3:
                        pe.wait_ge(xt_ready.sem, xt_ready.at(Q, g + 1))
                        ap, fl = f(f"X0_{GROUPS[g][0]}")
                        for c in range(n):
                            m = pe.transpose(ap[:, c * P:(c + 1) * P], XT[:, first + c, :], ident)
                        m.then_inc(fl, 1)
                    for lev in range(1, NLEV):
                        for g, first, n in G3:
                            pe.wait_ge(al_ready.sem, al_ready.at(Q, 3 * lev + g + 1))
                            if lev == 1:
                                pe.wait_ge(x0_ready.sem, x0_ready.at(Q, g + 1))
                            else:
                                pe.wait_ge(x_ready.sem, x_ready.at(Q, 3 * (lev - 2) + g + 1))
                            ap, fl = f(f"P{lev}_{GROUPS[g][0]}")
                            for c in range(n):
                                m = pe.matmul(ap[:, c * P:(c + 1) * P], AL[:, first + c, :], X_[:, first + c, :],
                                              start=True, stop=True)
                            m.then_inc(fl, 1)
                        for g, first, n in G3:
                            pe.wait_ge(p_ready.sem, p_ready.at(Q, 3 * (lev - 1) + g + 1))
                            if lev > 1:
                                pe.wait_ge(xt_ready.sem, xt_ready.at(Q, 3 * (lev - 1) + g + 1))
                            if lev < NLEV - 1:
                                ap, fl = f(f"D{lev}_{GROUPS[g][0]}")
                                for c in range(n):
                                    m = pe.matmul(ap[:, c * P:(c + 1) * P], XT[:, first + c, :], PS[:, first + c, :],
                                                  start=True, stop=True)
                                m.then_inc(fl, 1)
                            ap, fl = f(f"E{lev}_{GROUPS[g][0]}")
                            for c in range(n):
                                m = pe.matmul(ap[:, c * P:(c + 1) * P], PS[:, first + c, :], XT[:, first + c, :],
                                              start=True, stop=True)
                            m.then_inc(fl, 1)
                    for d in range(2):
                        pe.wait_ge(xt_ready.sem, xt_ready.at(Q, 3 * (NLEV - 1) + 3))
                        ap, fl = f(["vn_pf", "vn_pb"][d])
                        pe.matmul(ap[:, 0:P], XT[:, 8 + d, :], vtok[:, 4, :], start=True, stop=True).then_inc(fl, 1)
                    for j in range(3):
                        norms_squared(j, f, hd + 1)
                    pe.wait_ge(rows_delta.sem, rows_delta.at(Q, 1))
                    fill("delta", "cols0", L, hd)
                    turn_rows(mod_rows)
                    pe.wait_ge(vn_ready.sem, vn_ready.at(Q, 2))
                    pe.wait_ge(qkd_ready.sem, qkd_ready.at(Q, 1))
                    pe.wait_ge(kd_ready.sem, kd_ready.at(Q, 1))
                    ap, fl = f("o_p")
                    pe.matmul(ap[:, 0:P], DT[:, 8, :], vn[:, 2, :], start=True, stop=False)
                    pe.matmul(ap[:, 0:P], DT[:, 9, :], vn[:, 3, :], start=False, stop=True)
                    pe.matmul(ap[:, P:2 * P], kd[:, 8, :], vn[:, 2, :], start=True, stop=True)
                    pe.matmul(ap[:, 2 * P:3 * P], kd[:, 9, :], vn[:, 3, :], start=True, stop=True).then_inc(fl, 1)
                    for step in range(4):
                        for d in range(2):
                            c = step if d == 0 else 3 - step
                            if step:
                                pe.wait_ge(s_ready.sem, s_ready.at(Q, 1 + 2 * (step - 1) + d + 1))
                            else:
                                pe.wait_ge(s_ready.sem, s_ready.at(Q, 1))
                            ap, fl = f(f"kq{step}_{'fb'[d]}")
                            pe.matmul(ap[:, 0:P], qk(1, c), S[:, d, :], start=True, stop=True)
                            pe.matmul(ap[:, P:2 * P], qk(0, c), S[:, d, :], start=True, stop=True).then_inc(fl, 1)
                        for d in range(2):
                            c = step if d == 0 else 3 - step
                            pe.wait_ge(r_ready.sem, r_ready.at(Q, 2 * step + d + 1))
                            ap, fl = f(f"vn{step}_{'fb'[d]}")
                            pe.matmul(ap[:, 0:P], XT[:, 4 * d + c, :], rr[:, d, :], start=True, stop=True).then_inc(fl, 1)
                        for d in range(2):
                            c = step if d == 0 else 3 - step
                            pe.wait_ge(vn_ready.sem, vn_ready.at(Q, 2 + 2 * step + d + 1))
                            ap, fl = f(f"o{step}_{'fb'[d]}")
                            m = pe.matmul(ap[:, 0:P], DT[:, 4 * d + c, :], vn[:, d, :], start=True, stop=True)
                            if step < 3:
                                m = pe.matmul(ap[:, P:2 * P], kd[:, 4 * d + c, :], vn[:, d, :], start=True, stop=True)
                            m.then_inc(fl, 1)
                        if step < 2:
                            mod_units("delta", (4 + 2 * step, 5 + 2 * step), L, hd)
                    pe.wait_ge(rows_delta.sem, rows_delta.at(Q, 2))
                    fill("delta", "cols1", L, hd)
                    turn_rows(mod_rows)
                    pe.wait_ge(oscaled.sem, oscaled.at(Q, 1))
                    ap, fl = f("oT_s")
                    for c in range(4):
                        m = pe.transpose(ap[:, c * P:(c + 1) * P], oacc[:, c, :], ident)
                    m.then_inc(fl, 1)
                    ap, fl = f("oT_p")
                    pe.transpose(ap[:, 0:P], oacc[:, 4, :], ident).then_inc(fl, 1)

                pe.wait_ge(h_split.sem, h_split.at(L, 2))
                pe.sem_inc(passed, 1)
                with pe.Fori(0, 2) as i:
                    products("B", "t", 0, L, i, h_b)
                for s in range(2):
                    parts("V", 2 * s, L, 0)
                    parts("V", 2 * s + 1, L, 0)
                    slot = (PHASE_AT["V"][0] + 2 * s) % RAW
                    assert PHASE_AT["V"][1] % HI == 0
                    w = (whi[:, :].rearrange("p (u k n) -> p k u n", u=2, k=KC),
                         wlo[:, slot * UNIT:(slot + 2) * UNIT].rearrange("p (u k n) -> p k u n", u=2, k=KC))
                    for c in range(NCH):
                        if c % 2 == 0:
                            ap, fl = fill("V", f"c{c // 2}_{s}", L)
                        to = ap[:, (c % 2) * 2 * P:(c % 2 + 1) * 2 * P].rearrange("p (u n) -> p u n", u=2)
                        for k in range(KC):
                            for i, (wi, ai) in enumerate(((0, 0), (0, 1), (1, 0))):
                                m = pe.matmul(to, h_b[ai][k][:, c * P:(c + 1) * P], w[wi][:, k, :, :],
                                              start=(k == 0 and i == 0), stop=(k == KC - 1 and i == 2))
                        if c in (1, 3):
                            m.then_inc(fl, 1)
                    m.then_inc(unit_used, 2)

                with pe.Fori(0, H) as hd:
                    Q = L * H + hd

                    def f(name):
                        return fill("attn", name, L, hd)

                    pe.wait_ge(proj_b.sem, proj_b.at(L, 1))
                    for j, name in enumerate(("rot_q", "rot_k")):
                        ap, fl = f(name)
                        pe.matmul(ap, cn("perm"), PBq[:, bass.ds(hd + 4 * j, 1), 0:NS].rearrange("p a t -> p (a t)"),
                                  start=True, stop=True).then_inc(fl, 1)
                    pe.wait_ge(rot_done.sem, rot_done.at(Q, 2))
                    pe.wait_ge(qcopy.sem, qcopy.at(Q, 1))

                    def transposed(qb):
                        pe.wait_ge(a_ready.sem, a_ready.at(Q, qb + 1))
                        ap, fl = f(f"T4_{qb}")
                        for j in range(4):
                            m = pe.transpose(ap[:, j * P:(j + 1) * P], aa[:, qb % 2, j * P:(j + 1) * P], ident)
                        m.then_inc(fl, 1)
                        ap, fl = f(f"T1_{qb}")
                        pe.transpose(ap[:, 0:P], aa[:, qb % 2, 4 * P:5 * P], ident).then_inc(fl, 1)

                    for qb in range(4):
                        for m_ in range(2):
                            rows = slice(64 * m_, 64 * m_ + 64)
                            q_ = qall[rows, qb * P:(qb + 1) * P]
                            ap, fl = f(f"S{m_}_{qb}a")
                            pe.matmul(ap, q_, kall[rows, 0:NS], start=True, stop=True).then_inc(fl, 1)
                            ap, fl = f(f"S{m_}_{qb}b")
                            pe.matmul(ap[:, 0:P], q_, kall[rows, NS:NT], start=True, stop=True).then_inc(fl, 1)
                        mod_units("attn", (qb,), L, hd)
                        if qb:
                            transposed(qb - 1)
                    for m_ in range(2):
                        rows = slice(64 * m_, 64 * m_ + 64)
                        ap, fl = f(f"S_p{m_}")
                        pe.matmul(ap[:, 0:P], qall[rows, NS:NT], kall[rows, NT:NT + P], start=True, stop=True
                                  ).then_inc(fl, 1)
                    transposed(3)
                    pe.wait_ge(a_ready.sem, a_ready.at(Q, 5))
                    ap, fl = f("T_p")
                    pe.transpose(ap[:, 0:P], aa[:, 0, 0:P], ident)
                    pe.transpose(ap[:, P:2 * P], kall[:, NT:NT + P], ident).then_inc(fl, 1)
                    pe.wait_ge(rows_attn.sem, rows_attn.at(Q, 1))
                    fill("attn", "cols0", L, hd)
                    turn_rows(mod_rows_b)
                    pe.wait_ge(at_copied.sem, at_copied.at(Q, 8))
                    ap, fl = f("o_s")
                    for j in range(NCH):
                        m = pe.matmul(ap, vall[:, j, :], aT[:, j, :], start=(j == 0), stop=(j == NCH - 1))
                    m.then_inc(fl, 1)
                    pe.wait_ge(at_copied.sem, at_copied.at(Q, 9))
                    ap, fl = f("o_p")
                    pe.matmul(ap[:, 0:P], vall[:, 5, :], aTp, start=True, stop=True).then_inc(fl, 1)
                    pe.wait_ge(osq_done.sem, osq_done.at(Q, 1))
                    ap, fl = f("oss_s")
                    pe.matmul(ap, ones, osq[:, 0:NS], start=True, stop=True).then_inc(fl, 1)
                    ap, fl = f("oss_p")
                    pe.matmul(ap[:, 0:P], ones, osq[:, NS:NT], start=True, stop=True).then_inc(fl, 1)

                pe.wait_ge(h_split.sem, h_split.at(L, 3))
                pe.sem_inc(passed, 1)
                with pe.Fori(0, 3) as i:
                    products("C", "t", 0, L, i, h_c)
                pe.wait_ge(hyc_in.sem, hyc_in.at(L, 16))
                za, zb = HYC["z"]
                z_ = hyc[0:17, za:zb]
                for (name_s, name_p), wname, rows, src, k in ((("h1_s", "h1_p"), "hy_w1", 17, z_, 0),
                                                              (("h2_s", "h2_p"), "hy_w2", 64, hdn[0:64, :], 1)):
                    if k:
                        pe.wait_ge(sin_done.sem, sin_done.at(L, 1))
                    ap, fl = fill("hyfil", name_s, L)
                    pe.sem_inc(passed, 1)
                    pe.matmul(ap[0:64, :], pr(wname, rows), src[:, 0:NS], start=True, stop=True).then_inc(fl, 1)
                    ap, fl = fill("hyfil", name_p, L)
                    pe.sem_inc(passed, 1)
                    pe.matmul(ap[0:64, 0:NP], pr(wname, rows), src[:, NS:NT], start=True, stop=True).then_inc(fl, 1)
                pe.wait_ge(sin_done.sem, sin_done.at(L, 2))
                for c in range(NCH):
                    ap, fl = fill("hyfil", f"h3_{c}", L)
                    pe.matmul(ap, hdn[0:64, c * P:(c + 1) * P], pr("hy_w3", 64), start=True, stop=True).then_inc(fl, 1)
                ap, fl = fill("hyfil", "norm", L)
                for seq, chunks in ((0, (0, 1, 2, 3)), (1, (4,))):
                    for j in range(4):
                        for c in chunks:
                            if j == 0:
                                pe.wait_ge(abs_ready.sem, abs_ready.at(L, c + 1))
                            m = pe.matmul(ap[:, seq * 4 + j:seq * 4 + j + 1], ABSH[c][:, j * P:(j + 1) * P],
                                          ones[:, 0:1], start=(c == chunks[0]), stop=(c == chunks[-1]))
                m.then_inc(fl, 1)

                def spectra(phase, prefix):
                    for i in range(6):
                        ap, fl = fill(phase, f"{prefix}{i}", L)
                        for c in range(4):
                            m = pe.matmul(ap, fwd[:, c * L_S + i * P:c * L_S + (i + 1) * P], tok[:, c, :],
                                          start=(c == 0), stop=(c == 3))
                        m.then_inc(fl, 1)
                    for i in range(2):
                        ap, fl = fill(phase, f"{prefix}{6 + i}", L)
                        pe.matmul(ap[0:FQ_P, :], fwd[:, 4 * L_S + i * FQ_P:4 * L_S + (i + 1) * FQ_P], tok[:, 4, :],
                                  start=True, stop=True).then_inc(fl, 1)

                pe.wait_ge(fwd_in.sem, fwd_in.at(L, 16))
                pe.wait_ge(filt_ready.sem, filt_ready.at(L, NCH))
                spectra("hyfil", "H")
                for j in range(4):
                    pe.wait_ge(gv_ready.sem, gv_ready.at(L, j + 1))
                    ap, fl = fill("hytr", f"g_s{j}", L)
                    for c in range(4):
                        m = pe.transpose(ap[:, c * P:(c + 1) * P], ov[:, 8 + j, c * P:(c + 1) * P], ident)
                    m.then_inc(fl, 1)
                    ap, fl = fill("hytr", f"g_p{j}", L)
                    pe.transpose(ap[:, 0:P], ov[:, 8 + j, NS:NT], ident).then_inc(fl, 1)
                pe.wait_ge(gvtok.sem, gvtok.at(L, 4))
                spectra("hydft", "X")
                pe.wait_ge(inv_in.sem, inv_in.at(L, 16))
                for j in range(4):
                    ap, fl = fill("hydft", f"y_s{j}", L)
                    for i in range(6):
                        if j == 0 and i < 3:
                            pe.wait_ge(xprod.sem, xprod.at(L, i + 1))
                        m = pe.matmul(ap, Ys[:, i, j * P:(j + 1) * P], inv[:, i * NS:(i + 1) * NS],
                                      start=(i == 0), stop=(i == 5))
                    m.then_inc(fl, 1)
                pe.wait_ge(xprod.sem, xprod.at(L, 4))
                ap, fl = fill("hydft", "y_p", L)
                for j in range(4):
                    for i in range(2):
                        m = pe.matmul(ap[:, j * P:(j + 1) * P], Yp[0:FQ_P, i, j * P:(j + 1) * P],
                                      inv[0:FQ_P, 6 * NS + i * NP:6 * NS + (i + 1) * NP], start=(i == 0), stop=(i == 1))
                m.then_inc(fl, 1)

                pe.wait_ge(h_split.sem, h_split.at(L, 4))
                pe.sem_inc(passed, 1)
                with pe.Fori(0, 3) as b:
                    for half in range(2):
                        products("mix", f"g{half}_", 6 * half, L, b, h_b)
                        if half == 0:
                            pe.wait_ge(o_split, L * 3 + b + 1)
                        for s in range(2):
                            w = parts("mix", 6 * half + 4 + s, L, b, 256)
                            for t in range(2):
                                m = tile_product("mix", f"b{half}_{2 * s + t}", t, L, b, w, t * P, o_m, 4)
                                if t == 0:
                                    m.then_inc(branch_even, 1)
                            m.then_inc(unit_used, 1)
                pe.wait_ge(m_split.sem, m_split.at(L, 1))
                pe.sem_inc(passed, 1)
                with pe.Fori(0, 2) as i:
                    products("out", "t", 0, L, i, h_b)
                sum_squares("norm2", L, hv, KC, sq_ready)
                pe.wait_ge(hf_split.sem, hf_split.at(L, 1))
                for g, (first, n) in enumerate(F_GROUPS):
                    pe.sem_inc(passed, 1)
                    with pe.Fori(0, n // 2) as i:
                        products(f"f1_{g}", "t", 0, L, i, h_f)
                    pe.wait_ge(act_ready, L * (FT // 2) + ((first + n) // 2))
                    pe.sem_inc(passed, 1)
                    with pe.Fori(0, 2) as i:
                        products(f"f2_{g}", "t", 0, L, i, act_f, n)
            sum_squares("norm1", DEPTH, hv, KC, sq_ready)


        @block.scalar
        def _(act):
            def drained(phase, name, layer, step=0, unit=None):
                ap, fl, fr, n = turn(phase, name, layer, step)
                if unit is None:
                    act.wait_ge(fl, n)
                else:
                    act.wait_ge(*unit_filled(phase, unit, layer, step))
                return ap, fr

            def read_tile(phase, name, t, layer, step, unit, dst_s, dst_p, func=ACT.Copy):
                _, fr_b = drained(phase, name + "_b", layer, step, unit)
                _, _, fr_a, _ = turn(phase, name + "_a", layer, step)
                nc.scalar.activation(dst_s, over_banks[t % 2][:, 0:NS], func).then_inc(fr_a, 1)
                nc.scalar.activation(dst_p, over_banks[t % 2][:, NS:NT], func).then_inc(fr_b, 1)

            def tiles(view, at, a, b):
                return view[:, bass.ds(at, 1), a:b].rearrange("p a t -> p (a t)")

            act.wait_ge(consts_in, 32)
            nc.scalar.activation(ident_r[:, :], cn("ident"), ACT.Copy)
            nc.scalar.activation(ones_r[:, :], cn("ones"), ACT.Copy)
            nc.scalar.activation(big_r[:, :], cn("big"), ACT.Copy)
            act.drain()
            nc.scalar.activation(cond[:, :], cn("cond"), ACT.Silu).then_inc(cond_ready, 1)

            def copy_rows(rows, ready):
                nc.scalar.activation(rows, bank["GP"][0:2, :], ACT.Copy).then_inc(freed["GP"], 1)
                act.drain().then_inc(ready, 1)

            with act.Fori(0, FIRST_MOD // 4) as i:
                act.wait_ge(unit_used, i * 4 + 4)
                copy_rows(mod_rows, rows_first)

            def squares(layer, base):
                for k in range(KC):
                    nc.scalar.activation(hv[:, k, :], xv[:, k, :], ACT.Square).then_inc(sq_ready.sem, 1)

            def rms_root(phase, layer, k):
                ap, fr = drained(phase, "ss_s", layer)
                nc.scalar.activation(rstd[:, 0:NS], ap, ACT.Sqrt, bias=epsc[:, 0:1], scale=1.0 / D).then_inc(fr, 1)
                ap, fr = drained(phase, "ss_p", layer)
                nc.scalar.activation(rstd[:, NS:NT], ap[:, 0:NP], ACT.Sqrt, bias=epsc[:, 0:1], scale=1.0 / D
                                     ).then_inc(fr, 1)
                act.drain().then_inc(rms_ready.sem, 1)

            def round_tiles(layer, src, acts, sem_, value0=None):
                for k in range(len(src)):
                    nc.scalar.activation(acts[0][k], src[k], ACT.Copy).then_inc(sem_, 1)

            htiles = [hv[:, k, :] for k in range(KC)]

            def shift(layer, k0, mod_at):
                for k in range(KC):
                    act.wait_ge(hnorm.sem, hnorm.at(layer, k0 + k + 1))
                    nc.scalar.activation(hv[:, k, 0:NS], hv[:, k, 0:NS], ACT.Identity,
                                         bias=modv[:, mod_at + k, 0:1])
                    nc.scalar.activation(hv[:, k, NS:NT], hv[:, k, NS:NT], ACT.Identity,
                                         bias=modv[:, mod_at + k, 1:2])
                act.drain()

            with act.Fori(0, DEPTH) as L:
                act.dma_start(par[:, :], PARAMS[bass.ds(L, 1)].rearrange("a p n -> p (a n)")).then_inc(par_in.sem, 16)
                squares(L, 0)
                rms_root("norm1", L, 1)
                shift(L, 0, 0)
                act.drain().then_inc(h_ready.sem, 1)
                round_tiles(L, htiles, h_a, hi_ready.sem)
                act.wait_ge(pads_zero.sem, pads_zero.at(L, 1))
                act.sem_inc(passed, 1)
                with act.Fori(0, 4) as i:
                    for t in range(4):
                        read_tile("A", f"t{t}", t, L, i, t, tiles(PA, i * 4 + t, 2, 514), tiles(PA, i * 4 + t, 516, 644))
                act.drain().then_inc(proj_a.sem, 1)
                ap, fl, fr, n = turn("ba", "ba", L)
                act.wait_ge(fl, n)
                bav = ap[:, 0:80].rearrange("p (c n) -> p c n", c=NCH)
                nc.scalar.activation(beta, bav[:, :, 0:8], ACT.Sigmoid)
                act.drain().then_inc(beta_done.sem, 1)
                act.wait_ge(ab_lin.sem, ab_lin.at(L, 1))
                nc.scalar.activation(tmpd, tmpc, ACT.Abs)
                act.drain()
                nc.scalar.activation(tmpd, tmpd, ACT.Exp, scale=-1.0)
                nc.scalar.activation(expa, pr("a_log"), ACT.Exp)
                act.drain()
                nc.scalar.activation(tmpd, tmpd, ACT.Ln, bias=1.0)
                act.drain().then_inc(sp_ready.sem, 1)
                act.wait_ge(cums.sem, cums.at(L, 1))
                nc.scalar.activation(egc, gcum, ACT.Exp)
                nc.scalar.activation(egl, egl, ACT.Exp)
                nc.scalar.activation(ekd, ekd, ACT.Exp)
                act.drain().then_inc(cumx.sem, 1)

                def silu(j, n):
                    act.wait_ge(conv_done.sem, conv_done.at(staging(L, n), j + 1))
                    nc.scalar.activation(ahead[:, j, :], ahead[:, j, :], ACT.Silu)
                    act.drain()
                    if j < 2:
                        nc.scalar.activation(sq[:, j, 0:NS], ahead[:, j, 0:NS], ACT.Square)
                        nc.scalar.activation(sq[:, j, NS:NT], ahead[:, j, NS + 2:CW], ACT.Square)
                    act.drain().then_inc(silu_done.sem, 1)

                def norms(j, reader):
                    ap, fr = reader(("ssq_q", "ssq_k", "ssq_p")[j])
                    if j < 2:
                        nc.scalar.activation(sq[:, j, 0:NS], ap, ACT.Sqrt, bias=epsc[:, 1 - j:2 - j],
                                             scale=float(P) if j == 0 else 1.0).then_inc(fr, 1)
                    else:
                        nc.scalar.activation(sq[:, 0, NS:NT], ap[:, 0:P], ACT.Sqrt, bias=epsc[:, 1:2], scale=float(P))
                        nc.scalar.activation(sq[:, 1, NS:NT], ap[:, P:2 * P], ACT.Sqrt, bias=epsc[:, 0:1]).then_inc(fr, 1)
                        act.drain().then_inc(rq_ready.sem, 1)

                for j in range(3):
                    silu(j, 0)
                for j in range(3):
                    norms(j, lambda name: drained("first", name, L))

                with act.Fori(0, H) as hd:
                    Q = L * H + hd

                    def f(name):
                        return drained("delta", name, L, hd)

                    for g, first, n in G3:
                        ap, fr = f(["R_f", "R_b", "R_p"][g])
                        for c in range(n):
                            d = g if g < 2 else c
                            ch = c if g < 2 else 4
                            m = nc.scalar.activation(DT[:, first + c, :], ap[:, c * P:(c + 1) * P], ACT.Exp,
                                                     bias=ngc[:, ch, bass.ds(hd + 4 * d, 1)])
                        m.then_inc(fr, 1)
                        act.drain().then_inc(decay.sem, 1)
                    zt = PA[:, bass.ds(hd + 12, 1), 0:PADW].rearrange("p a t -> p (a t)")
                    nc.scalar.activation(zt, zt, ACT.Silu)
                    act.drain().then_inc(siluz.sem, 1)
                    ap, fr = f("tok_k")
                    nc.scalar.activation(ktok[:, 0:4, :], ap.rearrange("p (a b) -> p a b", a=4), ACT.Copy).then_inc(fr, 1)
                    ap, fr = f("tok_v")
                    nc.scalar.activation(vtok[:, 0:4, :], ap.rearrange("p (a b) -> p a b", a=4), ACT.Copy).then_inc(fr, 1)
                    ap, fr = f("tok_p")
                    nc.scalar.activation(ktok[:, 4, :], ap[:, 0:P], ACT.Copy)
                    nc.scalar.activation(vtok[:, 4, :], ap[:, P:2 * P], ACT.Copy).then_inc(fr, 1)
                    act.drain().then_inc(tok_ready.sem, 1)
                    for g, first, n in G3:
                        ap, fr = f(f"X0_{GROUPS[g][0]}")
                        nc.scalar.activation(X_[:, first:first + n, :], ap[:, 0:n * P].rearrange("p (a b) -> p a b", a=n),
                                             ACT.Copy).then_inc(fr, 1)
                        act.drain().then_inc(x0_ready.sem, 1)
                    drained("delta", "rows0", L, hd, 3)
                    copy_rows(mod_rows, rows_delta.sem)
                    for lev in range(1, NLEV):
                        for g, first, n in G3:
                            ap, fr = f(f"P{lev}_{GROUPS[g][0]}")
                            nc.scalar.activation(PS[:, first:first + n, :],
                                                 ap[:, 0:n * P].rearrange("p (a b) -> p a b", a=n), ACT.Copy
                                                 ).then_inc(fr, 1)
                            act.drain().then_inc(p_ready.sem, 1)
                        if lev in (3, 5):
                            silu((lev - 3) // 2, hd + 1)
                    for d in range(2):
                        ap, fr = f(["vn_pf", "vn_pb"][d])
                        nc.scalar.activation(vn[:, 2 + d, :], ap[:, 0:P], ACT.Copy,
                                             scale=beta[:, 4, bass.ds(hd + 4 * d, 1)]).then_inc(fr, 1)
                        act.drain().then_inc(vn_ready.sem, 1)
                    for j in range(3):
                        norms(j, f)
                    for step in range(4):
                        for d in range(2):
                            c = step if d == 0 else 3 - step
                            ap, fr = f(f"vn{step}_{'fb'[d]}")
                            nc.scalar.activation(vn[:, d, :], ap[:, 0:P], ACT.Copy,
                                                 scale=beta[:, c, bass.ds(hd + 4 * d, 1)]).then_inc(fr, 1)
                            act.drain().then_inc(vn_ready.sem, 1)
                        if step == 0:
                            silu(2, hd + 1)
                        if step == 2:
                            drained("delta", "rows1", L, hd, 7)
                            copy_rows(mod_rows, rows_delta.sem)
                    act.wait_ge(osum.sem, osum.at(Q, 1))
                    for c in range(NCH):
                        nc.scalar.activation(osq_d, oacc[:, c, :], ACT.Square, accum_out=orn[:, c:c + 1])
                        act.drain()
                    act.drain()
                    nc.scalar.activation(orn, orn, ACT.Sqrt, bias=epsc[:, 0:1], scale=1.0 / P)
                    act.drain().then_inc(orms.sem, 1)

                act.wait_ge(state_stored.sem, state_stored.at(L, 16))
                act.wait_ge(head_done.sem, head_done.at(L, 0) * H + H)
                round_tiles(L, htiles, h_b, hi_ready.sem)
                act.sem_inc(passed, 1)
                with act.Fori(0, 2) as i:
                    for t in range(4):
                        read_tile("B", f"t{t}", t, L, i, t, tiles(PBq, i * 4 + t, 0, NS), tiles(PBq, i * 4 + t, NS, NT))
                for s in range(2):
                    for c in range(3):
                        ap, fr = drained("V", f"c{c}_{s}", L, 0, 2 * s + 1 if c == 2 else None)
                        n = 2 if c < 2 else 1
                        nc.scalar.activation(VB[:, 2 * c:2 * c + n, 2 * s * P:2 * (s + 1) * P],
                                             ap[:, 0:n * 2 * P].rearrange("p (a b) -> p a b", a=n), ACT.Copy).then_inc(fr, 1)
                act.wait_ge(lam_dot.sem, lam_dot.at(L, 1))
                nc.scalar.activation(lamc[:, 2:4], lamc[:, 0:2], ACT.Exp)
                act.drain().then_inc(proj_b.sem, 1)

                with act.Fori(0, H) as hd:
                    Q = L * H + hd

                    def f(name):
                        return drained("attn", name, L, hd)

                    def turned(qb):
                        ap, fr = f(f"T4_{qb}")
                        nc.scalar.activation(aT[:, 0:4, qb * P:(qb + 1) * P], ap.rearrange("p (a b) -> p a b", a=4),
                                             ACT.Copy).then_inc(fr, 1)
                        ap, fr = f(f"T1_{qb}")
                        nc.scalar.activation(aT[:, 4, qb * P:(qb + 1) * P], ap[:, 0:P], ACT.Copy).then_inc(fr, 1)
                        act.drain().then_inc(at_copied.sem, 2)

                    for qb in range(5):
                        for m_ in range(2):
                            act.wait_ge(neg_max.sem, neg_max.at(Q, 2 * qb + m_ + 1))
                            if qb < 4:
                                pair = (pair0, pair1, pair_g)[(2 * qb + m_) % 3]
                                ba, _ = TURNS.at("attn", f"S{m_}_{qb}a", L, hd)
                                bb, _ = TURNS.at("attn", f"S{m_}_{qb}b", L, hd)
                                nc.scalar.activation(pp[:, qb % 2, m_, :], pair[:, 0:NT], ACT.Exp,
                                                     bias=mx[:, qb % 2, m_:m_ + 1], scale=0.125,
                                                     accum_out=rsum[:, qb % 2, m_:m_ + 1]).then_inc(freed[ba], 1)
                                act.drain().then_inc(freed[bb], 1)
                            else:
                                ap, fr = f(f"S_p{m_}")
                                nc.scalar.activation(pp[:, 0, m_, 0:P], ap[:, 0:P], ACT.Exp,
                                                     bias=mx[:, 0, m_:m_ + 1], scale=0.125,
                                                     accum_out=rsum[:, 0, m_:m_ + 1]).then_inc(fr, 1)
                            act.drain().then_inc(exp_done.sem, 1)
                        if 1 <= qb <= 4:
                            turned(qb - 1)
                    ap, fr = f("T_p")
                    nc.scalar.activation(aTp, ap[:, 0:P], ACT.Copy)
                    nc.scalar.activation(knew[:, bass.ds(hd, 1), :].rearrange("p a t -> p (a t)"), ap[:, P:2 * P],
                                         ACT.Copy).then_inc(fr, 1)
                    act.drain().then_inc(at_copied.sem, 1)
                    drained("attn", "rows0", L, hd, 3)
                    copy_rows(mod_rows_b, rows_attn.sem)
                    ap, fr = f("o_s")
                    nc.scalar.activation(osb[:, 0:NS], ap, ACT.Copy).then_inc(fr, 1)
                    ap, fr = f("o_p")
                    nc.scalar.activation(osb[:, NS:NT], ap[:, 0:P], ACT.Copy).then_inc(fr, 1)
                    act.drain()
                    nc.scalar.activation(osq, osb, ACT.Square)
                    act.drain().then_inc(osq_done.sem, 1)
                    ap, fr = f("oss_s")
                    nc.scalar.activation(osq[:, 0:NS], ap, ACT.Sqrt, bias=epsc[:, 0:1], scale=1.0 / P).then_inc(fr, 1)
                    ap, fr = f("oss_p")
                    nc.scalar.activation(osq[:, NS:NT], ap[:, 0:P], ACT.Sqrt, bias=epsc[:, 0:1], scale=1.0 / P
                                         ).then_inc(fr, 1)
                    act.drain().then_inc(orms_b.sem, 1)

                act.drain()
                act.dma_start(KNEW[bass.ds(L, 1)].rearrange("a p n -> p (a n)"), big[:, 6528:6528 + H * P]
                              ).then_inc(cache_stored.sem, 16)
                act.dma_start(VNEW[bass.ds(L, 1)].rearrange("a p n -> p (a n)"), VB[:, 4, :]
                              ).then_inc(cache_stored.sem, 16)
                act.wait_ge(attn_done.sem, attn_done.at(L, 0) * H + H)
                act.wait_ge(cache_stored.sem, cache_stored.at(L, 32))
                act.dma_start(hyc, HYCS).then_inc(hyc_in.sem, 16)
                round_tiles(L, htiles, h_c, hi_ready.sem)
                act.wait_ge(pads_zero.sem, pads_zero.at(L, 2))
                act.sem_inc(passed, 1)
                with act.Fori(0, 3) as i:
                    for t in range(4):
                        read_tile("C", f"t{t}", t, L, i, t, tiles(PA, i * 4 + t, 2, 514), tiles(PA, i * 4 + t, 516, 644))
                        act.drain().then_inc(c_tile, 1)
                act.dma_start(fwd, FWD).then_inc(fwd_in.sem, 16)
                for j in range(2):
                    act.wait_ge(arg_ready.sem, arg_ready.at(L, j + 1))
                    nc.scalar.activation(hdn[0:64, :], arg[0:64, :], ACT.Sin)
                    act.drain().then_inc(sin_done.sem, 1)
                da, db = HYC["deltas"]
                na, _ = HYC["ndist"]
                for c in range(NCH):
                    if c:
                        act.wait_ge(filt_ready.sem, filt_ready.at(L, c))
                    nc.scalar.activation(dec, hyc[:, da:db], ACT.Exp, scale=hyc[:, na + c:na + c + 1])
                    act.drain().then_inc(dec_ready.sem, 1)
                for c in range(NCH):
                    act.wait_ge(filt_ready.sem, filt_ready.at(L, c + 1))
                    nc.scalar.activation(ABSH[c], tok[:, c, :], ACT.Abs)
                    act.drain().then_inc(abs_ready.sem, 1)
                ap, fl, fr, n = turn("hyfil", "norm", L)
                act.wait_ge(fl, n)
                for i in range(8):
                    ap, fr = drained("hyfil", f"H{i}", L)
                    rows = P if i < 6 else FQ_P
                    nc.scalar.activation(Hs[0:rows, i, :], ap[0:rows, :], ACT.Copy).then_inc(fr, 1)
                    act.drain().then_inc(spec_ready.sem, 1)
                for j in range(4):
                    ap, fr = drained("hytr", f"g_s{j}", L)
                    nc.scalar.activation(tok[:, 0:4, j * P:(j + 1) * P], ap.rearrange("p (a b) -> p a b", a=4), ACT.Copy
                                         ).then_inc(fr, 1)
                    ap, fr = drained("hytr", f"g_p{j}", L)
                    nc.scalar.activation(tok[:, 4, j * P:(j + 1) * P], ap[:, 0:P], ACT.Copy).then_inc(fr, 1)
                    act.drain().then_inc(gvtok.sem, 1)
                act.wait_ge(gv_ready.sem, gv_ready.at(L, 4))
                act.dma_start(inv, INV).then_inc(inv_in.sem, 16)

                act.wait_ge(hy_done.sem, hy_done.at(L, 1))
                round_tiles(L, htiles, h_b, hi_ready.sem)
                act.sem_inc(passed, 1)
                with act.Fori(0, 3) as b:
                    act.wait_ge(merge, (L * 3 + b) * 4 + 2)
                    act.wait_ge(unit_used, unit_no("mix", 0, L, b))
                    for k in range(4):
                        nc.scalar.activation(o_m[0][k], ov[:, bass.ds(b * 4 + k, 1), :].rearrange("p a t -> p (a t)"),
                                             ACT.Copy).then_inc(om_hi, 1)
                    for half in range(2):
                        B = (L * 3 + b) * 2 + half
                        for t in range(4):
                            if t == 0:
                                act.wait_ge(merge, B * 2 + 2)
                                act.sem_inc(passed, 1)
                            read_tile("mix", f"g{half}_{t}", t, L, b, 6 * half + t, sig[:, t, 0:NS], sig[:, t, NS:NT],
                                      ACT.Sigmoid)
                        act.drain().then_inc(gates, 1)
                act.wait_ge(merged_ready.sem, merged_ready.at(L, 1))
                round_tiles(L, htiles, h_b, mg_hi.sem)
                act.wait_ge(xres1.sem, xres1.at(L, 1))
                squares(L, KC)
                rms_root("norm2", L, 2)
                shift(L, KC, 24)
                act.drain().then_inc(h_ready.sem, 1)
                round_tiles(L, htiles, h_f, hf_hi.sem)
                for g, (first, n) in enumerate(F_GROUPS):
                    act.sem_inc(passed, 1)
                    with act.Fori(0, n // 2) as i:
                        I = L * (FT // 2) + i + first // 2
                        act.wait_ge(act_room, I + 1)
                        act.sem_inc(passed, 1)
                        for t in range(2):
                            read_tile(f"f1_{g}", f"t{t}", t, L, i, t, gsil[:, t, 0:NS], gsil[:, t, NS:NT], ACT.Silu)
                        act.drain().then_inc(gate_silu, 1)
                        act.wait_ge(act_lin, I + 1)
                        nc.scalar.activation(room_a[:, bass.ds(i * 2 * NT, 2 * NT)].rearrange("p (a t) -> p a t", a=2),
                                             gsil, ACT.Copy)
                        act.drain().then_inc(act_hi, 1)
                act.wait_ge(layer_done.sem, layer_done.at(L, 1))
            squares(DEPTH, 0)
            rms_root("norm1", DEPTH, 1)

        @block.vector
        def _(dve):
            def drained(phase, name, layer, step=0, unit=None):
                ap, fl, fr, n = turn(phase, name, layer, step)
                if unit is None:
                    dve.wait_ge(fl, n)
                else:
                    dve.wait_ge(*unit_filled(phase, unit, layer, step))
                return ap, fr

            def low_tiles(src, acts, sem_, value, done):
                for k in range(len(src)):
                    dve.wait_ge(sem_, value + k)
                    tt(acts[1][k], src[k], acts[0][k].bitcast(F32), ALU.subtract)
                dve.drain().then_inc(done, 1)

            htiles = [hv[:, k, :] for k in range(KC)]

            def add_bias(turned, tile, bias):
                dve.wait_ge(mod_turned, turned)
                dve.sem_inc(passed, 1)
                tt(modv[:, bass.ds(tile, 4), :], bank["GP"][:, 0:8].rearrange("p (a b) -> p a b", a=4),
                   bias.unsqueeze(2).to_broadcast([P, 4, 2]), ALU.add).then_inc(freed["GP"], 1)

            def tile_product(phase, name, t, layer, step, unit, combine):
                _, _, fr_b, _ = turn(phase, name + "_b", layer, step)
                _, _, fr_a, _ = turn(phase, name + "_a", layer, step)
                if unit is not None:
                    dve.wait_ge(*unit_filled(phase, unit, layer, step))
                combine(over_banks[t % 2][:, 0:NS], 0, NS, 0).then_inc(fr_a, 1)
                combine(over_banks[t % 2][:, NS:NT], NS, NT, 1).then_inc(fr_b, 1)

            tt, ts, stt = nc.vector.tensor_tensor, nc.vector.tensor_scalar, nc.vector.scalar_tensor_tensor

            def inverse_rms(k, value):
                dve.wait_ge(rms_ready.sem, value)
                nc.vector.reciprocal(rstd, rstd)
                dve.drain()

            dve.memset(epsc[:, 0:1], EPS)
            dve.memset(epsc[:, 1:2], P * EPS)
            for b in BANKS:
                dve.sem_inc(freed[b], 1)
            dve.sem_inc(merge, 2)
            dve.sem_inc(act_room, 1)
            dve.sem_inc(attn_room, 1)
            dve.sem_inc(inverse_done, 1)
            dve.drain()
            dve.wait_ge(consts_in, 32)
            first_groups, groups = FIRST_MOD // 4, 3 * H
            with dve.Fori(0, first_groups) as i:
                add_bias(i + 1, i * 4, cn("b_first")[:, bass.ds(i * 4, 4)])
            dve.drain()
            with dve.Fori(0, DEPTH) as L:
                for v in pads:
                    dve.memset(v, 0.0)
                dve.drain().then_inc(pads_zero.sem, 1)
                dve.wait_ge(par_in.sem, par_in.at(L, 16))

                def gains(i, at, g):
                    stt(gainv[:, i, :, :], modv[:, at:at + KC, :], 1.0,
                        pr(g).unsqueeze(2).to_broadcast([P, KC, 2]), ALU.add, ALU.mult)
                    dve.drain()

                gains(0, 8, "g1")

                def scale(i, layer, value):
                    inverse_rms(i, value)
                    for k in range(KC):
                        for q, (a, b) in enumerate(((0, NS), (NS, NT))):
                            stt(hv[:, k, a:b], xv[:, k, a:b], gainv[:, i, k, q:q + 1], rstd[:, a:b], ALU.mult, ALU.mult)
                        dve.drain().then_inc(hnorm.sem, 1)

                scale(0, L, rms_ready.at(L, 1))
                dve.wait_ge(h_ready.sem, h_ready.at(L, 1))
                low_tiles(htiles, h_a, hi_ready.sem, hi_ready.at(L, 1), h_split.sem)

                lv = pr("lam").rearrange("p (i n) -> p i n", i=4)
                for i in range(2):
                    tt(cut(sc, 3840 + 64 * i, 64), lv[:, 2 * i, :], lv[:, 2 * i + 1, :], ALU.mult)
                dve.drain()
                nc.vector.tensor_reduce(lamc[:, 0:2], cut(sc, 3840, 2, 64), AX_X, ALU.add)
                ts(subg, pr("sub_g"), pr("one_minus_lam"), None, ALU.mult)
                dve.drain().then_inc(lam_dot.sem, 1)

                ap, fl, fr, n = turn("ba", "ba", L)
                dve.wait_ge(proj_a.sem, proj_a.at(L, 1))
                dve.wait_ge(fl, n)
                dve.wait_ge(beta_done.sem, beta_done.at(L, 1))
                bav = ap[:, 0:80].rearrange("p (c n) -> p c n", c=NCH)
                tt(tmpc, bav[:, :, 8:16], pr("dt_bias").unsqueeze(1).to_broadcast([P, NCH, 8]), ALU.add)
                dve.drain().then_inc(ab_lin.sem, 1)
                dve.wait_ge(sp_ready.sem, sp_ready.at(L, 1))
                ts(gg, tmpc, 0.0, None, ALU.max).then_inc(fr, 1)
                dve.drain()
                tt(gg, gg, tmpd, ALU.add)
                dve.drain()
                stt(gg, gg, -1.0, expa.unsqueeze(1).to_broadcast([P, NCH, 8]), ALU.mult, ALU.mult)
                dve.drain().then_inc(g_ready.sem, 1)
                ap, fr = drained("ba", "cum", L)
                cumv = ap[:, 0:120].rearrange("p (w c n) -> p w c n", w=3, c=NCH)
                for d in range(2):
                    nc.vector.tensor_copy(gcum[:, :, 4 * d:4 * d + 4], cumv[:, d, :, 4 * d:4 * d + 4])
                nc.vector.tensor_copy(egl, cumv[:, 2, :, :]).then_inc(fr, 1)
                dve.drain()
                ts(ngc, gcum, -1.0, None, ALU.mult)
                tt(ekd, egl, gcum, ALU.subtract)
                dve.drain().then_inc(cums.sem, 1)
                dve.wait_ge(cumx.sem, cumx.at(L, 1))
                ts(negc, egc, -1.0, None, ALU.mult)
                dve.drain()

                cw = pr("conv").rearrange("p (i d) -> p i d", d=5)

                def convolve(j, d, n):
                    src = PA[:, bass.ds(n + 4 * j, 1), 0:PADW].rearrange("p a t -> p (a t)")
                    tap = cw[:, bass.ds(n + 4 * j, 1), d]
                    if d == 0:
                        ts(ahead[:, j, :], src[:, 0:CW], tap, None, ALU.mult)
                    else:
                        stt(ahead[:, j, :], src[:, d:d + CW], tap, ahead[:, j, :], ALU.mult, ALU.add)
                    if d == 4:
                        dve.drain().then_inc(conv_done.sem, 1)
                    else:
                        dve.drain()

                for j in range(3):
                    for d in range(5):
                        convolve(j, d, 0)
                dve.wait_ge(rq_ready.sem, rq_ready.at(staging(L, 0), 1))
                nc.vector.reciprocal(sq, sq)
                dve.drain()

                with dve.Fori(0, H) as hd:
                    Q = L * H + hd

                    def f(name):
                        return drained("delta", name, L, hd)

                    for j in range(2):
                        tt(cv[:, j, 0:NS], ahead[:, j, 0:NS], sq[:, j, 0:NS], ALU.mult)
                        tt(cv[:, j, NS + 2:CW], ahead[:, j, NS + 2:CW], sq[:, j, NS:NT], ALU.mult)
                    dve.drain().then_inc(qk_ready.sem, 1)
                    kk, frk = f("KK_s")
                    qq, frq = f("QK_s")
                    kp, frp = f("KQ_p")

                    def interaction(g, first, n):
                        dve.wait_ge(decay.sem, decay.at(Q, g + 1))
                        for c in range(n):
                            src = kk[:, c * P:(c + 1) * P] if g < 2 else kp[:, 0:P]
                            d = g if g < 2 else c
                            ch = c if g < 2 else 4
                            stt(AT[:, first + c, :], src, beta[:, ch, bass.ds(hd + 4 * d, 1)], DT[:, first + c, :],
                                ALU.mult, ALU.mult)
                        dve.drain().then_inc(at_ready.sem, 1)

                    def query_decay(g, first, n):
                        for c in range(n) if g == 2 else range(1):
                            a, b = (first + c, first + c + 1) if g == 2 else (first, first + n)
                            src = (kp[:, P:2 * P].rearrange("p (a b) -> p a b", a=1) if g == 2
                                   else qq.rearrange("p (a b) -> p a b", a=4))
                            m = tt(DT[:, a:b, :], src, DT[:, a:b, :], ALU.mult)
                        return m

                    for g, first, n in G3:
                        interaction(g, first, n)
                    dve.drain().then_inc(frk, 1)
                    for g, first, n in G3:
                        dve.wait_ge(al_ready.sem, al_ready.at(Q, g + 1))
                        stt(XT[:, first:first + n, :], AL[:, first:first + n, :], -1.0, repeated(ident, n), ALU.mult, ALU.add)
                        dve.drain().then_inc(xt_ready.sem, 1)
                    query_decay(0, 0, 4)
                    query_decay(1, 4, 4).then_inc(frq, 1)
                    query_decay(2, 8, 2).then_inc(frp, 1)
                    dve.drain().then_inc(qkd_ready.sem, 1)
                    for lev in range(1, NLEV):
                        for g, first, n in G3:
                            m3 = slice(first, first + n)
                            if lev < NLEV - 1:
                                ap, fr = f(f"D{lev}_{GROUPS[g][0]}")
                                if lev == 1:
                                    dve.wait_ge(x0_ready.sem, x0_ready.at(Q, g + 1))
                                tt(X_[:, m3, :], X_[:, m3, :], ap[:, 0:n * P].rearrange("p (a b) -> p a b", a=n),
                                   ALU.subtract).then_inc(fr, 1)
                                dve.drain().then_inc(x_ready.sem, 1)
                            ap, fr = f(f"E{lev}_{GROUPS[g][0]}")
                            tt(XT[:, m3, :], XT[:, m3, :], ap[:, 0:n * P].rearrange("p (a b) -> p a b", a=n),
                               ALU.subtract).then_inc(fr, 1)
                            dve.drain().then_inc(xt_ready.sem, 1)
                            slot = 3 * (lev - 1) + g
                            if slot == 0:
                                dve.wait_ge(tok_ready.sem, tok_ready.at(Q, 1))
                            if slot < 15:
                                convolve(slot // 5, slot % 5, hd + 1)
                    dve.drain().then_inc(inverse_done, 1)
                    sv = pr("state").rearrange("p (i n) -> p i n", i=8)
                    for d in range(2):
                        nc.vector.tensor_copy(S[:, d, :], sv[:, bass.ds(hd + 4 * d, 1), :].rearrange("p a n -> p (a n)"))
                    dve.drain().then_inc(s_ready.sem, 1)
                    dve.wait_ge(tok_ready.sem, tok_ready.at(Q, 1))
                    add_bias(L * groups + hd * 2 + (first_groups + 1), hd * 8 + 16, pr("b_mod")[:, bass.ds(hd * 8 + 16, 4)])
                    ap, fr = f("o_p")
                    nc.vector.tensor_copy(oacc[:, 4, :], ap[:, 0:P])
                    for d in range(2):
                        m = nc.vector.tensor_copy(snew[:, bass.ds(hd + 4 * d, 1), :].rearrange("p a n -> p (a n)"),
                                                  ap[:, (1 + d) * P:(2 + d) * P])
                    m.then_inc(fr, 1)
                    for step in range(4):
                        for d in range(2):
                            c = step if d == 0 else 3 - step
                            cd = bass.ds(hd + 4 * d, 1)
                            ap, fr = f(f"kq{step}_{'fb'[d]}")
                            stt(rr[:, d, :], ap[:, 0:P], negc[:, c, cd], vtok[:, c, :], ALU.mult, ALU.add)
                            dve.drain().then_inc(r_ready.sem, 1)
                            if step < 2:
                                ts(t1[:, d, :], ap[:, P:2 * P], egc[:, c, cd], None, ALU.mult).then_inc(fr, 1)
                            else:
                                stt(t1[:, d, :], ap[:, P:2 * P], egc[:, c, cd], oacc[:, c, :], ALU.mult, ALU.add
                                    ).then_inc(fr, 1)
                        dve.drain()
                        for d in range(2):
                            c = step if d == 0 else 3 - step
                            cd = bass.ds(hd + 4 * d, 1)
                            ap, fr = f(f"o{step}_{'fb'[d]}")
                            if step < 3:
                                stt(S[:, d, :], S[:, d, :], egl[:, c, cd], ap[:, P:2 * P], ALU.mult, ALU.add)
                                dve.drain().then_inc(s_ready.sem, 1)
                            tt(oacc[:, c, :], t1[:, d, :], ap[:, 0:P], ALU.add).then_inc(fr, 1)
                        if step == 0:
                            dve.wait_ge(rq_ready.sem, rq_ready.at(staging(L, hd + 1), 1))
                        quarter = cut(sc, 1926 + step * (NT // 2), NT // 2)
                        nc.vector.reciprocal(quarter, quarter)
                        dve.drain()
                    dve.drain().then_inc(osum.sem, 1)
                    add_bias(L * groups + hd * 2 + (first_groups + 2), hd * 8 + 20, pr("b_mod")[:, bass.ds(hd * 8 + 20, 4)])
                    dve.wait_ge(orms.sem, orms.at(Q, 1))
                    nc.vector.reciprocal(orn, orn)
                    dve.drain()
                    for c in range(NCH):
                        ts(oacc[:, c, :], oacc[:, c, :], orn[:, c:c + 1], None, ALU.mult)
                    dve.drain().then_inc(oscaled.sem, 1)
                    dve.wait_ge(siluz.sem, siluz.at(Q, 1))
                    zt = PA[:, bass.ds(hd + 12, 1), 0:PADW].rearrange("p a t -> p (a t)")
                    ot = ov[:, bass.ds(hd, 1), :].rearrange("p a t -> p (a t)")
                    ap, fr = f("oT_s")
                    stt(ot[:, 0:NS], ap, pr("dn_g"), zt[:, 2:514], ALU.mult, ALU.mult).then_inc(fr, 1)
                    ap, fr = f("oT_p")
                    stt(ot[:, NS:NT], ap[:, 0:P], pr("dn_g"), zt[:, 516:644], ALU.mult, ALU.mult).then_inc(fr, 1)
                    dve.drain().then_inc(head_done.sem, 1)

                low_tiles(htiles, h_b, hi_ready.sem, hi_ready.at(L, KC + 1), h_split.sem)
                dve.wait_ge(proj_b.sem, proj_b.at(L, 1))
                tt(lamc[:, 4:5], lamc[:, 3:4], lamc[:, 2:3], ALU.subtract)
                dve.drain()
                tt(lamc[:, 5:6], lamc[:, 4:5], pr("lam_init"), ALU.subtract)
                dve.drain()

                with dve.Fori(0, H) as hd:
                    Q = L * H + hd

                    def f(name):
                        return drained("attn", name, L, hd)

                    dve.wait_ge(rope_in.sem, rope_in.at(L, 16))
                    ca, cb = ROPE["cos"]
                    sa, sb_ = ROPE["sin"]
                    for j, (name, dst) in enumerate((("rot_q", qall), ("rot_k", kall))):
                        src = PBq[:, bass.ds(hd + 4 * j, 1), 0:NS].rearrange("p a t -> p (a t)")
                        tt(dst[:, 0:NS], src, rope[:, ca:cb], ALU.mult)
                        ap, fr = f(name)
                        tt(rtmp, ap, rope[:, sa:sb_], ALU.mult).then_inc(fr, 1)
                        dve.drain()
                        tt(dst[:, 0:NS], dst[:, 0:NS], rtmp, ALU.add)
                        dve.drain().then_inc(rot_done.sem, 1)

                    def maxima(qb):
                        for m_ in range(2):
                            if qb < 4:
                                for part in "ab":
                                    b, n = TURNS.at("attn", f"S{m_}_{qb}{part}", L, hd)
                                    dve.wait_ge(filled[b], n)
                                src = (pair0, pair1, pair_g)[(2 * qb + m_) % 3][:, 0:NT]
                            else:
                                b, n = TURNS.at("attn", f"S_p{m_}", L, hd)
                                dve.wait_ge(filled[b], n)
                                src = bank[b][:, 0:P]
                            q = qb % 2
                            nc.vector.reduce_max(mx[:, q, m_:m_ + 1], src, AX_X)
                            dve.drain()
                            ts(mx[:, q, m_:m_ + 1], mx[:, q, m_:m_ + 1], -0.125, None, ALU.mult)
                            dve.drain().then_inc(neg_max.sem, 1)

                    def combine(qb):
                        q = qb % 2
                        w_ = NT if qb < 4 else P
                        dve.wait_ge(exp_done.sem, exp_done.at(Q, 2 * qb + 2))
                        if qb >= 2:
                            dve.wait_ge(at_copied.sem, at_copied.at(Q, 2 * (qb - 2) + 2))
                        nc.vector.reciprocal(rinv[:, q, :], rsum[:, q, :])
                        dve.drain()
                        ts(rinv[:, q, 1:2], rinv[:, q, 1:2], lamc[:, 5:6], None, ALU.mult)
                        ts(aa[:, q, 0:w_], pp[:, q, 0, 0:w_], rinv[:, q, 0:1], None, ALU.mult)
                        dve.drain()
                        stt(aa[:, q, 0:w_], pp[:, q, 1, 0:w_], rinv[:, q, 1:2], aa[:, q, 0:w_], ALU.mult, ALU.add)
                        dve.drain().then_inc(a_ready.sem, 1)

                    maxima(0)
                    for qb in range(1, 5):
                        maxima(qb)
                        combine(qb - 1)
                    combine(4)
                    add_bias(L * groups + hd + (first_groups + 2 * H + 1), hd * 4, pr("b_next")[:, bass.ds(hd * 4, 4)])
                    dve.wait_ge(orms_b.sem, orms_b.at(Q, 1))
                    nc.vector.reciprocal(osq, osq)
                    dve.drain()
                    stt(ov[:, bass.ds(hd + 4, 1), :].rearrange("p a t -> p (a t)"), osb, subg, osq, ALU.mult, ALU.mult)
                    dve.drain().then_inc(attn_done.sem, 1)
                    dve.drain().then_inc(attn_room, 1)

                low_tiles(htiles, h_c, hi_ready.sem, hi_ready.at(L, 2 * KC + 1), h_split.sem)
                dve.wait_ge(cache_stored.sem, cache_stored.at(L, 32))
                for v in pads:
                    dve.memset(v[:, 0:12, :], 0.0)
                dve.drain().then_inc(pads_zero.sem, 1)
                hw = pr("hconv").rearrange("p (i d) -> p i d", d=3)
                with dve.Fori(0, 3) as i:
                    for t in range(4):
                        dve.wait_ge(c_tile, L * 12 + i * 4 + (t + 1))
                        dve.sem_inc(passed, 1)
                        src = PA[:, bass.ds(i * 4 + t, 1), 0:PADW].rearrange("p a t -> p (a t)")
                        tap = [hw[:, bass.ds(i * 4 + t, 1), d] for d in range(3)]
                        ts(ctmp, src[:, 1:1 + CW], tap[0], pr("hconv_b")[:, bass.ds(i * 4 + t, 1)], ALU.mult, ALU.add)
                        dve.drain()
                        stt(ctmp, src[:, 2:2 + CW], tap[1], ctmp, ALU.mult, ALU.add)
                        dve.drain()
                        stt(src[:, 3:3 + CW], src[:, 3:3 + CW], tap[2], ctmp, ALU.mult, ALU.add)
                        dve.drain()
                for j, (ns_, np_, b_) in enumerate((("h1_s", "h1_p", "hy_b1"), ("h2_s", "h2_p", "hy_b2"))):
                    ap, fr = drained("hyfil", ns_, L)
                    ts(arg[0:64, 0:NS], ap[0:64, :], pr(b_, 64), pr("hy_fr", 64), ALU.add, ALU.mult).then_inc(fr, 1)
                    ap, fr = drained("hyfil", np_, L)
                    ts(arg[0:64, NS:NT], ap[0:64, 0:NP], pr(b_, 64), pr("hy_fr", 64), ALU.add, ALU.mult).then_inc(fr, 1)
                    dve.drain()
                    ts(redu[0:64, :], arg[0:64, :], 1.0 / TWO_PI, ROUND, ALU.mult, ALU.add)
                    dve.drain()
                    ts(redu[0:64, :], redu[0:64, :], -ROUND, None, ALU.add)
                    dve.drain()
                    for part in TWO_PI_PARTS:
                        stt(arg[0:64, :], redu[0:64, :], -part, arg[0:64, :], ALU.mult, ALU.add)
                        dve.drain()
                    ts(arg[0:64, :], arg[0:64, :], PI_BELOW, -PI_BELOW, ALU.min, ALU.max)
                    dve.drain().then_inc(arg_ready.sem, 1)
                for c in range(NCH):
                    ap, fr = drained("hyfil", f"h3_{c}", L)
                    dve.wait_ge(dec_ready.sem, dec_ready.at(L, c + 1))
                    tt(tok[:, c, :], ap, dec, ALU.mult).then_inc(fr, 1)
                    dve.drain().then_inc(filt_ready.sem, 1)
                ap, fr = drained("hyfil", "norm", L)
                nc.vector.reciprocal(hyn, ap[:, 0:8].rearrange("p (a b) -> p a b", a=2)).then_inc(fr, 1)
                dve.drain()
                for q, length in ((0, L_S), (1, L_P)):
                    ts(hyn[:, q, :], hyn[:, q, :], 2.0 / length, None, ALU.mult)
                dve.drain()
                for j in range(4):
                    for a, z, at in ((0, NS, 3), (NS, NT, 5)):
                        tt(ov[:, 8 + j, a:z], PA[:, 4 + j, a + at:z + at], PA[:, 8 + j, a + at:z + at], ALU.mult)
                    dve.drain().then_inc(gv_ready.sem, 1)
                for i in range(4):
                    rows = P if i < 3 else FQ_P
                    ic, is_ = (i, 3 + i) if i < 3 else (6, 7)
                    xc, frc = drained("hydft", f"X{ic}", L)
                    xs, frs = drained("hydft", f"X{is_}", L)
                    hc, hs = Hs[0:rows, ic, :], Hs[0:rows, is_, :]
                    yc, ys = (Ys[:, i, :], Ys[:, 3 + i, :]) if i < 3 else (Yp[0:rows, 0, :], Yp[0:rows, 1, :])
                    u = cut(big, 4 * PADW + N_INV + 1024, 512)[0:rows, :]
                    u2 = cut(sc, 3072, 512)[0:rows, :]
                    tt(yc, xc[0:rows, :], hc, ALU.mult)
                    tt(u, xs[0:rows, :], hs, ALU.mult)
                    tt(ys, xc[0:rows, :], hs, ALU.mult).then_inc(frc, 1)
                    tt(u2, xs[0:rows, :], hc, ALU.mult).then_inc(frs, 1)
                    dve.drain()
                    tt(yc, yc, u, ALU.subtract)
                    tt(ys, ys, u2, ALU.add)
                    dve.drain().then_inc(xprod.sem, 1)
                for j in range(4):
                    ts(ov[:, 8 + j, :], ov[:, 8 + j, :], pr("hy_d")[:, j:j + 1], None, ALU.mult)
                dve.drain()
                for j in range(4):
                    ap, fr = drained("hydft", f"y_s{j}", L)
                    g_ = ov[:, 8 + j, 0:NS]
                    stt(g_, ap, hyn[:, 0, j:j + 1], g_, ALU.mult, ALU.add).then_inc(fr, 1)
                    dve.drain()
                    tt(g_, g_, PA[:, j, 3:3 + NS], ALU.mult)
                ap, fr = drained("hydft", "y_p", L)
                for j in range(4):
                    g_ = ov[:, 8 + j, NS:NT]
                    m = stt(g_, ap[:, j * P:(j + 1) * P], hyn[:, 1, j:j + 1], g_, ALU.mult, ALU.add)
                m.then_inc(fr, 1)
                dve.drain()
                for j in range(4):
                    tt(ov[:, 8 + j, NS:NT], ov[:, 8 + j, NS:NT], PA[:, j, 5 + NS:5 + NT], ALU.mult)
                dve.drain().then_inc(hy_done.sem, 1)
                low_tiles(htiles, h_b, hi_ready.sem, hi_ready.at(L, 3 * KC + 1), h_split.sem)
                dve.memset(merged, 0.0)
                dve.drain()
                gains(1, 32, "g2")

                with dve.Fori(0, 3) as b:
                    for k in range(4):
                        dve.wait_ge(om_hi, (L * 3 + b) * 4 + k + 1)
                        tt(o_m[1][k], ov[:, bass.ds(b * 4 + k, 1), :].rearrange("p a t -> p (a t)"),
                           o_m[0][k].bitcast(F32), ALU.subtract)
                    dve.drain().then_inc(o_split, 1)
                    for half in range(2):
                        B = (L * 3 + b) * 2 + half
                        dve.wait_ge(gates, B + 1)
                        for s in range(2):
                            t0 = 4 * half + 2 * s
                            for t in range(2):
                                def gated(ap, a, z, q):
                                    return tt(mtmp[:, t, a:z], ap, sig[:, 2 * s + t, a:z], ALU.mult)
                                if t == 0:
                                    dve.wait_ge(branch_even, (L * 3 + b) * 4 + (2 * half + s + 1))
                                tile_product("mix", f"b{half}_{2 * s + t}", t, L, b, 6 * half + 4 + s if t else None, gated)
                            dve.drain()
                            tt(merged[:, t0:t0 + 2, :], merged[:, t0:t0 + 2, :], mtmp, ALU.add)
                            dve.drain().then_inc(merge, 1)
                dve.drain().then_inc(merged_ready.sem, 1)
                low_tiles(htiles, h_b, mg_hi.sem, mg_hi.at(L, 1), m_split.sem)

                def residual(phase, step, mod_at):
                    for t in range(4):
                        def add(ap, a, z, q):
                            xt = xv[:, bass.ds(step * 4 + t, 1), a:z].rearrange("p a t -> p (a t)")
                            gc = modv[:, bass.ds(step * 4 + (mod_at + t), 1), q]
                            return stt(xt, ap, gc, xt, ALU.mult, ALU.add)
                        tile_product(phase, f"t{t}", t, L, step, t, add)

                with dve.Fori(0, 2) as i:
                    residual("out", i, 16)
                dve.drain().then_inc(xres1.sem, 1)
                scale(1, L, rms_ready.at(L, 2))
                dve.wait_ge(h_ready.sem, h_ready.at(L, 2))
                low_tiles(htiles, h_f, hf_hi.sem, hf_hi.at(L, 1), hf_split.sem)
                for g, (first, n) in enumerate(F_GROUPS):
                    dve.sem_inc(passed, 1)
                    with dve.Fori(0, n // 2) as i:
                        I = L * (FT // 2) + i + first // 2
                        dve.wait_ge(gate_silu, I + 1)
                        for t in range(2):
                            def gated(ap, a, z, q):
                                return tt(gsil[:, t, a:z], ap, gsil[:, t, a:z], ALU.mult)
                            tile_product(f"f1_{g}", f"t{2 + t}", t, L, i, 2 + t, gated)
                        dve.drain().then_inc(act_lin, 1)
                        dve.wait_ge(act_hi, I + 1)
                        hi = room_a[:, bass.ds(i * 2 * NT, 2 * NT)].rearrange("p (a t) -> p a t", a=2)
                        lo = room_a[:, bass.ds(i * 2 * NT + 8 * NT, 2 * NT)].rearrange("p (a t) -> p a t", a=2)
                        tt(lo, gsil, hi.bitcast(F32), ALU.subtract)
                        dve.drain().then_inc(act_ready, 1)
                        dve.sem_inc(act_room, 1)
                    with dve.Fori(0, 2) as i:
                        residual(f"f2_{g}", i, 40)
                    dve.drain()
                dve.drain().then_inc(layer_done.sem, 1)
            inverse_rms(0, rms_ready.at(DEPTH, 1))
            for q, (a, b) in enumerate(((0, NS), (NS, NT))):
                for k in range(KC):
                    stt(hv[:, k, a:b], xv[:, k, a:b], cn("final_g")[:, k:k + 1], rstd[:, a:b], ALU.mult, ALU.mult)
                dve.drain().then_inc(y_ready, 1)

        @block.gpsimd
        def _(pool):
            def split(phase, units, layer, step=0):
                kinds = PHASE_AT[phase][2]
                for k in units:
                    q = kinds[:k].count("w")
                    base = FIRST_MOD + PHASE_AT[phase][0] + k
                    slot, to = base % RAW, (PHASE_AT[phase][1] + q) % HI
                    pool.wait_ge(landed[slot], 16 * (layer * (UNITS // RAW) + step * (len(kinds) // RAW) + (base // RAW + 1)))
                    pool.wait_ge(unit_used, layer * UNITS + step * len(kinds) + (base - 1))
                    pool.sem_inc(passed, 1)
                    hi = whi[:, to * UNIT:(to + 1) * UNIT]
                    raw = ring[:, slot * UNIT:(slot + 1) * UNIT]
                    nc.gpsimd.tensor_copy(hi, raw)
                    pool.drain()
                    nc.gpsimd.tensor_tensor(wlo[:, slot * UNIT:(slot + 1) * UNIT], raw, hi.bitcast(F32), ALU.subtract)
                    pool.drain().then_inc(unit_split, 1)

            def split_phase(phase, times, layer):
                kinds = PHASE_AT[phase][2]
                units = [k for k in range(len(kinds)) if kinds[k] == "w"]
                with pool.Fori(0, times) as i:
                    split(phase, units, layer, i)

            with pool.Fori(0, DEPTH) as L:
                split_phase("A", 4, L)
                pool.wait_ge(g_ready.sem, g_ready.at(L, 1))
                pool.wait_ge(cumx.sem, cumx.at(L, 1))
                pool.sem_inc(passed, 1)
                with pool.Fori(0, H) as hd:
                    Q = L * H + hd
                    pool.wait_ge(inverse_done, Q + 1)
                    pool.sem_inc(passed, 1)

                    def head_columns(src):
                        return src.rearrange("p c (d h) -> p c d h", d=2)[:, :, :, bass.ds(hd, 1)].rearrange(
                            "p c d a -> p c (d a)")
                    nc.gpsimd.tensor_copy(gh, head_columns(gg))
                    nc.gpsimd.tensor_copy(eh, head_columns(ekd))
                    pool.drain()
                    nc.gpsimd.tensor_copy(ghh, gh)
                    pool.drain()
                    nc.gpsimd.tensor_tensor(gh_lo, gh, ghh.bitcast(F32), ALU.subtract)
                    pool.drain()
                    for part, gu in ((ghh.bitcast(F32), gu_hi), (gh_lo, gu_lo)):
                        for g, first, n in G3:
                            for c in range(n):
                                d = g if g < 2 else c
                                ch = c if g < 2 else 4
                                nc.gpsimd.tensor_scalar(gu[:, (first + c) * P:(first + c + 1) * P], tri[:, d, :],
                                                        part[:, ch, d:d + 1], None, ALU.mult)
                    pool.drain().then_inc(gu_ready.sem, 1)

                    def level(lev):
                        for g, first, n in G3:
                            if lev == 0:
                                pool.wait_ge(at_ready.sem, at_ready.at(Q, g + 1))
                            elif lev == 1:
                                pool.wait_ge(xt_ready.sem, xt_ready.at(Q, g + 1))
                            else:
                                pool.wait_ge(p_ready.sem, p_ready.at(Q, 3 * (lev - 2) + g + 1))
                            m3 = slice(first, first + n)
                            mask = levels[:, lev, :, :] if g == 2 else repeated(levels[:, lev, g, :], n)
                            nc.gpsimd.tensor_tensor(AL[:, m3, :], AT[:, m3, :], mask, ALU.mult)
                            pool.drain().then_inc(al_ready.sem, 1)

                    level(0)
                    level(1)
                    pool.wait_ge(tok_ready.sem, tok_ready.at(Q, 1))
                    pool.sem_inc(passed, 1)
                    for g, first, n in G3:
                        for c in range(n):
                            d = g if g < 2 else c
                            ch = c if g < 2 else 4
                            nc.gpsimd.tensor_scalar(kd[:, first + c, :], ktok[:, ch, :], eh[:, ch, d:d + 1],
                                                    None, ALU.mult)
                    pool.drain().then_inc(kd_ready.sem, 1)
                    for lev in range(2, NLEV):
                        level(lev)
                pool.wait_ge(head_done.sem, head_done.at(L, 0) * H + H)
                pool.dma_start(SNEW[bass.ds(L, 1)].rearrange("a p n -> p (a n)"), big[:, PB0 + 3840:PB0 + 4864]
                               ).then_inc(state_stored.sem, 16)
                pool.dma_start(rope, ROPES).then_inc(rope_in.sem, 16)
                split_phase("B", 2, L)
                split("V", [0, 1, 2, 3], L)
                pool.wait_ge(proj_b.sem, proj_b.at(L, 1))
                pool.sem_inc(passed, 1)
                with pool.Fori(0, H) as hd:
                    Q = L * H + hd
                    with ExitStack():
                        src_q = PBq[:, bass.ds(hd, 1), NS:NT].rearrange("p a t -> p (a t)")
                        src_k = PBq[:, bass.ds(hd + 4, 1), NS:NT].rearrange("p a t -> p (a t)")
                        kc = pr("k_ctx").rearrange("p (i n) -> p i n", i=H)[:, bass.ds(hd, 1), :].rearrange("p a t -> p (a t)")
                        vc = pr("v_ctx").rearrange("p (i n) -> p i n", i=H)[:, bass.ds(hd, 1), :].rearrange("p a t -> p (a t)")
                        pool.wait_ge(attn_room, Q + 1)
                        nc.gpsimd.tensor_copy(qall[:, NS:NT], src_q)
                        nc.gpsimd.tensor_copy(kall[:, NT:NT + P], src_k)
                        nc.gpsimd.tensor_copy(kall[:, NS:NT], kc)
                        nc.gpsimd.tensor_copy(vall[:, 0:4, :], VB[:, 0:4, bass.ds(hd * P, P)])
                        nc.gpsimd.tensor_copy(vall[:, 5, :], VB[:, 4, bass.ds(hd * P, P)])
                        nc.gpsimd.tensor_copy(vall[:, 4, :], vc)
                    pool.drain().then_inc(qcopy.sem, 1)
                for phase, times in (("C", 3), ("mix", 3), ("out", 2), ("f1_0", 4), ("f2_0", 2), ("f1_1", 4), ("f2_1", 2),
                                     ("f1_2", 3), ("f2_2", 2)):
                    split_phase(phase, times, L)


ROUND = 1.5 * 2.0 ** 23
PI_BELOW = float(np.nextafter(np.float32(math.pi), np.float32(0)))


def two_pi_parts():
    a = 6.28125
    b = float(np.float32(round((TWO_PI - a) * 2 ** 21) / 2 ** 21))
    return a, b, float(np.float32(TWO_PI - a - b))


TWO_PI_PARTS = two_pi_parts()


def axial_rope():
    half = 32
    inv = (np.float32(10000.0) ** (-np.arange(0, half, 2, dtype=np.float32) / half)).astype(np.float32)
    t = np.arange(NS)
    pos = {0: (t // GRID_W).astype(np.float32), 1: (t % GRID_W).astype(np.float32)}
    cos, sin = np.zeros((P, NS), np.float32), np.zeros((P, NS), np.float32)
    for c in range(P):
        ang = (pos[(c % 64) // 32] * inv[c % 16]).astype(np.float32)
        cos[c], sin[c] = np.cos(ang), np.sin(ang)
    return np.concatenate([cos, sin], axis=1)


def constants(c, c_ctx, final_g, b_first):
    con = np.zeros((P, N_CON), np.float32)
    i = np.arange(P)

    def put(name, a):
        con[:, CON[name][0]:CON[name][1]] = a.reshape(P, -1)
    put("ident", np.eye(P, dtype=np.float32))
    put("ones", np.ones((P, P), np.float32))
    fwd = (i[:, None] <= i[None, :]).astype(np.float32)
    put("tri", np.stack([fwd, fwd.T], 1))
    put("big", np.where(np.stack([fwd, fwd.T], 1) > 0, 0.0, -1e30).astype(np.float32))
    perm = np.zeros((P, P), np.float32)
    for m in range(P):
        perm[m + 16 if m % 32 < 16 else m - 16, m] = -1.0 if m % 32 < 16 else 1.0
    put("perm", perm)
    lev = np.zeros((P, NLEV, 2, P), np.float32)
    for n in range(NLEV):
        same = (i[:, None] >> (n + 1)) == (i[None, :] >> (n + 1))
        f = same & ((i[:, None] >> n) % 2 == 0) & ((i[None, :] >> n) % 2 == 1)
        lev[:, n, 0], lev[:, n, 1] = f, f.T
    put("levels", lev)
    put("final_g", final_g.reshape(KC, P).T)
    put("b_first", b_first.reshape(-1, P).T[:, 0:16])
    put("cond", np.stack([c.reshape(KC, P).T, c_ctx.reshape(KC, P).T], 2))
    return con


def hyena_constants():
    hyc = np.zeros((P, N_HYC), np.float32)
    lo, hi = abs(math.log(1e-2) / 1.5), abs(math.log(1e-2) / 0.3)
    hyc[:, HYC["deltas"][0]:HYC["deltas"][1]] = np.linspace(lo, hi, 512, dtype=np.float32)
    at = 0
    for n in (NS, NP):
        j = np.arange(n, dtype=np.float32)
        t = j / np.float32(n - 1)
        ang = (np.float32(2.0 * math.pi) * j / np.float32(n))[:, None] * np.linspace(1e-4, 7, 8, dtype=np.float32)
        z = np.concatenate([t[:, None], np.cos(ang), -np.sin(ang)], axis=1).astype(np.float32)
        hyc[0:17, HYC["z"][0] + at:HYC["z"][0] + at + n] = z.T
        dist = np.abs(j - n // 2) / np.float32(n // 2)
        a = HYC["ndist"][0] + at // P
        hyc[:, a:a + n // P] = -dist.reshape(n // P, P).T
        at += n
    return hyc


def dft_tables():
    fwd, inv = np.zeros((P, N_FWD), np.float32), np.zeros((P, N_INV), np.float32)
    for n, length, tiles in ((NS, L_S, 3), (NP, L_P, 1)):
        fq = length // 2
        w = 2 * math.pi * (np.arange(fq) + 0.5) / length
        a = np.arange(n)[:, None] * w[None, :]
        both = np.concatenate([np.cos(a), np.sin(a)], 1)
        b = w[:, None] * (np.arange(n) + n // 2)[None, :]
        if n == NS:
            fwd[:, 0:4 * L_S] = both.reshape(4, P, 2 * fq).transpose(1, 0, 2).reshape(P, -1)
            back = np.concatenate([np.cos(b), np.sin(b)], 0)
            inv[:, 0:6 * NS] = back.reshape(6, P, NS).transpose(1, 0, 2).reshape(P, -1)
        else:
            fwd[:, 4 * L_S:] = both
            inv[0:fq, 6 * NS:] = np.concatenate([np.cos(b), np.sin(b)], 1)
    return fwd, inv


def units(w, width=P):
    k, n = w.shape
    out = np.zeros((n // width, P, UNIT), np.float32)
    out[:, :, 0:k // P * width] = w.reshape(k // P, P, n // width, width).transpose(2, 1, 0, 3).reshape(
        n // width, P, -1)
    return out


def kernel(x_prompt, x_sample, cache_k, cache_v, state_dn, c, c_ctx, norm1_g, norm2_g, w_mod, b_mod, w_in, dn_conv_w,
           dn_a_log, dn_dt_bias, dn_norm_g, da_lambda, da_subln_g, hy_conv_w, hy_conv_b, hy_w1, hy_b1, hy_freq,
           hy_w2, hy_b2, hy_w3, hy_d, w_br_a, w_br_b, w_br_c, w_out, w_ffn_in, w_ffn_out, final_g):
    import concourse.bacc as _bacc
    from concourse.bass_utils import run_bass_kernel_spmd as _run

    W = np.zeros((FIRST_MOD + DEPTH * UNITS, P, UNIT), np.float32)
    par = np.zeros((DEPTH, P, N_PAR), np.float32)
    mods = [units(np.asarray(w_mod[l])) for l in range(DEPTH)]
    W[0:FIRST_MOD] = mods[0][0:FIRST_MOD]
    at = FIRST_MOD
    for l in range(DEPTH):
        wi = np.asarray(w_in[l])
        cols = lambda a, n: units(wi[:, a:a + n])
        mod = mods[l][FIRST_MOD:]
        nxt = mods[(l + 1) % DEPTH][0:FIRST_MOD]
        f1, f2 = np.asarray(w_ffn_in[l]), np.asarray(w_ffn_out[l])
        a = np.concatenate([cols(0, 1536), cols(1552, 512)])
        b, v, u = cols(2064, 1024), cols(3088, 512), cols(3600, 1536)
        order = [a, mod, b, v, nxt, u]
        for j, w_br in enumerate((w_br_a, w_br_b, w_br_c)):
            for half in range(2):
                order.append(cols(5136 + j * D + half * 512, 512))
                order.append(units(np.asarray(w_br[l])[:, half * 512:(half + 1) * 512], 256))
        order.append(units(np.asarray(w_out[l])))
        for g, (first, n) in enumerate(F_GROUPS):
            for i in range(n // 2):
                c0 = (first + 2 * i) * P
                order.append(units(f1[:, c0:c0 + 256]))
                order.append(units(f1[:, D_FF + c0:D_FF + c0 + 256]))
            order.append(units(f2[first * P:(first + n) * P]))
        for part in order:
            W[at:at + part.shape[0]] = part
            at += part.shape[0]

        def put(name, a, rows=P):
            a = np.asarray(a)
            par[l, 0:rows, PAR[name][0]:PAR[name][1]] = a.reshape(rows, -1)

        def column(v):
            v = np.asarray(v)
            return v.reshape(-1, P).T

        def everywhere(v):
            v = np.asarray(v).reshape(1, -1)
            return np.broadcast_to(v, (P, v.shape[1]))
        put("b_mod", column(b_mod[l]))
        put("b_next", column(b_mod[(l + 1) % DEPTH])[:, 0:16])
        put("g1", column(norm1_g[l]))
        put("g2", column(norm2_g[l]))
        put("conv", np.pad(np.asarray(dn_conv_w[l]).reshape(5, 12, P).transpose(2, 1, 0), ((0, 0), (0, 1), (0, 0))))
        put("hconv", np.asarray(hy_conv_w[l]).reshape(3, 12, P).transpose(2, 1, 0))
        put("hconv_b", column(hy_conv_b[l]))
        put("a_log", everywhere(dn_a_log[l]))
        put("dt_bias", everywhere(dn_dt_bias[l]))
        put("dn_g", column(dn_norm_g[l]))
        put("sub_g", column(da_subln_g[l]))
        put("lam", everywhere(da_lambda[l]))
        put("w_ba", wi[:, 1536:1552].reshape(KC, P, 16).transpose(1, 0, 2))
        put("hy_w1", hy_w1[l], 17)
        put("hy_b1", hy_b1[l], 64)
        put("hy_fr", hy_freq[l], 64)
        put("hy_b2", hy_b2[l], 64)
        put("hy_w2", hy_w2[l], 64)
        put("hy_w3", hy_w3[l], 64)
        put("hy_d", column(hy_d[l]))
        put("state", np.asarray(state_dn)[0, l].reshape(8, P, P).transpose(1, 0, 2))
        put("k_ctx", np.asarray(cache_k)[0, l].transpose(2, 0, 1))
        put("v_ctx", np.asarray(cache_v)[0, l].transpose(1, 0, 2))
        lam_init = 0.8 - 0.6 * math.exp(-0.3 * l)
        put("lam_init", np.full((P, 1), lam_init, np.float32))
        put("one_minus_lam", np.full((P, 1), 1.0 - lam_init, np.float32))

    x = np.concatenate([np.asarray(x_sample)[0], np.asarray(x_prompt)[0]], 0)
    fwd, inv = dft_tables()
    arrays = {
        "W": W, "PARAMS": par, "CONSTS": constants(np.asarray(c), np.asarray(c_ctx), np.asarray(final_g), np.asarray(b_mod[0])),
        "ROPES": axial_rope(), "HYCS": hyena_constants(), "FWD": fwd, "INV": inv,
        "X": np.ascontiguousarray(x.T.reshape(KC, P, NT).transpose(1, 0, 2)),
    }
    nc = _bacc.Bacc("TRN2", target_bir_lowering=False, num_devices=1)
    args = {n: nc.dram_tensor(f"in_{n}", a.shape, F32, kind="ExternalInput").ap() for n, a in arrays.items()}
    shapes = {"Y": (P, KC, NT), "KNEW": (DEPTH, P, H * P), "VNEW": (DEPTH, P, H * P), "SNEW": (DEPTH, P, 8 * P)}
    args.update({n: nc.dram_tensor(f"out_{n}", s, F32, kind="ExternalOutput").ap() for n, s in shapes.items()})
    trunk_program(nc, **args)
    r = _run(nc, [{f"in_{n}": a for n, a in arrays.items()}], core_ids=[0]).results[0]
    y = np.asarray(r["out_Y"]).transpose(1, 0, 2).reshape(D, NT).T
    k_new = np.asarray(r["out_KNEW"]).reshape(DEPTH, P, H, P).transpose(0, 2, 1, 3)
    v_new = np.asarray(r["out_VNEW"]).reshape(DEPTH, P, H, P).transpose(0, 2, 1, 3)
    s_new = np.asarray(r["out_SNEW"]).reshape(DEPTH, P, 2, H, P).transpose(0, 2, 3, 1, 4)
    return (np.ascontiguousarray(y[None, NS:]), np.ascontiguousarray(y[None, :NS]),
            np.ascontiguousarray(k_new[None]), np.ascontiguousarray(v_new[None]), np.ascontiguousarray(s_new[None]))
```
